# Optimizing a Trainium2 kernel written in Bass

```python
import math
import jax, jax.numpy as jnp
from jax import lax
import numpy as np

D_MODEL = 2048
BATCH = 1
SEQ = 512
DEPTH = 1
DEC_BATCH = 8
DEC_SEQ = 1
PAST_LEN = 2048
PAGE_SIZE = 128

MIX_DIM = D_MODEL
CONV_DIM = MIX_DIM // 4
CONV_W = 3
HG_DIM = MIX_DIM // 4
HG_HEADS = 4
HG_DK = HG_DIM // HG_HEADS
HG_CHUNK = 16
HEAD_DIM = 64
ATTN_DIM = MIX_DIM - CONV_DIM - HG_DIM
N_HEADS = ATTN_DIM // HEAD_DIM
N_KV_HEADS = N_HEADS // 4
Q_PER_KV = N_HEADS // N_KV_HEADS
KV_DIM = N_KV_HEADS * HEAD_DIM
WINDOW = 128
N_GROUPS = 4
EXPERTS_PER_GROUP = 4
N_EXPERTS = N_GROUPS * EXPERTS_PER_GROUP
TOP_K = 2
D_EXPERT = D_MODEL // 4
ALPHA = (2 * DEPTH) ** 0.25
BETA = (8 * DEPTH) ** -0.25
LN_EPS = 1e-5
RMS_EPS = 1e-6
SPLIT_SIZES = (CONV_DIM, CONV_DIM, CONV_DIM, HG_DIM, HG_DIM, HG_DIM, HG_DIM, ATTN_DIM, KV_DIM, KV_DIM)
IN_DIM = sum(SPLIT_SIZES)

kernel_name = "hymba_hybrid_conv_hgrn2_swa_hmoe_step"

F32 = jnp.float32

def layer_norm(x, g, b):
    xf = x.astype(F32)
    mu = jnp.mean(xf, -1, keepdims=True)
    var = jnp.mean(jnp.square(xf - mu), -1, keepdims=True)
    return ((xf - mu) * lax.rsqrt(var + LN_EPS) * g + b).astype(x.dtype)

def alibi_slopes():
    h = jnp.arange(1, N_HEADS + 1, dtype=F32)
    return jnp.exp2(-8.0 * h / N_HEADS).reshape(N_KV_HEADS, Q_PER_KV)

def causal_short_conv(u, hist, w):
    ext = jnp.concatenate([hist.astype(u.dtype), u], axis=1)
    L = u.shape[1]
    y = w[0] * ext[:, 0:L]
    for j in range(1, CONV_W):
        y = y + w[j] * ext[:, j:j + L]
    return y, ext[:, ext.shape[1] - (CONV_W - 1):]

def hgrn2_recurrence(q, k, v, logf, s0, chunk):
    b_, l_, h_, _ = q.shape
    dv = v.shape[-1]
    n = l_ // chunk
    blk = lambda a: a.astype(F32).reshape(b_, n, chunk, h_, a.shape[-1])
    q, k, v, g = blk(q), blk(k), blk(v), blk(logf)
    cum = jnp.cumsum(g, axis=2)
    causal = jnp.tril(jnp.ones((chunk, chunk), dtype=bool))
    diff = cum[:, :, :, None] - cum[:, :, None, :]
    decay = jnp.exp(jnp.where(causal[:, :, None, None], diff, -jnp.inf))
    scores = jnp.einsum('bnthd,bnshd,bntshd->bnhts', q, k, decay)
    o_intra = jnp.einsum('bnhts,bnshv->bnthv', scores, v)
    last = cum[:, :, -1]
    k_to_end = k * jnp.exp(last[:, :, None] - cum)
    u = jnp.einsum('bnshd,bnshv->bnhdv', k_to_end, v)

    def step(state, inp):
        a, du = inp
        return jnp.exp(a)[..., None] * state + du, state

    s_final, s_before = lax.scan(step, s0.astype(F32),
                                 (jnp.moveaxis(last, 1, 0), jnp.moveaxis(u, 1, 0)))
    o_inter = jnp.einsum('bnthd,nbhdv->bnthv', q * jnp.exp(cum), s_before)
    return (o_intra + o_inter).reshape(b_, l_, h_, dv), s_final

def sink_attention(q, k, v, dist, valid, sinks):
    slopes = alibi_slopes()
    s = jnp.einsum('bnqkgd,bnskd->bnkgqs', q.astype(F32), k.astype(F32)) * (HEAD_DIM ** -0.5)
    s = s - slopes[:, :, None, None] * dist.astype(F32)
    s = jnp.where(valid[None, :, None, None], s, -jnp.inf)
    sink = sinks.astype(F32)[:, :, None, None]
    m = jnp.maximum(s.max(-1, keepdims=True), sink)
    p = jnp.exp(s - m)
    denom = p.sum(-1, keepdims=True) + jnp.exp(sink - m)
    return jnp.einsum('bnkgqs,bnskd->bnqkgd', p / denom, v.astype(F32))

def token_mixers(x, conv_hist, s0, kv_hist, lb, w_in, w_out, conv_w, hg_gain, sinks, hg_chunk):
    bsz, L, _ = x.shape
    proj = x @ w_in
    cb, cc, ch, hq, hf, hi, hgt, aq, ak, av = jnp.split(
        proj, np.cumsum(SPLIT_SIZES)[:-1].tolist(), axis=-1)
    conv_y, conv_state = causal_short_conv(cc * ch, conv_hist, conv_w)
    y_a = cb * conv_y
    f = lb + (1.0 - lb) * jax.nn.sigmoid(hf.astype(F32))
    heads = lambda a: a.reshape(bsz, L, HG_HEADS, HG_DK)
    o, s_new = hgrn2_recurrence(heads(hq.astype(F32)) * (HG_DK ** -0.5), heads(1.0 - f),
                                heads(hi), heads(jnp.log(f)), s0, hg_chunk)
    o = o * lax.rsqrt(jnp.mean(o * o, -1, keepdims=True) + RMS_EPS) * hg_gain
    y_b = (o * jax.nn.silu(heads(hgt).astype(F32))).reshape(bsz, L, HG_DIM).astype(x.dtype)
    q = aq.reshape(bsz, L, N_KV_HEADS, Q_PER_KV, HEAD_DIM)
    k = ak.reshape(bsz, L, N_KV_HEADS, HEAD_DIM)
    v = av.reshape(bsz, L, N_KV_HEADS, HEAD_DIM)
    sinks = sinks.reshape(N_KV_HEADS, Q_PER_KV)
    if kv_hist is None:
        nb = L // WINDOW
        qb = q.reshape(bsz, nb, WINDOW, N_KV_HEADS, Q_PER_KV, HEAD_DIM)
        kb = k.reshape(bsz, nb, WINDOW, N_KV_HEADS, HEAD_DIM)
        vb = v.reshape(bsz, nb, WINDOW, N_KV_HEADS, HEAD_DIM)
        pad = ((0, 0), (1, 0), (0, 0), (0, 0), (0, 0))
        kk = jnp.concatenate([jnp.pad(kb[:, :-1], pad), kb], axis=2)
        vv = jnp.concatenate([jnp.pad(vb[:, :-1], pad), vb], axis=2)
        i = jnp.arange(WINDOW)[:, None]
        j = jnp.arange(2 * WINDOW)[None, :]
        dist = i + WINDOW - j
        key_pos = jnp.arange(nb)[:, None, None] * WINDOW - WINDOW + j[None]
        valid = (dist >= 0) & (dist < WINDOW) & (key_pos >= 0)
        o_c = sink_attention(qb, kk, vv, dist, valid, sinks)
        w_buf = min(WINDOW, PAST_LEN)
        k_state, v_state = k[:, L - w_buf:], v[:, L - w_buf:]
    else:
        k_cache, v_cache = kv_hist
        w_buf = k_cache.shape[1]
        kk = jnp.concatenate([k_cache.astype(k.dtype), k], axis=1)
        vv = jnp.concatenate([v_cache.astype(v.dtype), v], axis=1)
        i = jnp.arange(L)[:, None]
        j = jnp.arange(w_buf + L)[None, :]
        dist = i + w_buf - j
        valid = ((dist >= 0) & (dist < WINDOW))[None]
        o_c = sink_attention(q[:, None], kk[:, None], vv[:, None], dist, valid, sinks)[:, 0]
        k_state, v_state = kk[:, L:], vv[:, L:]
    y_c = o_c.reshape(bsz, L, ATTN_DIM).astype(x.dtype)
    y = jnp.concatenate([y_a, y_b, y_c], axis=-1) @ w_out
    return y, conv_state, s_new.astype(x.dtype), k_state, v_state

def hier_moe(x, w_group, b_group, w_router, b_router, w_gate, w_up, w_down):
    shp = x.shape
    xf = x.reshape(-1, D_MODEL)
    t = xf.shape[0]
    g_logits = (xf @ w_group).astype(F32) + b_group
    g_prob = jax.nn.softmax(g_logits, axis=-1)
    _, g_idx = lax.top_k(g_logits, 1)
    e_logits = ((xf @ w_router).astype(F32) + b_router).reshape(t, N_GROUPS, EXPERTS_PER_GROUP)
    e_in_group = jnp.take_along_axis(e_logits, g_idx[:, :, None], axis=1)[:, 0]
    e_val, e_idx = lax.top_k(e_in_group, TOP_K)
    weights = jax.nn.softmax(e_val, axis=-1) * jnp.take_along_axis(g_prob, g_idx, axis=1)
    expert = g_idx * EXPERTS_PER_GROUP + e_idx
    gate = jnp.sum(jax.nn.one_hot(expert, N_EXPERTS, dtype=F32) * weights[..., None], axis=1)
    h = jax.nn.silu(jnp.einsum('td,edf->tef', xf, w_gate)) * jnp.einsum('td,edf->tef', xf, w_up)
    y = jnp.einsum('tef,te,efd->td', h, gate.astype(h.dtype), w_down)
    return y.reshape(shp)

def setup_inputs(seed: int = 0) -> dict:
    key = jax.random.key(seed)
    ks = jax.random.split(key, 24)
    nrm = lambda k, shape, scale: jax.random.normal(k, shape, F32) * scale
    w_buf = min(WINDOW, PAST_LEN)
    return {
        "x_prompt": nrm(ks[0], (BATCH, SEQ, D_MODEL), 1.0),
        "x_sample": nrm(ks[1], (DEC_BATCH, DEC_SEQ, D_MODEL), 1.0),
        "state_conv": nrm(ks[2], (DEPTH, DEC_BATCH, CONV_W - 1, CONV_DIM), 1.0),
        "state_hgrn": nrm(ks[3], (DEPTH, DEC_BATCH, HG_HEADS, HG_DK, HG_DK), 0.5),
        "cache_k_win": nrm(ks[4], (DEPTH, DEC_BATCH, w_buf, N_KV_HEADS, HEAD_DIM), 1.0),
        "cache_v_win": nrm(ks[5], (DEPTH, DEC_BATCH, w_buf, N_KV_HEADS, HEAD_DIM), 1.0),
        "w_in": nrm(ks[6], (DEPTH, D_MODEL, IN_DIM), D_MODEL ** -0.5),
        "w_out": nrm(ks[7], (DEPTH, MIX_DIM, D_MODEL), BETA * MIX_DIM ** -0.5),
        "conv_w": nrm(ks[8], (DEPTH, CONV_W, CONV_DIM), CONV_W ** -0.5),
        "hg_lb_param": nrm(ks[9], (DEPTH, HG_DIM), 1.0),
        "hg_gain": 1.0 + nrm(ks[10], (DEPTH, HG_DK), 0.02),
        "attn_sinks": nrm(ks[11], (DEPTH, N_HEADS), 1.0),
        "ln1_g": 1.0 + nrm(ks[12], (DEPTH, D_MODEL), 0.02),
        "ln1_b": nrm(ks[13], (DEPTH, D_MODEL), 0.02),
        "w_group": nrm(ks[14], (DEPTH, D_MODEL, N_GROUPS), D_MODEL ** -0.5),
        "b_group": nrm(ks[15], (DEPTH, N_GROUPS), 0.01),
        "w_router": nrm(ks[16], (DEPTH, D_MODEL, N_EXPERTS), D_MODEL ** -0.5),
        "b_router": nrm(ks[17], (DEPTH, N_EXPERTS), 0.01),
        "w_gate": nrm(ks[18], (DEPTH, N_EXPERTS, D_MODEL, D_EXPERT), D_MODEL ** -0.5),
        "w_up": nrm(ks[19], (DEPTH, N_EXPERTS, D_MODEL, D_EXPERT), D_MODEL ** -0.5),
        "w_down": nrm(ks[20], (DEPTH, N_EXPERTS, D_EXPERT, D_MODEL), BETA * D_EXPERT ** -0.5),
        "ln2_g": 1.0 + nrm(ks[21], (DEPTH, D_MODEL), 0.02),
        "ln2_b": nrm(ks[22], (DEPTH, D_MODEL), 0.02),
    }

def reference(x_prompt, x_sample, state_conv, state_hgrn, cache_k_win, cache_v_win,
              w_in, w_out, conv_w, hg_lb_param, hg_gain, attn_sinks, ln1_g, ln1_b,
              w_group, b_group, w_router, b_router, w_gate, w_up, w_down, ln2_g, ln2_b):
    lb_soft = jax.nn.softmax(hg_lb_param.astype(F32), axis=0)
    lb_all = jnp.cumsum(lb_soft, axis=0) - lb_soft[0]

    def layer(x, conv_hist, s0, kv_hist, hg_chunk, l):
        mix, cs, ss, ks_, vs_ = token_mixers(x, conv_hist, s0, kv_hist, lb_all[l], w_in[l], w_out[l],
                                             conv_w[l], hg_gain[l], attn_sinks[l], hg_chunk)
        x = layer_norm(ALPHA * x + mix, ln1_g[l], ln1_b[l])
        ffn = hier_moe(x, w_group[l], b_group[l], w_router[l], b_router[l],
                       w_gate[l], w_up[l], w_down[l])
        x = layer_norm(ALPHA * x + ffn, ln2_g[l], ln2_b[l])
        return x, cs, ss, ks_, vs_

    yp, ys = x_prompt, x_sample
    bp = x_prompt.shape[0]
    conv_p, conv_s, hg_p, hg_s, k_p, k_s, v_p, v_s = [], [], [], [], [], [], [], []
    for l in range(DEPTH):
        zero_conv = jnp.zeros((bp, CONV_W - 1, CONV_DIM), x_prompt.dtype)
        zero_s = jnp.zeros((bp, HG_HEADS, HG_DK, HG_DK), F32)
        yp, cs, ss, kst, vst = layer(yp, zero_conv, zero_s, None, HG_CHUNK, l)
        conv_p.append(cs); hg_p.append(ss); k_p.append(kst); v_p.append(vst)
        ys, cs, ss, kst, vst = layer(ys, state_conv[l], state_hgrn[l],
                                     (cache_k_win[l], cache_v_win[l]), x_sample.shape[1], l)
        conv_s.append(cs); hg_s.append(ss); k_s.append(kst); v_s.append(vst)

    return (yp, ys, jnp.stack(conv_p), jnp.stack(conv_s), jnp.stack(hg_p), jnp.stack(hg_s),
            jnp.stack(k_p), jnp.stack(k_s), jnp.stack(v_p), jnp.stack(v_s))


_drawn_inputs = setup_inputs


def setup_inputs(seed=0):
    import zlib

    import numpy as np

    out = dict(_drawn_inputs(seed))
    spreads = {}
    factors = {'hg_gain': 21.57,
     'b_group': 168.698,
     'b_router': 27.406,
     'ln2_g': 20.894,
     'ln2_b': 21.545,
     'attn_sinks': 9.04}
    for name, (base, spread) in spreads.items():
        noise = np.random.default_rng([zlib.crc32(name.encode()), seed]).standard_normal(out[name].shape)
        drawn = base * np.exp(spread * noise) if base else spread * noise
        out[name] = __import__('jax').numpy.asarray(drawn.astype(out[name].dtype))
    for name, factor in factors.items():
        out[name] = (out[name] * factor).astype(out[name].dtype)
    return out
```

```python
import math
from contextlib import ExitStack

import numpy as np
import concourse.bass as bass
from concourse import mybir

F32 = mybir.dt.float32
F32R = mybir.dt.float32r
F16 = mybir.dt.float16
I32 = mybir.dt.int32
ALU = mybir.AluOpType
ACT = mybir.ActivationFunctionType
AX = mybir.AxisListType

D = 2048
SEQ, DB = 512, 8
T = SEQ + DB
HALF = T // 2
NT, TT = 5, T // 5
KC = D // 128
NU = 40
HD, WIN = 64, 128
NE, EPG, NG = 16, 4, 4
CAP = 128
MAXB = (2 * T - NE) // CAP + NE
DK = 128
ALPHA = 2.0 ** 0.25
LN_EPS, RMS_EPS = 1e-5, 1e-6
SLOPE = [2.0 ** (-8.0 * (h + 1) / 16) for h in range(16)]
NEG = -3e38
POOL_LO = (3, 7)
SKIP = 4096.0

ATT0 = [0, 6]
HG0 = [12 + 4 * h for h in range(4)]
CV0 = [28 + 3 * j for j in range(4)]


def feature_order():
    cc, ch, cb = 512, 1024, 0
    hq, hf, hi, hg = 1536, 2048, 2560, 3072
    aq, ak, av = 3584, 4608, 4864
    out = []
    for t in range(2):
        out += [np.arange(ak + 128 * t, ak + 128 * t + 128), np.arange(av + 128 * t, av + 128 * t + 128)]
        for j in range(4):
            out.append(np.concatenate([np.arange(aq + 64 * h, aq + 64 * h + 64) for h in (8 * t + j, 8 * t + 4 + j)]))
    for h in range(4):
        out += [np.arange(b + 128 * h, b + 128 * h + 128) for b in (hq, hf, hi, hg)]
    for j in range(4):
        out += [np.arange(b + 128 * j, b + 128 * j + 128) for b in (cc, ch, cb)]
    return np.concatenate(out)


def mix_order():
    out = []
    for t in range(2):
        for j in range(4):
            out.append(np.concatenate([np.arange(1024 + 64 * h, 1024 + 64 * h + 64) for h in (8 * t + j, 8 * t + 4 + j)]))
    out += [np.arange(512 + 128 * h, 512 + 128 * h + 128) for h in range(4)]
    out += [np.arange(128 * j, 128 * j + 128) for j in range(4)]
    return np.concatenate(out)


NQ = 4 * NU
STEPS = [(l, qb) for l in range(2) for qb in range(4)]


def schedule():
    at = {q: [] for q in range(NQ + 40)}
    for t in range(2):
        b = (24, 52)[t]
        at[b].append(("att_setup", t))
        for i in range(8):
            at[b + 2 + 2 * i].append(("att_scores", 8 * t + i))
            at[b + 4 + 2 * i].append(("att_turn", 8 * t + i))
            at[b + 6 + 2 * i].append(("att_pv", 8 * t + i))
        for s in range(5):
            at[b + 18 + 2 * s + (2 if s > 0 else 0)].append((f"smp{s}", t))
    for h in range(4):
        b = 82 + 18 * h
        at[b - 2].append(("hg_prep", h))
        for l in range(8):
            at[b + l].append(("hg_factor", 8 * h + l))
            at[b + l + 1].append(("hg_level", 8 * h + l))
        at[b + 8].append(("hg_final", h))
        for s in range(6):
            at[b + 9 + s].append((f"hg{s}", h))
    for j, q in enumerate((134, 148, NQ - 3)):
        at[q].append(("conv", j))
    return at


def build(nc, a, o):
    MIX = schedule()
    x1_rows = nc.dram_tensor("x1_rows", [T, D], F32, kind="Internal").ap()
    y_rows = nc.dram_tensor("y_rows", [2 * T, D], F32, kind="Internal").ap()

    base = (nc.sbuf_base + 63) // 64 * 64

    def sb(name, shape, dt, off):
        return nc.alloc_sbuf_tensor_at(name, shape, dt, offset=base + off)

    IDENT = sb("IDENT", [128, 128], F32, 0)
    ONES = sb("ONES", [128, 128], F32, 512)
    NDIST = sb("NDIST", [128, 256], F32, 1024)
    MASK = sb("MASK", [128, 8, 128], F16, 2048)
    NDS = sb("NDS", [64, 2, 128], F32, 4096)
    SM = sb("SM", [128, 512], F32, 5120)
    O_RING = 7168
    RAW = sb("RAW", [128, 2, 2048], F32, O_RING)
    HI = sb("HI", [128, 2, 2048], F32R, O_RING + 16384)
    LO = sb("LO", [128, 2, 2048], F32R, O_RING + 32768)
    O_XT = O_RING + 49152
    XH = sb("XH", [128, KC, T], F32R, O_XT)
    XL = sb("XL", [128, KC, T], F32R, O_XT + 33280)
    O_Y = O_XT + 66560
    Y = sb("Y", [128, KC, T], F32, O_Y)
    O_PR = O_Y + 33280
    PR = sb("PR", [128, 16, T], F32, O_PR)
    O_T = O_PR + 33280
    SC = sb("SC", [128, 4, 256], F32, O_T)
    PT = sb("PT", [128, 2, 4, 128], F32, O_T + 4096)
    VT = sb("VT", [128, 4, 128], F32, O_T + 8192)
    KCA = sb("KCA", [128, DB, 128], F32, O_T + 10240)
    VCA = sb("VCA", [128, DB, 128], F32, O_T + 14336)
    SELF = sb("SELF", [DB, 2, 128], F32, O_T + 18432)
    KTS = sb("KTS", [128, DB, 128], F32, O_T)
    SST = sb("SST", [128, 64], F32, O_T + 19456)
    SSR = sb("SSR", [64, 128], F32, O_T + 19712)
    PST = sb("PST", [128, 64], F32, O_T + 20224)
    PF = sb("PF", [128, SEQ], F32, O_T)
    SF = sb("SF", [128, SEQ], F32, O_T + 2048)
    AT = sb("AT", [128, 4, 128], F32, O_T + 4096)
    TMP = sb("TMP", [128, T], F32, O_T + 6144)
    VTK = sb("VTK", [128, 4, 128], F32, O_T + 8256)
    EF = sb("EF", [128, 2, T], F32, O_T + 10304)
    QF = sb("QF", [128, 2, T], F32, O_T + 14464)
    S0 = sb("S0", [128, DB, 128], F32, O_T + 18624)
    CVO = sb("CVO", [128, 4, 18], F32, O_T + 22720)
    R = sb("R", [TT, NT, D], F32, O_PR)
    LG = sb("LG", [TT, D], F32, O_Y)
    LB = sb("LB", [TT, D], F32, O_Y + 8192)
    X1T = sb("X1T", [128, 2, KC, TT], F32, O_Y + 16384)
    WR = sb("WR", [128, KC, 20], F32, O_RING)
    O_RT = O_PR + 40960
    rt = [O_RT]

    def small(name, shape, dt=F32):
        n = int(np.prod(shape[1:])) * 4
        off = rt[0]
        rt[0] += (n + 31) // 32 * 32
        return sb(name, shape, dt, off)

    NRAW, NHL = 6, 3
    RAWB = sb("RAWB", [128, NRAW, 2048], F32, O_RING)
    HIB = sb("HIB", [128, NHL, 2048], F32R, O_RING + 49152)
    LOB = sb("LOB", [128, NHL, 2048], F32R, O_RING + 73728)
    O_M = O_RING + 98304
    XG = sb("XG", [128, D], F32, O_M)
    XGH = sb("XGH", [128, KC, 128], F32R, O_M + 8192)
    XGL = sb("XGL", [128, KC, 128], F32R, O_M + 16384)
    YO = sb("YO", [128, D], F32, O_M + 24576)
    H = sb("H", [128, 512], F32, O_M + 32768)
    SG = sb("SG", [128, 512], F32, O_M + 34816)
    HTH = sb("HTH", [128, 4, 128], F32R, O_M + 36864)
    HTL = sb("HTL", [128, 4, 128], F32R, O_M + 38912)
    YA = sb("YA", [TT, 2, D], F32, O_RING)
    YB = sb("YB", [TT, 2, D], F32, O_RING + 16384)
    LG2 = sb("LG2", [TT, D], F32, O_RING + 32768)
    LB2 = sb("LB2", [TT, D], F32, O_RING + 40960)

    BANK = nc.alloc_psum_tensor("BANK", [128, 8, 512], F32)

    SINK = SM[:, 0:16]
    GAIN = SM[:, 16:17]
    LBP = SM[:, 20:24]
    LB0 = SM[:, 24:28]
    OML = SM[:, 28:32]
    LBT = SM[:, 32:36]
    EPS_LN = SM[:, 36:37]
    EPS_RMS = SM[:, 37:38]
    SINKC = SM[:, 38:40]
    CW = SM[:, 40:52]
    HIST = SM[:, 64:128].rearrange("p (j b r) -> p j b r", j=4, b=DB)
    MX = SM[:, 128:144].rearrange("p (k j) -> p k j", j=4)
    MXS = SM[:, 144:150]
    DEC = SM[:, 152:156]
    FS = SM[:, 160:168]
    ST = SM[:, 192:312].rearrange("p (i n s) -> p i n s", i=NT, n=4)
    MV = SM[:, 320:340].rearrange("p (i s) -> p i s", i=NT)

    with ExitStack() as ctx:
        def sem(name):
            return ctx.enter_context(nc.semaphore(name))

        s_const = sem("const_in")
        s_ones = sem("ones_set")
        s_x = [sem(f"x_in{g}") for g in range(4)]
        s_xh = sem("x_hi")
        s_xl = sem("x_lo")
        s_raw = [sem(f"weights_in{s}") for s in range(2)]
        s_hi = sem("weights_hi")
        s_lo = sem("weights_lo")
        s_used = sem("out_weights_used")
        s_acc = sem("proj_ready")
        s_pr = sem("proj_copied")
        s_grp = sem("group_done")
        s_act = sem("act_chain")
        s_dve = sem("dve_chain")
        s_vt_t = sem("v_turned")
        s_vt = sem("v_copied")
        s_sc = sem("scores_ready")
        s_mx = sem("max_ready")
        s_ex = sem("exp_ready")
        s_p = sem("probs_ready")
        s_tp = sem("probs_turned")
        s_pt = sem("probs_t_copied")
        s_pv = sem("pv_ready")
        s_yc = sem("pv_copied")
        s_kc = sem("cache_in")
        s_self = sem("self_rows_in")
        s_w_kv = sem("kv_states_out")
        s_m = [sem(f"sample_{n}") for n in ("kt", "kt_copied", "scores", "scores_copied", "turned", "max", "exp", "probs", "pt", "pt_copied", "out")]
        h_clamp = sem("hg_clamped")
        h_e = sem("hg_exp")
        h_f = sem("hg_f")
        h_g = sem("hg_logf")
        h_fac = sem("hg_factors_exp")
        h_mul = sem("hg_factors_ready")
        h_k = sem("hg_k_ready")
        h_upd = sem("hg_sums_updated")
        h_lev = sem("hg_level_ready")
        h_acc = sem("hg_level_added")
        h_vt = sem("hg_v_turned")
        h_vtc = sem("hg_v_copied")
        h_fin = sem("hg_final_exp")
        h_ks = sem("hg_k_to_end")
        h_kt = sem("hg_k_turned")
        h_ktc = sem("hg_k_copied")
        h_u = sem("hg_u_ready")
        h_st = sem("hg_states_ready")
        h_s0 = sem("hg_state_in")
        h_vb = sem("hg_v_spread")
        h_sn = sem("hg_sample_states")
        h_o = sem("hg_out_ready")
        h_sq = sem("hg_squares")
        h_ss = sem("hg_square_sums")
        h_rt = sem("hg_root")
        h_out = sem("hg_states_out")
        c_out = sem("conv_states_out")
        c_rdy = sem("conv_state_ready")
        s_yh = sem("mix_hi")
        s_yl = sem("mix_lo")
        s_r = sem("residual_in")
        s_ob = sem("out_ready")
        s_oe = sem("out_added")
        s_lg = sem("ln1_in")
        s_wr = sem("router_in")
        s_var = sem("ln_var")
        s_sd = sem("ln_sd")
        s_rs = sem("ln_rstd")
        s_nrm = sem("ln_normed")
        s_x1 = sem("x1_ready")
        s_x1w = sem("x1_out")
        s_t1 = sem("x1_turned")
        s_t1a = sem("x1_t_copied_act")
        s_t1d = sem("x1_t_copied_dve")
        s_log = sem("logits_ready")
        s_rc = sem("route_consts")
        r_e = sem("route_exp_in")
        r_x = sem("route_exp")
        r_hot = sem("route_hot")
        r_rank = sem("route_rank")
        r_tab = sem("route_onehots")
        r_tabm = sem("route_table")
        r_idx = sem("route_indices")
        b_raw = [sem(f"expert_in{s}") for s in range(NRAW)]
        b_hi = sem("expert_hi")
        b_lo = [sem(f"expert_lo{s}") for s in range(NHL)]
        b_used = sem("expert_used")
        b_xg = sem("tokens_in")
        b_tx = sem("tokens_turned")
        b_ix = sem("gather_indices")
        b_iy = sem("scatter_indices")
        b_xh = sem("tokens_hi")
        b_xl = sem("tokens_lo")
        b_sg = sem("silu_ready")
        b_h = sem("h_ready")
        b_th = sem("h_turned")
        b_hh = sem("h_hi")
        b_hl = sem("h_lo")
        b_y = sem("down_copied")
        b_yw = sem("block_out")
        s_passed = sem("waits_passed")
        f_in = [sem(f"y_in{s}") for s in range(2)]
        f_ln = sem("ln2_in")
        f_st = sem("ln2_var")
        f_sd = sem("ln2_sd")
        f_rs = sem("ln2_rstd")
        f_nm = sem("ln2_normed")
        f_y = sem("y_ready")
        f_out = sem("y_out")

        TRI = small("TRI", [TT, TT])
        IO128 = small("IO128", [TT, 128])
        IO24 = small("IO24", [TT, MAXB + 1])
        IO4 = small("IO4", [TT, 4])
        IO16 = small("IO16", [TT, 16])
        TID = small("TID", [TT, NT])
        SKP = small("SKP", [128, 1])
        RB = small("RB", [TT, 20])
        LO_G = small("LO_G", [TT, NT, 20])
        G4 = [small(f"G4_{k}", [TT, NT, 4]) for k in range(2)]
        E16 = [small(f"E16_{k}", [TT, NT, 16]) for k in range(6)]
        C5 = [small(f"C5_{k}", [TT, NT]) for k in range(14)]
        NB16 = [small(f"NB16_{k}", [TT, 16]) for k in range(4)]
        OH = small("OH", [TT, 2, NT, 128])
        TB = small("TB", [TT, 2, NT, 3, MAXB + 1])
        TABF = small("TABF", [128, 3, MAXB + 1])
        TIX = small("TIX", [128, MAXB + 1], I32)
        YIX = small("YIX", [128, MAXB + 1], I32)
        TIXC = small("TIXC", [128, 1], I32)
        YIXC = small("YIXC", [128, 1], I32)
        EBC = small("EBC", [TT, MAXB + 1, 16])
        EBF = small("EBF", [TT, 32])
        TABZ = small("TABZ", [128, MAXB + 1])
        EBI = small("EBI", [1, 32], I32)

        def used(eng, u):
            if u < NU:
                eng.wait_ge(s_acc, 2 * u + 2)
            elif (u - NU) % 4 < 3:
                eng.wait_ge(s_used, 3 * ((u - NU) // 4) + (u - NU) % 4 + 1)
            else:
                eng.wait_ge(s_ob, NT * ((u - NU) // 4 + 1))

        block = ctx.enter_context(nc.Block())

        def acc(m):
            return BANK[:, m % 3, 0:HALF]

        MB = [BANK[:, 3 + k, :] for k in range(5)]

        def slot(u):
            return PR[:, u % 16, :]

        def passed(eng):
            eng.sem_inc(s_passed, 1)

        def turn_copies(eng, copy, i, acts):
            for g in range(4):
                is_act = acts
                if (g % 2 == 0) != is_act:
                    continue
                eng.wait_ge(s_t1, 4 * i + g + 1)
                if i >= 2:
                    eng.wait_ge(s_log, i - 1)
                dst = X1T[:, i % 2, 4 * g:4 * g + 4, :]
                src = BANK[:, (4 * i + g) % 6, 0:4 * TT].rearrange("p (c n) -> p c n", c=4)
                if is_act:
                    copy(dst, src, ACT.Copy).then_inc(s_t1a, 1)
                else:
                    copy(dst, src).then_inc(s_t1d, 1)

        @block.sync
        def _(sp):
            def unit(u, w):
                if u >= 2:
                    sp.wait_ge(s_lo, u - 1)
                sp.dma_start(RAW[:, u % 2, :], w).then_inc(s_raw[u % 2], 16)

            xr = a["xT"].rearrange("p (g n) -> p g n", g=4)
            sp.dma_start(Y[:, 0:4, :], xr[:, 0, :]).then_inc(s_x[0], 16)
            unit(0, a["w_in"][0])
            for g in range(1, 4):
                sp.dma_start(Y[:, 4 * g:4 * g + 4, :], xr[:, g, :]).then_inc(s_x[g], 16)
            unit(1, a["w_in"][1])
            for t, s in ((IDENT, "ident"), (NDIST, "ndist"), (MASK, "mask"), (NDS, "nds")):
                sp.dma_start(t[:], a[s]).then_inc(s_const, 16)
            for t, s in ((SINK, "sink"), (SINKC[0:64, :], "sinkc"), (GAIN, "gain"), (LBP, "lbp"), (CW, "cw"), (SM[:, 64:128], "hist")):
                sp.dma_start(t, a[s]).then_inc(s_const, 16)
            kc = a["cache_k"].rearrange("b s n -> s b n")
            vc = a["cache_v"].rearrange("b s n -> s b n")

            def caches(t):
                if t:
                    sp.wait_ge(s_grp, t)
                    sp.wait_ge(s_w_kv, 64 * t)
                for dst, src in ((KCA, kc), (VCA, vc)):
                    sp.dma_start(dst[0:127, :, :], src[1:128, :, 128 * t:128 * t + 128]).then_inc(s_kc, 16)

            def att_setup(t):
                sp.wait_ge(s_vt, 2 * t + 2)
                sp.dma_start(KCA[127:128, :, :], SELF[:, 0, :]).then_inc(s_self, 16)
                sp.dma_start(VCA[127:128, :, :], SELF[:, 1, :]).then_inc(s_self, 16)
                k_slot = slot(ATT0[t])
                sp.dma_start(o["kp"][t], k_slot[:, SEQ - WIN:SEQ]).then_inc(s_w_kv, 16)
                sp.dma_start(o["vp"][t], VT[:, 3, :]).then_inc(s_w_kv, 16)

            def smp0(t):
                sp.wait_ge(s_kc, 32 * (t + 1))
                sp.wait_ge(s_self, 32 * (t + 1))
                sp.dma_start(o["ks"][t], KCA[:, :, :]).then_inc(s_w_kv, 16)
                sp.dma_start(o["vs"][t], VCA[:, :, :]).then_inc(s_w_kv, 16)

            def hg_prep(h):
                if h:
                    sp.wait_ge(h_out, 32 * h)
                    sp.wait_ge(h_o, h)
                sp.dma_start(S0[:, :, :], a["s0"][h]).then_inc(h_s0, 16)

            def hg3(h):
                sp.wait_ge(h_st, h + 1)
                sp.dma_start(o["hp"][h], SF[:, 384:512]).then_inc(h_out, 16)
                sp.wait_ge(h_sn, 2 * h + 2)
                sp.dma_start(o["hs"][h], S0[:, :, :]).then_inc(h_out, 16)

            caches(0)
            for q in range(NQ):
                if q % 4 == 0 and q // 4 + 2 < NU:
                    unit(q // 4 + 2, a["w_in"][q // 4 + 2])
                for what, n in MIX[q]:
                    if what == "att_setup":
                        if n == 1:
                            caches(1)
                        att_setup(n)
                    elif what == "smp0":
                        smp0(n)
                    elif what == "hg_prep":
                        if n == 0:
                            sp.wait_ge(s_grp, 2)
                            sp.wait_ge(s_w_kv, 128)
                        hg_prep(n)
                    elif what == "hg3":
                        hg3(n)
            for k in range(2):
                unit(NU + k, a["w_out"][k])
            sp.wait_ge(s_grp, 10)
            sp.wait_ge(h_out, 128)
            sp.dma_start(o["cs"], CVO[:, :, :]).then_inc(c_out, 16)
            sp.wait_ge(c_out, 16)
            for i in range(NT):
                sp.dma_start(R[:, i, :], a["x"][i * TT:(i + 1) * TT, :]).then_inc(s_r, 16)
            for n in range(4):
                for k in range(4):
                    u = NU + 4 * n + k
                    if u + 2 < NU + 16:
                        unit(u + 2, a["w_out"][u + 2 - NU])
                if n == 0:
                    sp.wait_ge(s_yl, 4)
                    sp.dma_start(LG[:, :], a["ln1g"]).then_inc(s_lg, 16)
                    sp.dma_start(LB[:, :], a["ln1b"]).then_inc(s_lg, 16)
                    for t, s in ((TRI, "tri"), (IO128, "io128"), (IO24, "io24"), (IO4, "io4"), (IO16, "io16"), (TID, "tid"), (SKP, "skp"), (RB, "rb")):
                        sp.dma_start(t[:], a[s]).then_inc(s_rc, 16)
            sp.wait_ge(s_lo, NU + 16)
            sp.dma_start(WR[:, :, :], a["wr"]).then_inc(s_wr, 16)
            for i in range(NT):
                sp.wait_ge(s_x1, i + 1)
                sp.dma_start(x1_rows[i * TT:(i + 1) * TT, :], R[:, i, :]).then_inc(s_x1w, 16)

            sp.wait_ge(r_idx, 1)
            sp.wait_ge(s_log, NT)
            nb = sp.value_load(EBI[0:1, 31:32], min_val=8, max_val=MAXB - 1) + 1

            def gate_up(j, m0):
                e = sp.value_load(EBI[0:1, bass.ds(j, 1)], min_val=0, max_val=NE - 1)
                for i in range(8):
                    bload(i, m0, (a["w_gate"], a["w_up"])[i % 2][bass.ds(e, 1), :, 2048 * (i // 2):2048 * (i // 2) + 2048].rearrange("a p n -> p (a n)"), j)

            def bload(i, m0, w, j):
                s = (2 + i) % NRAW if m0 is not None else i % NRAW
                if m0 is None:
                    if i >= NRAW:
                        sp.wait_ge(b_lo[(i - NRAW) % NHL], (i - NRAW) // NHL + 1)
                else:
                    sp.wait_ge(b_lo[(2 + i) % NHL], (2 + i) // NHL + 1 + 4 * (j - 1))
                    passed(sp)
                sp.dma_start(RAWB[:, s, :], w).then_inc(b_raw[s], 16)

            def down(j, first):
                e = sp.value_load(EBI[0:1, bass.ds(j - 1, 1)], min_val=0, max_val=NE - 1)
                for n in range(4):
                    w = a["w_down"][bass.ds(e, 1), :, :, 512 * n:512 * n + 512].rearrange("a p c n -> p (a c) n")
                    i = first + n
                    s = (2 + i) % NRAW
                    sp.wait_ge(b_lo[(2 + i) % NHL], (2 + i) // NHL + 1 + 4 * (j - 1))
                    passed(sp)
                    sp.dma_start(RAWB[:, s, :].rearrange("p (c n) -> p c n", c=4), w).then_inc(b_raw[s], 16)

            gate_up(0, None)
            with sp.Fori(1, MAXB) as j:
                with sp.If(j < nb):
                    gate_up(j, 0)
                    down(j, 8)
            down(nb, 0)

            sp.wait_ge(b_yw, 16 * nb + 16)
            passed(sp)
            sp.wait_ge(b_used, 12 * nb)
            passed(sp)
            sp.dma_start(LG2[:, :], a["ln2g"]).then_inc(f_ln, 16)
            sp.dma_start(LB2[:, :], a["ln2b"]).then_inc(f_ln, 16)
            for i in range(NT):
                if i >= 2:
                    sp.wait_ge(f_st, i - 1)
                for c, dst in ((0, YA), (1, YB)):
                    sp.dma_start(dst[:, i % 2, :], y_rows[c * T + i * TT:c * T + (i + 1) * TT, :]).then_inc(f_in[i % 2], 16)
            for i in range(NT):
                sp.wait_ge(f_y, i + 1)
                n = TT if i < NT - 1 else TT - DB
                sp.dma_start(o["yp"][i * TT:i * TT + n, :], R[0:n, i, :]).then_inc(f_out, 16)
            sp.dma_start(o["ys"], R[TT - DB:TT, NT - 1, :]).then_inc(f_out, 16)
            sp.wait_ge(f_out, 16 * (NT + 1))
            sp.wait_ge(s_w_kv, 128)
            sp.wait_ge(h_out, 128)
            sp.wait_ge(c_out, 16)

        @block.gpsimd
        def _(pool):
            def lo(u):
                pool.wait_ge(s_hi, u + 1)
                pool.tensor_tensor(LO[:, u % 2, :], RAW[:, u % 2, :], HI[:, u % 2, :].bitcast(F32), ALU.subtract).then_inc(s_lo, 1)

            pool.memset(ONES[:, :], 1.0).then_inc(s_ones, 1)
            for u in range(NU + 16):
                lo(u)

            pool.wait_ge(r_idx, 1)
            pool.wait_ge(s_log, NT)
            pool.wait_ge(s_x1w, 16 * NT)
            nb = pool.value_load(EBI[0:1, 31:32], min_val=8, max_val=MAXB - 1) + 1
            pool.memset(XG[:, :], 0.0).then_inc(s_ones, 1)
            pool.wait_ge(s_ones, 2)

            last_token, last_row = pool.to_reg(T - 1), pool.to_reg(2 * T - 1)

            def gather(j, landed):
                pool.tensor_copy(TIXC[:, :], TIX[:, bass.ds(j, 1)]).then_inc(b_ix, 1)
                pool.wait_ge(b_ix, j + 1)
                passed(pool)
                pool.indirect_dma_start(
                    out=XG[:, :], out_offset=None, in_=x1_rows,
                    in_offset=bass.IndirectOffsetOnAxis(ap=TIXC[:, 0:1], axis=0),
                    bounds_check=last_token, oob_is_err=False).then_inc(landed, 16)

            def blo(i, m0, j):
                s, r = (i % NHL, i % NRAW) if m0 is None else ((2 + i) % NHL, (2 + i) % NRAW)
                pool.wait_ge(b_hi, i + 1 if m0 is None else 12 * j + i - 3)
                pool.tensor_tensor(LOB[:, s, :], RAWB[:, r, :], HIB[:, s, :].bitcast(F32), ALU.subtract).then_inc(b_lo[s], 1)

            def scatter(j):
                pool.wait_ge(b_y, 4 * j + 2)
                passed(pool)
                pool.tensor_copy(YIXC[:, :], YIX[:, bass.ds(j - 1, 1)]).then_inc(b_iy, 1)
                pool.wait_ge(b_iy, j)
                passed(pool)
                pool.indirect_dma_start(
                    out=y_rows, out_offset=bass.IndirectOffsetOnAxis(ap=YIXC[:, 0:1], axis=0),
                    in_=YO[:, :], in_offset=None,
                    bounds_check=last_row, oob_is_err=False).then_inc(b_yw, 16)

            gather(0, b_yw)
            pool.wait_ge(b_tx, 4)
            gather(1, b_xg)
            for i in POOL_LO:
                if i < 8:
                    blo(i, None, 0)
            with pool.Fori(1, MAXB) as j:
                with pool.If(j < nb):
                    pool.wait_ge(b_tx, 4 * j + 4)
                    passed(pool)
                    gather(j + 1, b_xg)
                    for i in POOL_LO:
                        blo(i, 0, j)
                    scatter(j)
            scatter(nb)
            pool.wait_ge(b_xg, 16 * nb)
            passed(pool)

        @block.scalar
        def _(act):
            chain = [0]

            def done(ins):
                chain[0] += 1
                ins.then_inc(s_act, 1)
                act.wait_ge(s_act, chain[0])

            def hi(u):
                act.wait_ge(s_raw[u % 2], 16 * (u // 2 + 1))
                if u >= 2:
                    used(act, u - 2)
                act.activation(HI[:, u % 2, :], RAW[:, u % 2, :], ACT.Copy).then_inc(s_hi, 1)

            def copy_proj(m):
                u, hf = m // 2, m % 2
                act.wait_ge(s_acc, m + 1)
                if u >= 16 and hf == 0:
                    g = [0] * 6 + [1] * 6 + [2 + k // 4 for k in range(16)]
                    act.wait_ge(s_grp, g[u - 16] + 1)
                    if u - 16 in (0, 6):
                        act.wait_ge(s_w_kv, 64 * (1 + (u - 16) // 6))
                scale = 1.0
                if u in range(2, 6) or u in range(8, 12):
                    scale = HD ** -0.5
                if u in HG0:
                    scale = DK ** -0.5
                act.activation(PR[:, u % 16, hf * HALF:(hf + 1) * HALF], acc(m), ACT.Copy, scale=scale).then_inc(s_pr, 1)

            def att_setup(t):
                act.wait_ge(s_vt_t, 2 * t + 1)
                if t:
                    act.wait_ge(s_w_kv, 64 * t)
                act.activation(VT[:, :, :], MB[2].rearrange("p (c n) -> p c n", c=4), ACT.Copy).then_inc(s_vt, 1)
                act.wait_ge(s_vt_t, 2 * t + 2)
                act.activation(SELF[:, :, :], MB[3][0:DB, 0:256].rearrange("p (c n) -> p c n", c=2), ACT.Copy).then_inc(s_vt, 1)

            def att_scores(s):
                l, qb = STEPS[s % 8]
                k0 = 128 if qb == 0 else 0
                act.wait_ge(s_mx, s + 1)
                for j in range(4):
                    ins = act.activation(SC[:, j, k0:256], SC[:, j, k0:256], ACT.Exp, bias=MX[:, 1, j:j + 1],
                                         accum_out=MX[:, 3, j:j + 1])
                done(ins)
                act.activation(MX[:, 2, :], MX[:, 2, :], ACT.Exp).then_inc(s_ex, 1)

            def att_turn(s):
                l, qb = STEPS[s % 8]
                h0 = 1 if qb == 0 else 0
                act.wait_ge(s_tp, s + 1)
                if s >= 1:
                    act.wait_ge(s_pv, s)
                for k in range(h0, 2):
                    ins = act.activation(PT[:, k, :, :], MB[2 + k].rearrange("p (c n) -> p c n", c=4), ACT.Copy)
                ins.then_inc(s_pt, 1)

            def smp(s, t):
                if s == 0:
                    act.wait_ge(s_m[0], t + 1)
                    for k in range(2):
                        ins = act.activation(KTS[:, 4 * k:4 * k + 4, :], MB[2 + k].rearrange("p (c n) -> p c n", c=4), ACT.Copy)
                    ins.then_inc(s_m[1], 1)
                elif s == 1:
                    act.wait_ge(s_m[2], t + 1)
                    act.activation(SST[:, 0:32], MB[0][:, 0:32], ACT.Copy)
                    act.activation(SST[:, 32:64], MB[1][:, 0:32], ACT.Copy).then_inc(s_m[3], 1)
                elif s == 2:
                    act.wait_ge(s_m[5], t + 1)
                    done(act.activation(SSR[:, :], SSR[:, :], ACT.Exp, bias=MXS[0:64, 1:2], accum_out=MXS[0:64, 3:4]))
                    act.activation(MXS[0:64, 2:3], MXS[0:64, 2:3], ACT.Exp).then_inc(s_m[6], 1)
                elif s == 3:
                    act.wait_ge(s_m[8], t + 1)
                    act.activation(PST[:, :], MB[3][:, 0:64], ACT.Copy).then_inc(s_m[9], 1)

            def hg_prep(h):
                q0 = HG0[h]
                act.wait_ge(h_clamp, h + 1)
                f, g = slot(q0 + 1), slot(q0 + 3)
                act.activation(f, f, ACT.Exp, scale=-1.0)
                act.activation(EF[:, 0, :], EF[:, 0, :], ACT.Exp, scale=-1.0).then_inc(h_e, 1)
                act.wait_ge(h_f, h + 1)
                act.activation(PF[:, :], f[:, 0:SEQ], ACT.Ln).then_inc(h_g, 1)

            def runs(tile, n):
                return tile.rearrange("p (b s n) -> p b s n", s=2, n=n)

            def hg_factor(x):
                h, l = x // 8, x % 8
                if l == 0:
                    return
                n = 1 << (l - 1)
                k = l % 2
                act.wait_ge(h_k, h + 1)
                if l >= 2:
                    act.wait_ge(h_upd, 7 * h + l - 1)
                if l >= 3:
                    act.wait_ge(h_lev, 8 * h + l - 1)
                e = runs(EF[:, k, 0:SEQ], n)
                act.activation(e[:, :, 1, :], runs(PF[:, :], n)[:, :, 1, :], ACT.Exp)
                act.activation(e[:, :, 0, :], runs(SF[:, :], n)[:, :, 0, :], ACT.Exp).then_inc(h_fac, 1)

            def hg_final(h):
                act.wait_ge(h_vt, h + 1)
                act.activation(VTK[:, :, :], MB[2].rearrange("p (c n) -> p c n", c=4), ACT.Copy).then_inc(h_vtc, 1)
                act.wait_ge(h_acc, 8 * h + 8)
                act.activation(EF[:, 0, 0:SEQ], PF[:, :], ACT.Exp)
                act.activation(EF[:, 1, 0:SEQ], SF[:, :], ACT.Exp).then_inc(h_fin, 1)

            def hg(s, h):
                if s == 1:
                    act.wait_ge(h_kt, h + 1)
                    act.activation(PF[:, :], MB[2], ACT.Copy).then_inc(h_ktc, 1)
                elif s == 5:
                    act.wait_ge(h_ss, h + 1)
                    act.activation(QF[:, 1, 0:SEQ], MB[1], ACT.Sqrt, bias=EPS_RMS, scale=1.0 / DK)
                    act.activation(QF[:, 1, SEQ:T], MB[2][:, 0:DB], ACT.Sqrt, bias=EPS_RMS, scale=1.0 / DK).then_inc(h_rt, 1)

            for g in range(4):
                act.wait_ge(s_x[g], 16)
                act.activation(XH[:, 4 * g:4 * g + 4, :], Y[:, 4 * g:4 * g + 4, :], ACT.Copy).then_inc(s_xh, 1)
                if g == 0:
                    hi(0)
            for q in range(NQ):
                if q % 2 == 0 and q >= 2:
                    copy_proj(q // 2 - 1)
                if q % 4 == 0 and q // 4 + 1 < NU:
                    hi(q // 4 + 1)
                for what, n in MIX[q]:
                    if what == "att_setup":
                        att_setup(n)
                    elif what == "att_scores":
                        att_scores(n)
                    elif what == "att_turn":
                        att_turn(n)
                    elif what.startswith("smp"):
                        smp(int(what[3:]), n)
                    elif what == "hg_prep":
                        hg_prep(n)
                    elif what == "hg_factor":
                        hg_factor(n)
                    elif what == "hg_final":
                        hg_final(n)
                    elif what in ("hg1", "hg5"):
                        hg(int(what[2:]), n)
            copy_proj(2 * NU - 1)

            act.wait_ge(s_acc, 2 * NU)
            for g in range(4):
                if g >= 2:
                    act.wait_ge(s_grp, 8 if g == 2 else 10)
                act.activation(XH[:, 4 * g:4 * g + 4, :], Y[:, 4 * g:4 * g + 4, :], ACT.Copy).then_inc(s_yh, 1)
                if g == 0:
                    hi(NU)
            for u in range(NU + 1, NU + 16):
                hi(u)
            for i in range(NT):
                act.wait_ge(s_var, i + 1)
                act.activation(MV[0:TT, i, 2:3], MV[0:TT, i, 1:2], ACT.Sqrt, bias=EPS_LN[0:TT, :]).then_inc(s_sd, 1)
                act.wait_ge(s_rs, i + 1)
                act.activation(R[:, i, :], R[:, i, :], ACT.Identity, scale=MV[0:TT, i, 2:3], bias=MV[0:TT, i, 3:4]).then_inc(s_nrm, 1)
                if i >= 1:
                    turn_copies(act, act.activation, i - 1, True)
            turn_copies(act, act.activation, NT - 1, True)

            act.wait_ge(r_e, 1)
            act.activation(G4[1][:, :, :], G4[1][:, :, :], ACT.Exp).then_inc(r_x, 1)
            act.wait_ge(r_e, 2)
            act.activation(C5[2][:, :], C5[2][:, :], ACT.Exp).then_inc(r_x, 1)

            act.wait_ge(r_idx, 1)
            act.wait_ge(s_log, NT)
            nb = act.value_load(EBI[0:1, 31:32], min_val=8, max_val=MAXB - 1) + 1

            def bhi(i, m0, j):
                s, r = (i % NHL, i % NRAW) if m0 is None else ((2 + i) % NHL, (2 + i) % NRAW)
                if m0 is None:
                    act.wait_ge(b_raw[r], 16 * (i // NRAW + 1))
                    if i >= NHL:
                        act.wait_ge(b_used, i - NHL + 1)
                else:
                    act.wait_ge(b_raw[r], 16 * ((8 + i) // NRAW + 1) + 32 * (j - 1))
                    act.wait_ge(b_used, 12 * j + i - 6)
                act.activation(HIB[:, s, :], RAWB[:, r, :], ACT.Copy).then_inc(b_hi, 1)

            def silu(j):
                act.wait_ge(b_used, 12 * j + 4 if not isinstance(j, int) else 8)
                act.activation(SG[:, :], BANK[:, 0, :], ACT.Silu).then_inc(b_sg, 1)

            def token_hi(g, j):
                act.wait_ge(b_tx, 4 * j + g + 1)
                act.activation(XGH[:, 4 * g:4 * g + 4, :], BANK[:, 2 + g % 2, :].rearrange("p (c n) -> p c n", c=4), ACT.Copy).then_inc(b_xh, 1)

            def h_hi(j):
                act.wait_ge(b_th, j + 1)
                act.activation(HTH[:, :, :], BANK[:, 6, :].rearrange("p (c n) -> p c n", c=4), ACT.Copy).then_inc(b_hh, 1)

            def out_copy(n, i, j):
                act.wait_ge(b_used, 12 * j - 3 + i)
                act.activation(YO[:, 512 * n:512 * n + 512], BANK[:, 4 + n % 2, :], ACT.Copy).then_inc(b_y, 1)

            act.sem_inc(b_y, 2)
            for g in range(4):
                token_hi(g, 0)
            for i in range(8):
                bhi(i, None, 0)
            silu(0)
            for g in range(4):
                token_hi(g, 1)
            with act.Fori(1, MAXB) as j:
                with act.If(j < nb):
                    bhi(0, 0, j)
                    bhi(1, 0, j)
                    h_hi(j - 1)
                    for i in range(2, 10):
                        bhi(i, 0, j)
                    silu(j)
                    token_hi(0, j + 1)
                    bhi(10, 0, j)
                    act.wait_ge(b_yw, 16 * j)
                    out_copy(0, 8, j)
                    token_hi(1, j + 1)
                    bhi(11, 0, j)
                    out_copy(1, 9, j)
                    token_hi(2, j + 1)
                    out_copy(2, 10, j)
                    token_hi(3, j + 1)
                    out_copy(3, 11, j)
            h_hi(nb - 1)
            for n in range(3):
                bhi(n, 0, nb)
            act.wait_ge(b_yw, 16 * nb)
            out_copy(0, 0, nb)
            bhi(3, 0, nb)
            for n in range(1, 4):
                out_copy(n, n, nb)

            for i in range(NT):
                act.wait_ge(f_st, i + 1)
                act.activation(MV[0:TT, i, 2:3], MV[0:TT, i, 1:2], ACT.Sqrt, bias=EPS_LN[0:TT, :]).then_inc(f_sd, 1)
                act.wait_ge(f_rs, i + 1)
                act.activation(R[:, i, :], R[:, i, :], ACT.Identity, scale=MV[0:TT, i, 2:3], bias=MV[0:TT, i, 3:4]).then_inc(f_nm, 1)

        @block.vector
        def _(dve):
            chain = [0]

            def done(ins):
                chain[0] += 1
                ins.then_inc(s_dve, 1)
                dve.wait_ge(s_dve, chain[0])

            dve.memset(EPS_LN, LN_EPS)
            dve.memset(EPS_RMS, RMS_EPS)
            for g in range(4):
                dve.wait_ge(s_xh, g + 1)
                dve.tensor_tensor(XL[:, 4 * g:4 * g + 4, :], Y[:, 4 * g:4 * g + 4, :], XH[:, 4 * g:4 * g + 4, :].bitcast(F32), ALU.subtract).then_inc(s_xl, 1)
            dve.wait_ge(s_const, 160)
            done(dve.tensor_tensor(LBT, LBP, LBP, ALU.subtract))
            done(dve.tensor_scalar(LBT, LBT, 1.0, None, ALU.add))
            done(dve.reciprocal(OML, LBT))
            done(dve.tensor_tensor(LBT, LBT, OML, ALU.mult))
            done(dve.tensor_tensor(LB0, LBT, LBT, ALU.subtract))
            done(dve.tensor_scalar(OML, LB0, -1.0, 1.0, ALU.mult, ALU.add))

            def att_scores(s):
                t, (l, qb) = s // 8, STEPS[s % 8]
                k0 = 128 if qb == 0 else 0
                dve.wait_ge(s_sc, s + 1)
                if s >= 1:
                    dve.wait_ge(s_tp, s)
                for j in range(4):
                    h = 8 * t + 4 * l + j
                    src = MB[j // 2].rearrange("p (c n) -> p c n", c=2)[:, j % 2, k0:256]
                    ins = dve.scalar_tensor_tensor(SC[:, j, k0:256], NDIST[:, k0:256], SLOPE[h], src, ALU.mult, ALU.add)
                done(ins)
                done(dve.tensor_reduce(MX[:, 0, :], SC[:, :, k0:256], AX.X, ALU.max))
                sk = SINK[:, 8 * t + 4 * l:8 * t + 4 * l + 4]
                done(dve.tensor_tensor(MX[:, 0, :], MX[:, 0, :], sk, ALU.max))
                dve.tensor_scalar(MX[:, 1, :], MX[:, 0, :], -1.0, None, ALU.mult)
                dve.tensor_tensor(MX[:, 2, :], sk, MX[:, 0, :], ALU.subtract).then_inc(s_mx, 1)
                dve.wait_ge(s_ex, s + 1)
                done(dve.tensor_tensor(MX[:, 3, :], MX[:, 3, :], MX[:, 2, :], ALU.add))
                done(dve.reciprocal(MX[:, 3, :], MX[:, 3, :]))
                for j in range(4):
                    ins = dve.tensor_scalar(SC[:, j, k0:256], SC[:, j, k0:256], MX[:, 3, j:j + 1], None, ALU.mult)
                ins.then_inc(s_p, 1)

            def att_pv(s):
                t, (l, qb) = s // 8, STEPS[s % 8]
                dve.wait_ge(s_pv, s + 1)
                b = 64 * l
                dve.tensor_copy(Y[b:b + 64, 4 * t:4 * t + 4, 128 * qb:128 * qb + 128],
                                MB[4][b:b + 64, :].rearrange("p (c n) -> p c n", c=4)).then_inc(s_yc, 1)

            def smp(s, t):
                if s == 2:
                    dve.wait_ge(s_m[4], t + 1)
                    done(dve.tensor_tensor(SSR[:, :], MB[1][0:64, 0:128], NDS[:, t, :], ALU.add))
                    done(dve.tensor_reduce(MXS[0:64, 0:1], SSR[:, :], AX.X, ALU.max))
                    sk = SINKC[0:64, t:t + 1]
                    done(dve.tensor_tensor(MXS[0:64, 0:1], MXS[0:64, 0:1], sk, ALU.max))
                    dve.tensor_scalar(MXS[0:64, 1:2], MXS[0:64, 0:1], -1.0, None, ALU.mult)
                    dve.tensor_tensor(MXS[0:64, 2:3], sk, MXS[0:64, 0:1], ALU.subtract).then_inc(s_m[5], 1)
                    dve.wait_ge(s_m[6], t + 1)
                    done(dve.tensor_tensor(MXS[0:64, 3:4], MXS[0:64, 3:4], MXS[0:64, 2:3], ALU.add))
                    done(dve.reciprocal(MXS[0:64, 3:4], MXS[0:64, 3:4]))
                    dve.tensor_scalar(SSR[:, :], SSR[:, :], MXS[0:64, 3:4], None, ALU.mult).then_inc(s_m[7], 1)
                elif s == 4:
                    dve.wait_ge(s_m[10], t + 1)
                    dve.tensor_copy(Y[:, 4 * t:4 * t + 4, SEQ:T],
                                    MB[4][:, 0:32].rearrange("p (b g) -> p g b", b=DB)).then_inc(s_grp, 1)

            def hg_prep(h):
                q0 = HG0[h]
                q, f, v, g = (slot(q0 + k) for k in range(4))
                dve.wait_ge(s_pr, 2 * q0 + 8)
                if h:
                    dve.wait_ge(h_out, 32 * h)
                else:
                    dve.wait_ge(s_w_kv, 128)
                dve.tensor_scalar(f, f, -44.0, None, ALU.max)
                dve.tensor_scalar(EF[:, 0, :], g, -80.0, None, ALU.max).then_inc(h_clamp, 1)
                dve.wait_ge(h_e, h + 1)
                done(dve.tensor_scalar(f, f, 1.0, None, ALU.add))
                done(dve.reciprocal(f, f))
                done(dve.tensor_scalar(f, f, OML[:, h:h + 1], LB0[:, h:h + 1], ALU.mult, ALU.add))
                dve.tensor_copy(FS, f[:, SEQ:T]).then_inc(h_f, 1)
                done(dve.tensor_scalar(EF[:, 0, :], EF[:, 0, :], 1.0, None, ALU.add))
                done(dve.reciprocal(EF[:, 0, :], EF[:, 0, :]))
                dve.scalar_tensor_tensor(g, g, GAIN, EF[:, 0, :], ALU.mult, ALU.mult)
                done(dve.memset(SF[:, :], 0.0))
                dve.wait_ge(h_g, h + 1)
                dve.tensor_scalar(f, f, -1.0, 1.0, ALU.mult, ALU.add).then_inc(h_k, 1)

            def runs(tile, n):
                return tile.rearrange("p (b s n) -> p b s n", s=2, n=n)

            def hg_factor(x):
                h, l = x // 8, x % 8
                q, k = slot(HG0[h]), slot(HG0[h] + 1)
                if l == 0:
                    return
                z = l % 2
                dve.wait_ge(h_fac, 7 * h + l)
                if l >= 3:
                    dve.wait_ge(h_lev, 8 * h + l - 1)
                dve.tensor_tensor(QF[:, z, 0:SEQ], q[:, 0:SEQ], EF[:, z, 0:SEQ], ALU.mult)
                dve.tensor_tensor(EF[:, z, 0:SEQ], k[:, 0:SEQ], EF[:, z, 0:SEQ], ALU.mult).then_inc(h_mul, 1)
                n = 1 << (l - 1)
                p, s = runs(PF[:, :], n), runs(SF[:, :], n)
                nb = SEQ // (2 * n)
                done(dve.tensor_tensor(s[:, :, 0, :], s[:, :, 0, :], p[:, :, 1, n - 1:n].to_broadcast([128, nb, n]), ALU.add))
                ins = dve.tensor_tensor(p[:, :, 1, :], p[:, :, 1, :], p[:, :, 0, n - 1:n].to_broadcast([128, nb, n]), ALU.add)
                ins.then_inc(h_upd, 1)

            def hg_level(x):
                h, l = x // 8, x % 8
                dve.wait_ge(h_lev, 8 * h + l + 1)
                m = MASK[:, l:l + 1, :].to_broadcast([128, 4, 128])
                src = MB[l % 2].rearrange("p (c n) -> p c n", c=4)
                if l == 0:
                    dve.tensor_tensor(AT[:, :, :], src, m, ALU.mult).then_inc(h_acc, 1)
                else:
                    t4 = TMP[:, 0:SEQ].rearrange("p (c n) -> p c n", c=4)
                    done(dve.tensor_tensor(t4, src, m, ALU.mult))
                    dve.tensor_tensor(AT[:, :, :], AT[:, :, :], t4, ALU.add).then_inc(h_acc, 1)

            def hg(s, h):
                q0 = HG0[h]
                q, k, v, g = (slot(q0 + c) for c in range(4))
                if s == 0:
                    dve.wait_ge(h_fin, h + 1)
                    dve.tensor_copy(DEC, EF[:, 0, 127:SEQ:128])
                    dve.tensor_tensor(QF[:, 0, 0:SEQ], q[:, 0:SEQ], EF[:, 0, 0:SEQ], ALU.mult)
                    dve.tensor_tensor(EF[:, 1, 0:SEQ], k[:, 0:SEQ], EF[:, 1, 0:SEQ], ALU.mult).then_inc(h_ks, 1)
                elif s in (1, 2):
                    c = s - 1
                    if c == 0:
                        dve.wait_ge(h_s0, 16 * (h + 1))
                    b0 = 4 * c
                    st = S0[:, b0:b0 + 4, :]
                    dve.wait_ge(h_vb, 2 * h + c + 1)
                    t4 = TMP[:, 0:SEQ].rearrange("p (c n) -> p c n", c=4)
                    dve.tensor_tensor(t4, MB[4].rearrange("p (c n) -> p c n", c=4),
                                      k[:, SEQ + b0:SEQ + b0 + 4].unsqueeze(2).to_broadcast([128, 4, 128]), ALU.mult)
                    done(dve.tensor_tensor(st, st, FS[:, b0:b0 + 4].unsqueeze(2).to_broadcast([128, 4, 128]), ALU.mult))
                    dve.tensor_tensor(st, st, t4, ALU.add).then_inc(h_sn, 1)
                elif s == 3:
                    dve.wait_ge(h_u, h + 1)
                    done(dve.tensor_copy(SF[:, 0:128], MB[3][:, 0:128]))
                    for c in range(1, 4):
                        ins = dve.scalar_tensor_tensor(SF[:, 128 * c:128 * c + 128], SF[:, 128 * c - 128:128 * c], DEC[:, c:c + 1],
                                                       MB[3][:, 128 * c:128 * c + 128], ALU.mult, ALU.add)
                        if c < 3:
                            done(ins)
                    ins.then_inc(h_st, 1)
                elif s == 4:
                    dve.wait_ge(h_o, h + 1)
                    dve.tensor_copy(TMP[:, 0:SEQ], MB[0])
                    done(dve.tensor_copy(TMP[:, SEQ:T], MB[4][:, 0:DB]))
                    dve.tensor_tensor(EF[:, 0, :], TMP[:, :], TMP[:, :], ALU.mult).then_inc(h_sq, 1)
                elif s == 5:
                    dve.wait_ge(h_rt, h + 1)
                    done(dve.reciprocal(QF[:, 1, :], QF[:, 1, :]))
                    done(dve.tensor_tensor(TMP[:, :], TMP[:, :], QF[:, 1, :], ALU.mult))
                    dve.tensor_tensor(Y[:, 8 + h, :], TMP[:, :], g, ALU.mult).then_inc(s_grp, 1)

            def conv(j):
                cc, ch, cb = (slot(CV0[j] + k) for k in range(3))
                dve.wait_ge(s_pr, 2 * CV0[j] + 6)
                y = Y[:, 12 + j, :]
                w = [CW[:, 3 * j + k:3 * j + k + 1] for k in range(3)]
                done(dve.tensor_tensor(cc, cc, ch, ALU.mult))
                dve.tensor_copy(CVO[:, j, 0:2], cc[:, SEQ - 2:SEQ])
                so = CVO[:, j, 2:18].rearrange("p (b r) -> p b r", r=2)
                dve.tensor_copy(so[:, :, 0], HIST[:, j, :, 1])
                dve.tensor_copy(so[:, :, 1], cc[:, SEQ:T])
                done(dve.tensor_scalar(y, cc, w[2], None, ALU.mult))
                dve.scalar_tensor_tensor(y[:, 1:SEQ], cc[:, 0:SEQ - 1], w[1], y[:, 1:SEQ], ALU.mult, ALU.add)
                done(dve.scalar_tensor_tensor(y[:, SEQ:T], HIST[:, j, :, 1], w[1], y[:, SEQ:T], ALU.mult, ALU.add))
                dve.scalar_tensor_tensor(y[:, 2:SEQ], cc[:, 0:SEQ - 2], w[0], y[:, 2:SEQ], ALU.mult, ALU.add)
                done(dve.scalar_tensor_tensor(y[:, SEQ:T], HIST[:, j, :, 0], w[0], y[:, SEQ:T], ALU.mult, ALU.add))
                dve.tensor_tensor(y, y, cb, ALU.mult).then_inc(s_grp, 1)

            for q in range(NQ):
                for what, n in MIX[q]:
                    if what == "att_scores":
                        att_scores(n)
                    elif what == "att_pv":
                        att_pv(n)
                    elif what.startswith("smp"):
                        smp(int(what[3:]), n)
                    elif what == "hg_prep":
                        hg_prep(n)
                    elif what == "hg_factor":
                        hg_factor(n)
                    elif what == "hg_level":
                        hg_level(n)
                    elif what in ("hg0", "hg1", "hg2", "hg3", "hg4", "hg5"):
                        hg(int(what[2:]), n)
                    elif what == "conv":
                        conv(n)
            conv(3)

            for g in range(4):
                dve.wait_ge(s_yh, g + 1)
                dve.tensor_tensor(XL[:, 4 * g:4 * g + 4, :], Y[:, 4 * g:4 * g + 4, :], XH[:, 4 * g:4 * g + 4, :].bitcast(F32), ALU.subtract).then_inc(s_yl, 1)
            for n in range(4):
                for i in range(NT):
                    k = NT * n + i
                    dve.wait_ge(s_ob, k + 1)
                    if n == 0:
                        dve.wait_ge(s_r, 16 * NT)
                    r = R[:, i, 512 * n:512 * n + 512]
                    ins = dve.scalar_tensor_tensor(r, r, ALPHA, BANK[0:TT, k % 8, :], ALU.mult, ALU.add)
                    ins.then_inc(s_oe, 1)
                    dve.wait_ge(s_oe, k + 1)
                    ins = dve.bn_stats(ST[0:TT, i, n, :], r)
                    if n == 3:
                        done(ins)
                        dve.bn_aggr(MV[0:TT, i, 0:2], ST[0:TT, i, :, :].rearrange("p n s -> p (n s)")).then_inc(s_var, 1)
            dve.wait_ge(s_lg, 32)

            def rstd(i, sd, rs):
                dve.wait_ge(sd, i + 1)
                done(dve.reciprocal(MV[0:TT, i, 2:3], MV[0:TT, i, 2:3]))
                dve.scalar_tensor_tensor(MV[0:TT, i, 3:4], MV[0:TT, i, 0:1], -1.0, MV[0:TT, i, 2:3], ALU.mult, ALU.mult).then_inc(rs, 1)

            rstd(0, s_sd, s_rs)
            for i in range(NT):
                if i + 1 < NT:
                    rstd(i + 1, s_sd, s_rs)
                dve.wait_ge(s_nrm, i + 1)
                done(dve.tensor_tensor(R[:, i, :], R[:, i, :], LG[:, :], ALU.mult))
                dve.tensor_tensor(R[:, i, :], R[:, i, :], LB[:, :], ALU.add).then_inc(s_x1, 1)
                if i >= 1:
                    turn_copies(dve, dve.tensor_copy, i - 1, False)
            turn_copies(dve, dve.tensor_copy, NT - 1, False)

            dve.wait_ge(s_log, NT)
            dve.wait_ge(s_rc, 128)
            tt, ts = dve.tensor_tensor, dve.tensor_scalar

            def bc(x, *shape):
                return x.to_broadcast(list(shape))

            def col(x):
                return x[:, :].unsqueeze(2)

            done(tt(LO_G[:, :, :], BANK[0:TT, 6, 0:100].rearrange("p (i n) -> p i n", i=NT), bc(RB[:, :].unsqueeze(1), TT, NT, 20), ALU.add))
            gl, el = LO_G[:, :, 0:4], LO_G[:, :, 4:20]
            gm, gs, dif, w1, w2, v1, v2 = (C5[k] for k in range(7))
            done(dve.tensor_reduce(gm[:, :], gl, AX.X, ALU.max))
            done(tt(G4[0][:, :, :], gl, bc(col(gm), TT, NT, 4), ALU.is_equal))
            tt(G4[1][:, :, :], gl, bc(col(gm), TT, NT, 4), ALU.subtract).then_inc(r_e, 1)

            def first(hot, iota, n, tmp):
                io = bc(iota[:, :].unsqueeze(1), TT, NT, n)
                done(dve.scalar_tensor_tensor(hot, io, float(n), hot, ALU.subtract, ALU.mult))
                done(dve.tensor_reduce(tmp[:, :], hot, AX.X, ALU.min))
                done(ts(tmp[:, :], tmp[:, :], float(n), None, ALU.add))
                done(tt(hot, io, bc(col(tmp), TT, NT, n), ALU.is_equal))

            first(G4[0][:, :, :], IO4, 4, C5[7])
            ghot = G4[0][:, :, :]
            em, hot1, hot2, em2, rk, sel = (E16[k] for k in range(6))
            g16 = ghot.unsqueeze(3).to_broadcast([TT, NT, 4, 4])
            done(ts(hot2[:, :, :].rearrange("p i (g e) -> p i g e", g=4), g16, -NEG, NEG, ALU.mult, ALU.add))
            done(tt(em[:, :, :].rearrange("p i (g e) -> p i g e", g=4), el.rearrange("p i (g e) -> p i g e", g=4), g16, ALU.mult))
            done(tt(em[:, :, :], em[:, :, :], hot2[:, :, :], ALU.add))
            done(dve.tensor_reduce(v1[:, :], em[:, :, :], AX.X, ALU.max))
            done(tt(hot1[:, :, :], em[:, :, :], bc(col(v1), TT, NT, 16), ALU.is_equal))
            first(hot1[:, :, :], IO16, 16, C5[7])
            done(dve.scalar_tensor_tensor(em2[:, :, :], hot1[:, :, :], NEG, em[:, :, :], ALU.mult, ALU.add))
            done(dve.tensor_reduce(v2[:, :], em2[:, :, :], AX.X, ALU.max))
            done(tt(hot2[:, :, :], em2[:, :, :], bc(col(v2), TT, NT, 16), ALU.is_equal))
            first(hot2[:, :, :], IO16, 16, C5[7])
            tt(rk[:, :, :], hot1[:, :, :], hot2[:, :, :], ALU.add).then_inc(r_hot, 1)
            tt(dif[:, :], v2[:, :], v1[:, :], ALU.subtract).then_inc(r_e, 1)
            dve.wait_ge(r_x, 2)
            done(dve.tensor_reduce(gs[:, :], G4[1][:, :, :], AX.X, ALU.add))
            done(dve.reciprocal(gs[:, :], gs[:, :]))
            done(ts(w1[:, :], dif[:, :], 1.0, None, ALU.add))
            done(dve.reciprocal(w1[:, :], w1[:, :]))
            done(tt(w2[:, :], w1[:, :], dif[:, :], ALU.mult))
            done(tt(w1[:, :], w1[:, :], gs[:, :], ALU.mult))
            done(tt(w2[:, :], w2[:, :], gs[:, :], ALU.mult))
            dve.wait_ge(r_rank, 1)
            before = BANK[0:TT, 0, 0:80].rearrange("p (i e) -> p i e", i=NT)
            total = BANK[0:TT, 1, 0:80].rearrange("p (i e) -> p i e", i=NT)
            cnt, nblk, bstart, tmp16 = (NB16[k] for k in range(4))
            done(dve.tensor_copy(em[:, :, :], total))
            done(dve.tensor_copy(sel[:, :, :], before))
            for i in range(1, NT):
                done(tt(em2[:, i, :], em[:, i - 1, :], em2[:, i - 1, :], ALU.add) if i > 1 else dve.tensor_copy(em2[:, 1, :], em[:, 0, :]))
                done(tt(sel[:, i, :], sel[:, i, :], em2[:, i, :], ALU.add))
            done(tt(cnt[:, :], em[:, NT - 1, :], em2[:, NT - 1, :], ALU.add))
            done(ts(nblk[:, :], cnt[:, :], 0.5, None, ALU.is_ge))
            for b in range(1, NT):
                done(dve.scalar_tensor_tensor(nblk[:, :], cnt[:, :], CAP * b + 0.5, nblk[:, :], ALU.is_ge, ALU.add))
            done(dve.memset(bstart[:, 0:1], 0.0))
            for e in range(1, NE):
                done(tt(bstart[:, e:e + 1], bstart[:, e - 1:e], nblk[:, e - 1:e], ALU.add))
            done(tt(EBC[:, :, :], bc(bstart[:, :].unsqueeze(1), TT, MAXB + 1, 16), bc(IO24[:, :].unsqueeze(2), TT, MAXB + 1, 16), ALU.is_le))
            done(dve.memset(EBF[:, :], 0.0))
            done(dve.tensor_reduce(EBF[:, 0:MAXB + 1], EBC[:, :, :], AX.X, ALU.add))
            done(ts(EBF[:, 0:MAXB + 1], EBF[:, 0:MAXB + 1], -1.0, None, ALU.add))
            done(dve.scalar_tensor_tensor(EBF[:, 31:32], bstart[:, 15:16], -1.0, nblk[:, 15:16], ALU.add, ALU.add))
            dve.tensor_copy(EBI[:, :], EBF[0:1, :])
            for c, hot, w in ((0, hot1, w1), (1, hot2, w2)):
                r, b, bb, row = C5[8], C5[9], C5[10], C5[11 + c]
                done(tt(em[:, :, :], hot[:, :, :], sel[:, :, :], ALU.mult))
                done(dve.tensor_reduce(r[:, :], em[:, :, :], AX.X, ALU.add))
                done(tt(em[:, :, :], hot[:, :, :], bc(bstart[:, :].unsqueeze(1), TT, NT, 16), ALU.mult))
                done(dve.tensor_reduce(b[:, :], em[:, :, :], AX.X, ALU.add))
                done(ts(bb[:, :], r[:, :], CAP - 0.5, None, ALU.is_ge))
                for k in range(2, NT):
                    done(dve.scalar_tensor_tensor(bb[:, :], r[:, :], CAP * k - 0.5, bb[:, :], ALU.is_ge, ALU.add))
                done(tt(b[:, :], b[:, :], bb[:, :], ALU.add))
                done(dve.scalar_tensor_tensor(r[:, :], bb[:, :], -float(CAP), r[:, :], ALU.mult, ALU.add))
                done(ts(row[:, :], TID[:, :], float(c * T), None, ALU.add))
                tt(OH[:, c, :, :], bc(IO128[:, :].unsqueeze(1), TT, NT, 128), bc(col(r), TT, NT, 128), ALU.is_equal)
                one = TB[:, c, :, 0, :]
                done(tt(one, bc(IO24[:, :].unsqueeze(1), TT, NT, MAXB + 1), bc(col(b), TT, NT, MAXB + 1), ALU.is_equal))
                done(tt(TB[:, c, :, 1, :], one, bc(col(w), TT, NT, MAXB + 1), ALU.mult))
                done(tt(TB[:, c, :, 2, :], one, bc(col(row), TT, NT, MAXB + 1), ALU.mult))
                tt(one, one, bc(TID[:, :].unsqueeze(2), TT, NT, MAXB + 1), ALU.mult).then_inc(r_tab, 1)
                dve.wait_ge(r_tab, c + 1)
            dve.wait_ge(r_tabm, 1)
            done(dve.tensor_copy(TABF[:, :, :], BANK[:, 2, 0:3 * (MAXB + 1)].rearrange("p (k j) -> p k j", k=3)))
            for k, dst, skip in ((0, TIX, SKP[:, 0:1]), (2, YIX, SKIP)):
                v = TABF[:, k, :]
                done(ts(TABZ[:, :], v, 0.0, skip, ALU.is_equal, ALU.mult))
                done(ts(v, v, -1.0, 0.0, ALU.add, ALU.max))
                done(tt(TABZ[:, :], TABZ[:, :], v, ALU.add))
                if k == 0:
                    done(dve.tensor_copy(dst[:, :], TABZ[:, :]))
                else:
                    dve.tensor_copy(dst[:, :], TABZ[:, :]).then_inc(r_idx, 1)

            dve.wait_ge(r_idx, 1)
            nb = dve.value_load(EBI[0:1, 31:32], min_val=8, max_val=MAXB - 1) + 1

            def blo(i, m0, j):
                if i in POOL_LO:
                    return
                s, r = (i % NHL, i % NRAW) if m0 is None else ((2 + i) % NHL, (2 + i) % NRAW)
                dve.wait_ge(b_hi, i + 1 if m0 is None else 12 * j + i - 3)
                dve.tensor_tensor(LOB[:, s, :], RAWB[:, r, :], HIB[:, s, :].bitcast(F32), ALU.subtract).then_inc(b_lo[s], 1)

            def h_made(j):
                dve.wait_ge(b_sg, j + 1)
                if not isinstance(j, int) or j >= 1:
                    dve.wait_ge(b_th, j)
                dve.scalar_tensor_tensor(H[:, :], SG[:, :], TABF[:, 1, bass.ds(j, 1)], BANK[:, 1, :], ALU.mult, ALU.mult).then_inc(b_h, 1)

            def token_lo(g, j):
                dve.wait_ge(b_xh, 4 * j + g + 1)
                dve.tensor_tensor(XGL[:, 4 * g:4 * g + 4, :], BANK[:, 2 + g % 2, :].rearrange("p (c n) -> p c n", c=4),
                                  XGH[:, 4 * g:4 * g + 4, :].bitcast(F32), ALU.subtract).then_inc(b_xl, 1)

            def h_lo(j):
                dve.wait_ge(b_hh, j + 1)
                dve.tensor_tensor(HTL[:, :, :], BANK[:, 6, :].rearrange("p (c n) -> p c n", c=4), HTH[:, :, :].bitcast(F32),
                                  ALU.subtract).then_inc(b_hl, 1)

            for g in range(4):
                token_lo(g, 0)
            for i in range(8):
                blo(i, None, 0)
            h_made(0)
            for g in range(4):
                token_lo(g, 1)
            with dve.Fori(1, MAXB) as j:
                with dve.If(j < nb):
                    blo(0, 0, j)
                    blo(1, 0, j)
                    h_lo(j - 1)
                    for i in range(2, 10):
                        blo(i, 0, j)
                    h_made(j)
                    token_lo(0, j + 1)
                    blo(10, 0, j)
                    token_lo(1, j + 1)
                    blo(11, 0, j)
                    token_lo(2, j + 1)
                    token_lo(3, j + 1)
            h_lo(nb - 1)
            for n in range(4):
                dve.wait_ge(b_hi, 12 * nb + n - 3)
                s, r = (2 + n) % NHL, (2 + n) % NRAW
                dve.tensor_tensor(LOB[:, s, :], RAWB[:, r, :], HIB[:, s, :].bitcast(F32), ALU.subtract).then_inc(b_lo[s], 1)

            dve.wait_ge(f_ln, 32)

            def added(i):
                dve.wait_ge(f_in[i % 2], 32 * (i // 2 + 1))
                r = R[:, i, :]
                done(dve.scalar_tensor_tensor(r, r, ALPHA, YA[:, i % 2, :], ALU.mult, ALU.add))
                done(tt(r, r, YB[:, i % 2, :], ALU.add))
                for n in range(4):
                    ins = dve.bn_stats(ST[0:TT, i, n, :], R[:, i, 512 * n:512 * n + 512])
                done(ins)
                dve.bn_aggr(MV[0:TT, i, 0:2], ST[0:TT, i, :, :].rearrange("p n s -> p (n s)")).then_inc(f_st, 1)

            added(0)
            rstd(0, f_sd, f_rs)
            for i in range(NT):
                if i + 1 < NT:
                    added(i + 1)
                    rstd(i + 1, f_sd, f_rs)
                dve.wait_ge(f_nm, i + 1)
                done(tt(R[:, i, :], R[:, i, :], LG2[:, :], ALU.mult))
                tt(R[:, i, :], R[:, i, :], LB2[:, :], ALU.add).then_inc(f_y, 1)

        @block.tensor
        def _(pe):
            def quarter(u, hf, kq):
                m = 2 * u + hf
                if hf == 0 and kq == 0:
                    pe.wait_ge(s_hi, u + 1)
                    pe.wait_ge(s_lo, u + 1)
                if kq == 0 and m >= 3:
                    pe.wait_ge(s_pr, m - 2)
                hw = HI[:, u % 2, :].rearrange("p (c n) -> p c n", c=KC)
                lw = LO[:, u % 2, :].rearrange("p (c n) -> p c n", c=KC)
                cols = slice(hf * HALF, (hf + 1) * HALF)
                for c in range(8 * kq, 8 * kq + 8):
                    if u == 0 and hf == 0 and c % 4 == 0:
                        pe.wait_ge(s_xl, c // 4 + 1)
                    pe.matmul(acc(m), hw[:, c, :], XH[:, c, cols], start=(c == 0), stop=False)
                    pe.matmul(acc(m), hw[:, c, :], XL[:, c, cols], start=False, stop=False)
                    ins = pe.matmul(acc(m), lw[:, c, :], XH[:, c, cols], start=False, stop=(c == KC - 1))
                if kq == 1:
                    ins.then_inc(s_acc, 1)

            def att_setup(t):
                u0 = ATT0[t]
                pe.wait_ge(s_pr, 2 * u0 + 12)
                pe.wait_ge(s_const, 160)
                if t:
                    pe.wait_ge(s_grp, t)
                for c in range(4):
                    ins = pe.transpose(MB[2][:, 128 * c:128 * c + 128], slot(u0 + 1)[:, 128 * c:128 * c + 128], IDENT[:, :])
                ins.then_inc(s_vt_t, 1)
                for k in range(2):
                    ins = pe.transpose(MB[3][0:DB, 128 * k:128 * k + 128], slot(u0 + k)[:, SEQ:T], IDENT[:, :])
                ins.then_inc(s_vt_t, 1)

            def att_scores(s):
                t, (l, qb) = s // 8, STEPS[s % 8]
                u0, b = ATT0[t], 64 * l
                k0 = 128 if qb == 0 else 0
                if s >= 1:
                    pe.wait_ge(s_mx, s)
                for j in range(4):
                    dst = MB[j // 2].rearrange("p (c n) -> p c n", c=2)[:, j % 2, k0:256]
                    ins = pe.matmul(dst, slot(u0 + 2 + j)[b:b + 64, 128 * qb:128 * qb + 128],
                                    slot(u0)[b:b + 64, 128 * qb - 128 + k0:128 * qb + 128], start=True, stop=True)
                ins.then_inc(s_sc, 1)

            def att_turn(s):
                t, (l, qb) = s // 8, STEPS[s % 8]
                pe.wait_ge(s_p, s + 1)
                if s >= 1:
                    pe.wait_ge(s_pt, s)
                pe.wait_ge(s_vt, 2 * t + 2)
                for k in range(1 if qb == 0 else 0, 2):
                    for j in range(4):
                        ins = pe.transpose(MB[2 + k][:, 128 * j:128 * j + 128], SC[:, j, 128 * k:128 * k + 128], IDENT[:, :])
                ins.then_inc(s_tp, 1)

            def att_pv(s):
                t, (l, qb) = s // 8, STEPS[s % 8]
                b = 64 * l
                pe.wait_ge(s_pt, s + 1)
                if s >= 1:
                    pe.wait_ge(s_yc, s)
                ks = [1] if qb == 0 else [0, 1]
                for k in ks:
                    ins = pe.matmul(MB[4][b:b + 64, :], VT[:, qb - 1 + k, b:b + 64], PT[:, k, :, :],
                                    start=(k == ks[0]), stop=(k == 1))
                ins.then_inc(s_pv, 1)

            def smp(s, t):
                u0 = ATT0[t]
                if s == 0:
                    pe.wait_ge(s_kc, 32 * (t + 1))
                    pe.wait_ge(s_self, 32 * (t + 1))
                    pe.wait_ge(s_pt, 8 * t + 8)
                    for b in range(DB):
                        ins = pe.transpose(MB[2 + b // 4][:, 128 * (b % 4):128 * (b % 4) + 128], KCA[:, b, :], IDENT[:, :])
                    ins.then_inc(s_m[0], 1)
                elif s == 1:
                    pe.wait_ge(s_m[1], t + 1)
                    pe.wait_ge(s_mx, 8 * t + 8)
                    for b in range(DB):
                        for l in range(2):
                            s0 = (u0 + 2) % 16
                            ins = pe.matmul(MB[l][:, 4 * b:4 * b + 4], KTS[64 * l:64 * l + 64, b, :],
                                            PR[64 * l:64 * l + 64, s0:s0 + 4, SEQ + b], start=True, stop=True)
                    ins.then_inc(s_m[2], 1)
                elif s == 2:
                    pe.wait_ge(s_m[3], t + 1)
                    pe.transpose(MB[1][0:64, 0:128], SST[:, :], IDENT[:, :]).then_inc(s_m[4], 1)
                elif s == 3:
                    pe.wait_ge(s_m[7], t + 1)
                    pe.transpose(MB[3][:, 0:64], SSR[:, :], IDENT[0:64, 0:64]).then_inc(s_m[8], 1)
                elif s == 4:
                    pe.wait_ge(s_m[9], t + 1)
                    pe.wait_ge(s_yc, 8 * t + 8)
                    for b in range(DB):
                        for l in range(2):
                            c = 32 * l + 4 * b
                            ins = pe.matmul(MB[4][64 * l:64 * l + 64, 4 * b:4 * b + 4], VCA[:, b, 64 * l:64 * l + 64],
                                            PST[:, c:c + 4], start=True, stop=True)
                    ins.then_inc(s_m[10], 1)

            def hg_level(x):
                h, l = x // 8, x % 8
                q, k = slot(HG0[h]), slot(HG0[h] + 1)
                z = l % 2
                if l == 0:
                    pe.wait_ge(h_k, h + 1)
                else:
                    pe.wait_ge(h_mul, 7 * h + l)
                if l >= 2:
                    pe.wait_ge(h_acc, 8 * h + l - 1)
                for c in range(4):
                    cols = slice(128 * c, 128 * c + 128)
                    kk, qq = (k[:, cols], q[:, cols]) if l == 0 else (EF[:, z, cols], QF[:, z, cols])
                    ins = pe.matmul(MB[l % 2][:, cols], kk, qq, start=True, stop=True)
                ins.then_inc(h_lev, 1)
                if l == 4:
                    v = slot(HG0[h] + 2)
                    for c in range(4):
                        ins = pe.transpose(MB[2][:, 128 * c:128 * c + 128], v[:, 128 * c:128 * c + 128], IDENT[:, :])
                    ins.then_inc(h_vt, 1)

            def spread(h, c):
                v = slot(HG0[h] + 2)
                if c:
                    pe.wait_ge(h_sn, 2 * h + c)
                for b in range(4):
                    t = SEQ + 4 * c + b
                    ins = pe.matmul(MB[4][:, 128 * b:128 * b + 128], v[:, t:t + 1].to_broadcast([128, 128]), IDENT[:, :], start=True, stop=True)
                ins.then_inc(h_vb, 1)

            def hg(s, h):
                q = slot(HG0[h])
                if s == 0:
                    spread(h, 0)
                elif s == 1:
                    pe.wait_ge(h_ks, h + 1)
                    pe.wait_ge(h_vtc, h + 1)
                    for c in range(4):
                        ins = pe.transpose(MB[2][:, 128 * c:128 * c + 128], EF[:, 1, 128 * c:128 * c + 128], IDENT[:, :])
                    ins.then_inc(h_kt, 1)
                elif s == 2:
                    spread(h, 1)
                    pe.wait_ge(h_ktc, h + 1)
                    for c in range(4):
                        ins = pe.matmul(MB[3][:, 128 * c:128 * c + 128], PF[:, 128 * c:128 * c + 128], VTK[:, c, :], start=True, stop=True)
                    ins.then_inc(h_u, 1)
                elif s == 4:
                    pe.wait_ge(h_st, h + 1)
                    pe.wait_ge(h_sn, 2 * h + 2)
                    pe.wait_ge(h_acc, 8 * h + 8)
                    for c in range(4):
                        cols = slice(128 * c, 128 * c + 128)
                        pe.matmul(MB[0][:, cols], VTK[:, c, :], AT[:, c, :], start=True, stop=(c == 0))
                        if c:
                            pe.matmul(MB[0][:, cols], SF[:, 128 * c - 128:128 * c], QF[:, 0, cols], start=False, stop=True)
                    for b in range(DB):
                        ins = pe.matmul(MB[4][:, b:b + 1], S0[:, b, :], q[:, SEQ + b:SEQ + b + 1], start=True, stop=True)
                    ins.then_inc(h_o, 1)
                elif s == 5:
                    pe.wait_ge(h_sq, h + 1)
                    pe.wait_ge(s_ones, 1)
                    pe.matmul(MB[1], ONES[:, :], EF[:, 0, 0:SEQ], start=True, stop=True)
                    pe.matmul(MB[2][:, 0:DB], ONES[:, :], EF[:, 0, SEQ:T], start=True, stop=True).then_inc(h_ss, 1)

            for q in range(NQ):
                quarter(q // 4, q % 4 // 2, q % 2)
                for what, n in MIX[q]:
                    if what == "att_setup":
                        att_setup(n)
                    elif what == "att_scores":
                        att_scores(n)
                    elif what == "att_turn":
                        att_turn(n)
                    elif what == "att_pv":
                        att_pv(n)
                    elif what.startswith("smp"):
                        smp(int(what[3:]), n)
                    elif what == "hg_level":
                        hg_level(n)
                    elif what in ("hg0", "hg1", "hg2", "hg4", "hg5"):
                        hg(int(what[2:]), n)

            for n in range(4):
                for g in range(4):
                    u = NU + 4 * n + g
                    pe.wait_ge(s_hi, u + 1)
                    pe.wait_ge(s_lo, u + 1)
                    if n == 0:
                        pe.wait_ge(s_yl, g + 1)
                        if g == 0:
                            pe.wait_ge(s_pr, 2 * NU)
                            pe.wait_ge(s_grp, 8)
                    hw = HI[:, u % 2, :].rearrange("p (c n) -> p c n", c=4)
                    lw = LO[:, u % 2, :].rearrange("p (c n) -> p c n", c=4)
                    for i in range(NT):
                        k = NT * n + i
                        if g == 0 and k >= 8:
                            pe.wait_ge(s_oe, k - 7)
                        b = BANK[0:TT, k % 8, :]
                        rows = slice(i * TT, (i + 1) * TT)
                        for c in range(4):
                            cc = 4 * g + c
                            pe.matmul(b, XH[:, cc, rows], hw[:, c, :], start=(cc == 0), stop=False)
                            pe.matmul(b, XL[:, cc, rows], hw[:, c, :], start=False, stop=False)
                            ins = pe.matmul(b, XH[:, cc, rows], lw[:, c, :], start=False, stop=(cc == KC - 1))
                        if g == 3:
                            ins.then_inc(s_ob, 1)
                        elif i == NT - 1:
                            ins.then_inc(s_used, 1)

            pe.wait_ge(s_oe, 4 * NT)
            for i in range(NT):
                pe.wait_ge(s_x1, i + 1)
                for g in range(4):
                    k = 4 * i + g
                    if k >= 6:
                        w = (k - 6) // 4, (k - 6) % 4
                        (pe.wait_ge(s_t1a, 2 * w[0] + w[1] // 2 + 1) if w[1] % 2 == 0 else pe.wait_ge(s_t1d, 2 * w[0] + w[1] // 2 + 1))
                    for c in range(4):
                        cc = 4 * g + c
                        ins = pe.transpose(BANK[:, k % 6, c * TT:(c + 1) * TT], R[:, i, 128 * cc:128 * cc + 128], IDENT[0:TT, 0:TT])
                    ins.then_inc(s_t1, 1)
                pe.wait_ge(s_t1a, 2 * i + 2)
                pe.wait_ge(s_t1d, 2 * i + 2)
                if i == 0:
                    pe.wait_ge(s_wr, 16)
                for c in range(KC):
                    ins = pe.matmul(BANK[0:TT, 6, 20 * i:20 * i + 20], X1T[:, i % 2, c, :], WR[:, c, :], start=(c == 0), stop=(c == KC - 1))
                ins.then_inc(s_log, 1)
            pe.wait_ge(r_hot, 1)
            pe.wait_ge(s_rc, 128)
            hot = E16[4][:, :, :].rearrange("p i e -> p (i e)")
            pe.matmul(BANK[0:TT, 0, 0:80], TRI[:, :], hot, start=True, stop=True)
            pe.matmul(BANK[0:TT, 1, 0:80], ONES[0:TT, 0:TT], hot, start=True, stop=True).then_inc(r_rank, 1)
            pe.wait_ge(r_tab, 2)
            for c in range(2):
                for i in range(NT):
                    ins = pe.matmul(BANK[:, 2, 0:3 * (MAXB + 1)], OH[:, c, i, :], TB[:, c, i, :, :].rearrange("p k j -> p (k j)"),
                                    start=(c == 0 and i == 0), stop=(c == 1 and i == NT - 1))
            ins.then_inc(r_tabm, 1)

            pe.wait_ge(r_idx, 1)
            nb = pe.value_load(EBI[0:1, 31:32], min_val=8, max_val=MAXB - 1) + 1

            def tokens(g, j):
                if g == 0:
                    pe.wait_ge(b_yw, 16) if isinstance(j, int) and j == 0 else pe.wait_ge(b_xg, 16 * j)
                if not isinstance(j, int) or 4 * j + g >= 2:
                    pe.wait_ge(b_xl, 4 * j + g - 1)
                for c in range(4):
                    ins = pe.transpose(BANK[:, 2 + g % 2, 128 * c:128 * c + 128], XG[:, 4 * g + c:D:KC], IDENT[:, :])
                ins.then_inc(b_tx, 1)

            def ready(i, m0, j):
                s = i % NHL if m0 is None else (2 + i) % NHL
                pe.wait_ge(b_lo[s], i // NHL + 1 if m0 is None else (8 + i) // NHL + 1 + 4 * (j - 1))
                return HIB[:, s, :].rearrange("p (c n) -> p c n", c=4), LOB[:, s, :].rearrange("p (c n) -> p c n", c=4)

            def gate_up(j, m0):
                pe.wait_ge(b_xl, 4 * j + 4)
                if m0 is not None:
                    pe.wait_ge(b_h, j)
                for i in range(8):
                    hw, lw = ready(i, m0, j)
                    b = BANK[:, i % 2, :]
                    for c in range(4):
                        cc = 4 * (i // 2) + c
                        pe.matmul(b, XGH[:, cc, :], hw[:, c, :], start=(cc == 0), stop=False)
                        pe.matmul(b, XGL[:, cc, :], hw[:, c, :], start=False, stop=False)
                        ins = pe.matmul(b, XGH[:, cc, :], lw[:, c, :], start=False, stop=(cc == KC - 1))
                    ins.then_inc(b_used, 1)

            def turn_h(j):
                pe.wait_ge(b_h, j + 1)
                if not isinstance(j, int):
                    pe.wait_ge(b_hl, j)
                for c in range(4):
                    ins = pe.transpose(BANK[:, 6, 128 * c:128 * c + 128], H[:, c:512:4], IDENT[:, :])
                ins.then_inc(b_th, 1)

            def down(n, i, j):
                if n == 0:
                    pe.wait_ge(b_hl, j)
                pe.wait_ge(b_y, 4 * (j - 1) + n + 1)
                hw, lw = ready(i, 0, j)
                b = BANK[:, 4 + n % 2, :]
                for c in range(4):
                    pe.matmul(b, HTH[:, c, :], hw[:, c, :], start=(c == 0), stop=False)
                    pe.matmul(b, HTL[:, c, :], hw[:, c, :], start=False, stop=False)
                    ins = pe.matmul(b, HTH[:, c, :], lw[:, c, :], start=False, stop=(c == 3))
                ins.then_inc(b_used, 1)

            for g in range(4):
                tokens(g, 0)
            gate_up(0, None)
            for g in range(4):
                tokens(g, 1)
            turn_h(0)
            with pe.Fori(1, MAXB) as j:
                with pe.If(j < nb):
                    gate_up(j, 0)
                    for n in range(4):
                        tokens(n, j + 1)
                        down(n, 8 + n, j)
                    turn_h(j)
            for n in range(4):
                down(n, n, nb)


def kernel(x_prompt, x_sample, state_conv, state_hgrn, cache_k_win, cache_v_win,
           w_in, w_out, conv_w, hg_lb_param, hg_gain, attn_sinks, ln1_g, ln1_b,
           w_group, b_group, w_router, b_router, w_gate, w_up, w_down, ln2_g, ln2_b):
    import concourse.bacc as bacc
    from concourse.bass_utils import run_bass_kernel_spmd as run

    A = np.asarray
    x = np.concatenate([A(x_prompt)[0], A(x_sample)[:, 0]], axis=0)
    arrays = {
        "x": x,
        "xT": x.reshape(T, KC, 128).transpose(2, 1, 0).reshape(128, KC * T),
        "w_in": A(w_in)[0][:, feature_order()].reshape(KC, 128, NU, 128).transpose(2, 1, 0, 3).reshape(NU, 128, 2048),
        "w_out": A(w_out)[0][mix_order()].reshape(4, 4, 128, 4, 512).transpose(3, 0, 2, 1, 4).reshape(16, 128, 2048),
        "w_gate": A(w_gate)[0].reshape(NE, 128, KC * 512),
        "w_up": A(w_up)[0].reshape(NE, 128, KC * 512),
        "w_down": A(w_down)[0].reshape(NE, 128, 4, D),
        "wr": np.concatenate([A(w_group)[0], A(w_router)[0]], axis=1).reshape(KC, 128, 20).transpose(1, 0, 2),
        "rb": np.broadcast_to(np.concatenate([A(b_group)[0], A(b_router)[0]]), (TT, 20)),
        "sink": np.broadcast_to(A(attn_sinks)[0], (128, 16)),
        "sinkc": np.broadcast_to(A(attn_sinks)[0].reshape(2, 2, 1, 4), (2, 2, DB, 4)).reshape(2, 64).T,
        "gain": A(hg_gain)[0].reshape(128, 1),
        "lbp": A(hg_lb_param)[0].reshape(4, 128).T,
        "cw": A(conv_w)[0].reshape(3, 4, 128).transpose(2, 1, 0).reshape(128, 12),
        "hist": A(state_conv)[0].reshape(DB, 2, 4, 128).transpose(3, 2, 0, 1).reshape(128, 64),
        "s0": A(state_hgrn)[0].transpose(1, 2, 0, 3),
        "cache_k": A(cache_k_win)[0].reshape(DB, WIN, 256),
        "cache_v": A(cache_v_win)[0].reshape(DB, WIN, 256),
        "ln1g": np.broadcast_to(A(ln1_g)[0], (TT, D)),
        "ln1b": np.broadcast_to(A(ln1_b)[0], (TT, D)),
        "ln2g": np.broadcast_to(A(ln2_g)[0], (TT, D)),
        "ln2b": np.broadcast_to(A(ln2_b)[0], (TT, D)),
    }
    f = np.float32
    i, j = np.arange(128)[:, None], np.arange(256)[None, :]
    dist = i + WIN - j
    s, t = np.arange(128)[:, None], np.arange(128)[None, :]
    levels = [s == t] + [(s // (2 * n) == t // (2 * n)) & (s % (2 * n) < n) & (t % (2 * n) >= n) for n in (1, 2, 4, 8, 16, 32, 64)]
    row = np.arange(64)[:, None]
    head = 8 * np.arange(2)[None, :] + 4 * (row // 32) + row % 4
    slope = np.array(SLOPE, f)[head]
    arrays |= {
        "ident": np.eye(128, dtype=f),
        "ndist": np.where((dist >= 0) & (dist < WIN), -dist, NEG).astype(f),
        "mask": np.stack(levels, axis=1).astype(np.float16),
        "nds": (-slope[:, :, None] * (127 - np.arange(128))[None, None, :].astype(f)).astype(f),
        "tri": (np.arange(TT)[:, None] < np.arange(TT)[None, :]).astype(f),
        "io128": np.broadcast_to(np.arange(128, dtype=f), (TT, 128)),
        "io24": np.broadcast_to(np.arange(MAXB + 1, dtype=f), (TT, MAXB + 1)),
        "io4": np.broadcast_to(np.arange(4, dtype=f), (TT, 4)),
        "io16": np.broadcast_to(np.arange(16, dtype=f), (TT, 16)),
        "tid": (np.arange(TT)[:, None] + TT * np.arange(NT)[None, :] + 1).astype(f),
        "skp": np.where(np.arange(128)[:, None] > 0, SKIP, 0.0).astype(f),
    }
    outs = {"yp": (SEQ, D), "ys": (DB, D), "cs": (128, 4, 18), "hp": (4, 128, 128), "hs": (4, 128, DB, 128),
            "kp": (2, 128, 128), "vp": (2, 128, 128), "ks": (2, 128, DB, 128), "vs": (2, 128, DB, 128)}

    nc = bacc.Bacc("TRN2", target_bir_lowering=False, num_devices=1)
    arrays = {n: np.ascontiguousarray(v) for n, v in arrays.items()}
    a = {n: nc.dram_tensor(f"in_{n}", v.shape, mybir.dt.from_np(v.dtype), kind="ExternalInput").ap() for n, v in arrays.items()}
    o = {n: nc.dram_tensor(f"out_{n}", sh, F32, kind="ExternalOutput").ap() for n, sh in outs.items()}
    build(nc, a, o)
    r = run(nc, [{f"in_{n}": v for n, v in arrays.items()}], core_ids=[0]).results[0]
    r = {n: r[f"out_{n}"] for n in outs}

    cs = r["cs"].transpose(2, 1, 0).reshape(18, 512)
    return (
        r["yp"].reshape(1, SEQ, D),
        r["ys"].reshape(DB, 1, D),
        cs[0:2].reshape(1, 1, 2, 512),
        cs[2:18].reshape(1, DB, 2, 512),
        r["hp"].reshape(1, 1, 4, 128, 128),
        r["hs"].transpose(2, 0, 1, 3).reshape(1, DB, 4, 128, 128),
        r["kp"].transpose(2, 0, 1).reshape(1, 1, WIN, 4, HD),
        r["ks"].transpose(2, 1, 0, 3).reshape(1, DB, WIN, 4, HD),
        r["vp"].transpose(1, 0, 2).reshape(1, 1, WIN, 4, HD),
        r["vs"].transpose(2, 1, 0, 3).reshape(1, DB, WIN, 4, HD),
    )
```

```python
import math
from contextlib import ExitStack

import numpy as np
import concourse.bass as bass
from concourse import mybir

F32 = mybir.dt.float32
F32R = mybir.dt.float32r
F16 = mybir.dt.float16
I32 = mybir.dt.int32
ALU = mybir.AluOpType
ACT = mybir.ActivationFunctionType
AX = mybir.AxisListType

D = 2048
SEQ, DB = 512, 8
T = SEQ + DB
HALF = T // 2
NT, TT = 5, T // 5
KC = D // 128
NU = 40
HD, WIN = 64, 128
NE, EPG, NG = 16, 4, 4
CAP = 128
MAXB = (2 * T - NE) // CAP + NE
DK = 128
ALPHA = 2.0 ** 0.25
LN_EPS, RMS_EPS = 1e-5, 1e-6
SLOPE = [2.0 ** (-8.0 * (h + 1) / 16) for h in range(16)]
NEG = -3e38
AHEAD = 3
SKIP = 4096.0

ATT0 = [0, 6]
HG0 = [12 + 4 * h for h in range(4)]
CV0 = [28 + 3 * j for j in range(4)]


def feature_order():
    cc, ch, cb = 512, 1024, 0
    hq, hf, hi, hg = 1536, 2048, 2560, 3072
    aq, ak, av = 3584, 4608, 4864
    out = []
    for t in range(2):
        out += [np.arange(ak + 128 * t, ak + 128 * t + 128), np.arange(av + 128 * t, av + 128 * t + 128)]
        for j in range(4):
            out.append(np.concatenate([np.arange(aq + 64 * h, aq + 64 * h + 64) for h in (8 * t + j, 8 * t + 4 + j)]))
    for h in range(4):
        out += [np.arange(b + 128 * h, b + 128 * h + 128) for b in (hq, hf, hi, hg)]
    for j in range(4):
        out += [np.arange(b + 128 * j, b + 128 * j + 128) for b in (cc, ch, cb)]
    return np.concatenate(out)


def mix_order():
    out = []
    for t in range(2):
        for j in range(4):
            out.append(np.concatenate([np.arange(1024 + 64 * h, 1024 + 64 * h + 64) for h in (8 * t + j, 8 * t + 4 + j)]))
    out += [np.arange(512 + 128 * h, 512 + 128 * h + 128) for h in range(4)]
    out += [np.arange(128 * j, 128 * j + 128) for j in range(4)]
    return np.concatenate(out)


NQ = 4 * NU
STEPS = [(l, qb) for l in range(2) for qb in range(4)]


def schedule():
    at = {q: [] for q in range(NQ + 40)}
    for t in range(2):
        b = (24, 56)[t]
        at[b].append(("att_setup", t))
        for i in range(8):
            at[b + 1 + 3 * i].append(("att_scores", 8 * t + i))
            at[b + 4 + 3 * i].append(("att_turn", 8 * t + i))
            at[b + 5 + 3 * i].append(("att_pv", 8 * t + i))
        for s, q in enumerate((26, 27, 28, 30, 31)):
            at[b + q].append((f"smp{s}", t))
    for h in range(4):
        b = 90 + 17 * h
        at[b - (6 if h else 3)].append(("hg_prep", h))
        at[b - 2].append(("hg_k", h))
        for l in range(8):
            at[b + l].append(("hg_factor", 8 * h + l))
            at[b + l + 1].append(("hg_level", 8 * h + l))
        at[b + 8].append(("hg_final", h))
        for s in range(6):
            at[b + 9 + s].append((f"hg{s}", h))
    for j, q in enumerate((139, 150, NQ - 3)):
        at[q].append(("conv", j))
    return at


def build(nc, a, o):
    MIX = schedule()
    x1_rows = nc.dram_tensor("x1_rows", [T, D], F32, kind="Internal").ap()
    y_rows = nc.dram_tensor("y_rows", [2 * T, D], F32, kind="Internal").ap()

    base = (nc.sbuf_base + 63) // 64 * 64

    def sb(name, shape, dt, off):
        return nc.alloc_sbuf_tensor_at(name, shape, dt, offset=base + off)

    IDENT = sb("IDENT", [128, 128], F32, 0)
    ONES = sb("ONES", [128, 128], F32, 512)
    NDIST = sb("NDIST", [128, 256], F32, 1024)
    MASK = sb("MASK", [128, 8, 128], F16, 2048)
    NDS = sb("NDS", [64, 2, 128], F32, 4096)
    SM = sb("SM", [128, 512], F32, 5120)
    O_RING = 7168
    RAW = sb("RAW", [128, 2, 2048], F32, O_RING)
    HI = sb("HI", [128, 2, 2048], F32R, O_RING + 16384)
    LO = sb("LO", [128, 2, 2048], F32R, O_RING + 32768)
    O_XT = O_RING + 49152
    XH = sb("XH", [128, KC, T], F32R, O_XT)
    XL = sb("XL", [128, KC, T], F32R, O_XT + 33280)
    O_Y = O_XT + 66560
    Y = sb("Y", [128, KC, T], F32, O_Y)
    O_PR = O_Y + 33280
    PR = sb("PR", [128, 16, T], F32, O_PR)
    O_T = O_PR + 33280
    SC = sb("SC", [128, 4, 256], F32, O_T)
    PT = sb("PT", [128, 2, 4, 128], F32, O_T + 4096)
    VT = sb("VT", [128, 4, 128], F32, O_T + 8192)
    KCA = sb("KCA", [128, DB, 128], F32, O_T + 10240)
    VCA = sb("VCA", [128, DB, 128], F32, O_T + 14336)
    SELF = sb("SELF", [DB, 2, 128], F32, O_T + 18432)
    KTS = sb("KTS", [128, DB, 128], F32, O_T)
    SST = sb("SST", [128, 64], F32, O_T + 19456)
    SSR = sb("SSR", [64, 128], F32, O_T + 19712)
    PST = sb("PST", [128, 64], F32, O_T + 20224)
    PF = sb("PF", [128, SEQ], F32, O_T)
    SF = sb("SF", [128, SEQ], F32, O_T + 2048)
    AT = sb("AT", [128, 4, 128], F32, O_T + 4096)
    TMP = sb("TMP", [128, T], F32, O_T + 6144)
    VTK = sb("VTK", [128, 4, 128], F32, O_T + 8256)
    EF = sb("EF", [128, 2, T], F32, O_T + 10304)
    QF = sb("QF", [128, 2, T], F32, O_T + 14464)
    S0 = sb("S0", [128, DB, 128], F32, O_T + 18624)
    CVO = sb("CVO", [128, 4, 18], F32, O_T + 22720)
    R = sb("R", [TT, NT, D], F32, O_PR)
    NRT = 8
    RT = sb("RT", [128, NRT, T], F32, O_Y)
    LG = sb("LG", [TT, D], F32, O_Y + NRT * T * 4)
    LB = sb("LB", [TT, D], F32, O_Y + NRT * T * 4 + 8192)
    WR = sb("WR", [128, KC, 20], F32, 2048)
    GB1 = sb("GB1", [128, 2, KC], F32, 2048 + KC * 80)
    GW = sb("GW", [128, KC, 20], F32, 2048 + KC * 88)
    O_RT = O_PR + 40960
    rt = [O_RT]

    def small(name, shape, dt=F32):
        n = int(np.prod(shape[1:])) * 4
        off = rt[0]
        rt[0] += (n + 31) // 32 * 32
        return sb(name, shape, dt, off)

    NRAW, NHL = 6, 3
    RAWB = sb("RAWB", [128, NRAW, 2048], F32, O_RING)
    HIB = sb("HIB", [128, NHL, 2048], F32R, O_RING + 49152)
    LOB = sb("LOB", [128, NHL, 2048], F32R, O_RING + 73728)
    O_M = O_RING + 98304
    XG = sb("XG", [128, D], F32, O_M)
    XGH = sb("XGH", [128, KC, 128], F32R, O_M + 8192)
    XGL = sb("XGL", [128, KC, 128], F32R, O_M + 16384)
    YO = sb("YO", [128, D], F32, O_M + 24576)
    H = sb("H", [128, 512], F32, O_M + 32768)
    SG = sb("SG", [128, 512], F32, O_M + 34816)
    HTH = sb("HTH", [128, 4, 128], F32R, O_M + 36864)
    HTL = sb("HTL", [128, 4, 128], F32R, O_M + 38912)
    YA = sb("YA", [TT, 2, D], F32, O_RING)
    YB = sb("YB", [TT, 2, D], F32, O_RING + 16384)
    LG2 = sb("LG2", [TT, D], F32, O_RING + 32768)
    LB2 = sb("LB2", [TT, D], F32, O_RING + 40960)

    BANK = nc.alloc_psum_tensor("BANK", [128, 8, 512], F32)

    SINK = SM[:, 0:16]
    GAIN = SM[:, 16:17]
    LBP = SM[:, 20:24]
    LB0 = SM[:, 24:28]
    OML = SM[:, 28:32]
    LBT = SM[:, 32:36]
    EPS_LN = SM[:, 36:37]
    EPS_RMS = SM[:, 37:38]
    SINKC = SM[:, 38:40]
    CW = SM[:, 40:52]
    HIST = SM[:, 64:128].rearrange("p (j b r) -> p j b r", j=4, b=DB)
    MX = SM[:, 128:144].rearrange("p (k j) -> p k j", j=4)
    MXS = SM[:, 144:150]
    DEC = SM[:, 152:156]
    FS = [SM[:, 160:168], SM[:, 168:176]]
    ST = SM[:, 192:312].rearrange("p (i n s) -> p i n s", i=NT, n=4)
    MV = SM[:, 320:340].rearrange("p (i s) -> p i s", i=NT)

    with ExitStack() as ctx:
        def sem(name):
            return ctx.enter_context(nc.semaphore(name))

        s_const = sem("const_in")
        s_ones = sem("ones_set")
        s_x = [sem(f"x_in{g}") for g in range(4)]
        s_xh = sem("x_hi")
        s_xl = sem("x_lo")
        s_raw = [sem(f"weights_in{s}") for s in range(2)]
        s_hi = sem("weights_hi")
        s_lo = sem("weights_lo")
        s_acc = sem("proj_ready")
        s_pr = sem("proj_copied")
        s_grp = sem("group_done")
        s_act = sem("act_chain")
        s_dve = sem("dve_chain")
        s_vt_t = sem("v_turned")
        s_vt = sem("v_copied")
        s_sc = sem("scores_ready")
        s_mx = sem("max_ready")
        s_ex = sem("exp_ready")
        s_p = sem("probs_ready")
        s_tp = sem("probs_turned")
        s_pt = sem("probs_t_copied")
        s_pv = sem("pv_ready")
        s_yc = sem("pv_copied")
        s_kc = sem("cache_in")
        s_self = sem("self_rows_in")
        s_w_kv = sem("kv_states_out")
        s_m = [sem(f"sample_{n}") for n in ("kt", "kt_copied", "scores", "scores_copied", "turned", "max", "exp", "probs", "pt", "pt_copied", "out")]
        h_clamp = sem("hg_clamped")
        h_e = sem("hg_exp")
        h_f = sem("hg_f")
        h_g = sem("hg_logf")
        h_fac = sem("hg_factors_exp")
        h_mul = sem("hg_factors_ready")
        h_k = sem("hg_k_ready")
        h_gc = sem("hg_gate_clamped")
        h_ge = sem("hg_gate_exp")
        h_upd = sem("hg_sums_updated")
        h_lev = sem("hg_level_ready")
        h_acc = sem("hg_level_added")
        h_vt = sem("hg_v_turned")
        h_vtc = sem("hg_v_copied")
        h_fin = sem("hg_final_exp")
        h_ks = sem("hg_k_to_end")
        h_kt = sem("hg_k_turned")
        h_ktc = sem("hg_k_copied")
        h_u = sem("hg_u_ready")
        h_st = sem("hg_states_ready")
        h_s0 = sem("hg_state_in")
        h_vb = sem("hg_v_spread")
        h_sn = sem("hg_sample_states")
        h_o = sem("hg_out_ready")
        h_sq = sem("hg_squares")
        h_ss = sem("hg_square_sums")
        h_rt = sem("hg_root")
        h_out = sem("hg_states_out")
        c_out = sem("conv_states_out")
        c_rdy = sem("conv_state_ready")
        s_yh = sem("mix_hi")
        s_yl = sem("mix_lo")
        s_r = [sem(f"residual_in{k}") for k in range(NRT)]
        s_ob = sem("out_ready")
        s_rt = sem("out_added")
        s_turn = sem("residual_turned")
        s_rcp = sem("residual_copied")
        s_gw = sem("router_scaled")
        s_lg = sem("ln1_in")
        s_wr = sem("router_in")
        s_var = sem("ln_var")
        s_sd = sem("ln_sd")
        s_rs = sem("ln_rstd")
        s_nrm = sem("ln_normed")
        s_nd = sem("ln_normed_last")
        s_x1g = sem("x1_gained")
        s_x1 = sem("x1_ready_pool")
        s_x1d = sem("x1_ready_dve")
        s_x1w = sem("x1_out")
        s_log = sem("logits_ready")
        s_rc = sem("route_consts")
        r_e = sem("route_exp_in")
        r_x = sem("route_exp")
        r_hot = sem("route_hot")
        r_rank = sem("route_rank")
        r_tab = sem("route_onehots")
        r_tabm = sem("route_table")
        r_idx = sem("route_indices")
        b_raw = [sem(f"expert_in{s}") for s in range(NRAW)]
        b_hi = sem("expert_hi")
        b_lo = [sem(f"expert_lo{s}") for s in range(NHL)]
        b_used = sem("expert_used")
        b_xg = sem("tokens_in")
        b_tx = sem("tokens_turned")
        b_ix = sem("gather_indices")
        b_iy = sem("scatter_indices")
        b_xh = sem("tokens_hi")
        b_xl = sem("tokens_lo")
        b_sg = sem("silu_ready")
        b_h = sem("h_ready")
        b_th = sem("h_turned")
        b_hh = sem("h_hi")
        b_hl = sem("h_lo")
        b_y = sem("down_copied")
        b_yw = sem("block_out")
        s_passed = sem("waits_passed")
        f_in = [sem(f"y_in{s}") for s in range(2)]
        f_ln = sem("ln2_in")
        f_ab = sem("y_rows_added")
        f_st = sem("ln2_mean")
        f_sd = sem("ln2_sd")
        f_rs = sem("ln2_rstd")
        f_nm = sem("ln2_normed")
        f_y = sem("y_ready")
        f_out = sem("y_out")

        TRI = small("TRI", [TT, TT])
        IO128 = small("IO128", [TT, 128])
        IO24 = small("IO24", [TT, MAXB + 1])
        IO4 = small("IO4", [TT, 4])
        IO16 = small("IO16", [TT, 16])
        TID = small("TID", [TT, NT])
        SKP = small("SKP", [128, 1])
        RB = small("RB", [TT, 20])
        LO_G = small("LO_G", [TT, NT, 20])
        G4 = [small(f"G4_{k}", [TT, NT, 4]) for k in range(2)]
        E16 = [small(f"E16_{k}", [TT, NT, 16]) for k in range(6)]
        C5 = [small(f"C5_{k}", [TT, NT]) for k in range(14)]
        NB16 = [small(f"NB16_{k}", [TT, 16]) for k in range(4)]
        OH = small("OH", [TT, 2, NT, 128])
        TB = small("TB", [TT, 2, NT, 3, MAXB + 1])
        TABF = small("TABF", [128, 3, MAXB + 1])
        TIX = small("TIX", [128, MAXB + 1], I32)
        YIX = small("YIX", [128, MAXB + 1], I32)
        TIXC = small("TIXC", [128, 1], I32)
        YIXC = small("YIXC", [128, 1], I32)
        EBC = small("EBC", [TT, MAXB + 1, 16])
        EBF = small("EBF", [TT, 32])
        TABZ = small("TABZ", [128, MAXB + 1])
        EBI = small("EBI", [1, 32], I32)

        def used(eng, u):
            if u < NU:
                eng.wait_ge(s_acc, 2 * u + 2)
            else:
                eng.wait_ge(s_ob, 2 * (u - NU) + 2)

        block = ctx.enter_context(nc.Block())

        def acc(m):
            return BANK[:, m % 3, 0:HALF]

        MB = [BANK[:, 3 + k, :] for k in range(5)]

        def slot(u):
            return PR[:, u % 16, :]

        def passed(eng):
            eng.sem_inc(s_passed, 1)

        @block.sync
        def _(sp):
            def unit(u, w):
                if u >= 2:
                    sp.wait_ge(s_lo, u - 1)
                sp.dma_start(RAW[:, u % 2, :], w).then_inc(s_raw[u % 2], 16)

            xr = a["xT"].rearrange("p (g n) -> p g n", g=4)
            sp.dma_start(Y[:, 0:4, :], xr[:, 0, :]).then_inc(s_x[0], 16)
            unit(0, a["w_in"][0])
            for g in range(1, 4):
                sp.dma_start(Y[:, 4 * g:4 * g + 4, :], xr[:, g, :]).then_inc(s_x[g], 16)
            unit(1, a["w_in"][1])
            for t, s in ((IDENT, "ident"), (NDIST, "ndist"), (MASK, "mask"), (NDS, "nds")):
                sp.dma_start(t[:], a[s]).then_inc(s_const, 16)
            for t, s in ((SINK, "sink"), (SINKC[0:64, :], "sinkc"), (GAIN, "gain"), (LBP, "lbp"), (CW, "cw"), (SM[:, 64:128], "hist")):
                sp.dma_start(t, a[s]).then_inc(s_const, 16)
            kc = a["cache_k"].rearrange("b s n -> s b n")
            vc = a["cache_v"].rearrange("b s n -> s b n")

            def caches(t):
                if t:
                    sp.wait_ge(s_grp, t)
                    sp.wait_ge(s_w_kv, 64 * t)
                for dst, src in ((KCA, kc), (VCA, vc)):
                    sp.dma_start(dst[0:127, :, :], src[1:128, :, 128 * t:128 * t + 128]).then_inc(s_kc, 16)

            def att_setup(t):
                sp.wait_ge(s_vt, 2 * t + 2)
                sp.dma_start(KCA[127:128, :, :], SELF[:, 0, :]).then_inc(s_self, 16)
                sp.dma_start(VCA[127:128, :, :], SELF[:, 1, :]).then_inc(s_self, 16)
                k_slot = slot(ATT0[t])
                sp.dma_start(o["kp"][t], k_slot[:, SEQ - WIN:SEQ]).then_inc(s_w_kv, 16)
                sp.dma_start(o["vp"][t], VT[:, 3, :]).then_inc(s_w_kv, 16)

            def smp0(t):
                sp.wait_ge(s_kc, 32 * (t + 1))
                sp.wait_ge(s_self, 32 * (t + 1))
                sp.dma_start(o["ks"][t], KCA[:, :, :]).then_inc(s_w_kv, 16)
                sp.dma_start(o["vs"][t], VCA[:, :, :]).then_inc(s_w_kv, 16)

            def hg_states(h):
                if h:
                    sp.wait_ge(h_out, 32 * h)
                    sp.wait_ge(h_o, h)
                sp.dma_start(S0[:, :, :], a["s0"][h]).then_inc(h_s0, 16)

            def hg3(h):
                sp.wait_ge(h_st, h + 1)
                sp.dma_start(o["hp"][h], SF[:, 384:512]).then_inc(h_out, 16)
                sp.wait_ge(h_sn, 2 * h + 2)
                sp.dma_start(o["hs"][h], S0[:, :, :]).then_inc(h_out, 16)

            caches(0)
            for q in range(NQ):
                if q % 4 == 0 and q // 4 + 2 < NU:
                    unit(q // 4 + 2, a["w_in"][q // 4 + 2])
                for what, n in MIX[q]:
                    if what == "att_setup":
                        if n == 1:
                            caches(1)
                        att_setup(n)
                    elif what == "smp0":
                        smp0(n)
                    elif what == "hg_k":
                        if n == 0:
                            sp.wait_ge(s_grp, 2)
                            sp.wait_ge(s_w_kv, 128)
                        hg_states(n)
                    elif what == "hg3":
                        hg3(n)
            for k in range(2):
                unit(NU + k, a["w_out"][k])
            sp.wait_ge(s_grp, 10)
            sp.wait_ge(h_out, 128)
            sp.dma_start(o["cs"], CVO[:, :, :]).then_inc(c_out, 16)
            sp.wait_ge(c_out, 16)

            def residual(m):
                if m < NRT:
                    sp.wait_ge(s_yl, m + 1)
                else:
                    sp.wait_ge(s_log, (m - NRT) // 4 + 1)
                sp.dma_start(RT[:, m % NRT, :], a["xT"][:, T * m:T * m + T]).then_inc(s_r[m % NRT], 16)

            for m in range(4):
                residual(m)

            def bload(i, m0, w, j):
                s = (2 + i) % NRAW if m0 is not None else i % NRAW
                if m0 is None:
                    if i >= NRAW:
                        sp.wait_ge(b_lo[(i - NRAW) % NHL], (i - NRAW) // NHL + 1)
                else:
                    sp.wait_ge(b_lo[(2 + i) % NHL], (2 + i) // NHL + 1 + 4 * (j - 1))
                    passed(sp)
                sp.dma_start(RAWB[:, s, :], w).then_inc(b_raw[s], 16)

            for n in range(KC):
                if n + 2 < KC:
                    unit(NU + n + 2, a["w_out"][n + 2])
                if n + 4 < KC:
                    residual(n + 4)
                if n == 0:
                    sp.wait_ge(s_yl, KC)
                    sp.dma_start(WR[:, :, :], a["wr"]).then_inc(s_wr, 16)
                    sp.dma_start(GB1[:, :, :], a["gb1"]).then_inc(s_wr, 16)
                    sp.dma_start(LG[:, :], a["ln1g"]).then_inc(s_lg, 16)
                    sp.dma_start(LB[:, :], a["ln1b"]).then_inc(s_lg, 16)
                    for t, s in ((TRI, "tri"), (IO128, "io128"), (IO24, "io24"), (IO4, "io4"), (IO16, "io16"), (TID, "tid"), (SKP, "skp"), (RB, "rb")):
                        sp.dma_start(t[:], a[s]).then_inc(s_rc, 16)
            sp.wait_ge(s_lo, NU + 16)
            for i in range(NRAW):
                if i == 2:
                    sp.wait_ge(s_ob, 2 * KC)
                bload(i, None, (a["w_gate"], a["w_up"])[i % 2][0, :, 2048 * (i // 2):2048 * (i // 2) + 2048], 0)
            for i in (NT - 1, *range(NT - 1)):
                if i == NT - 1:
                    sp.wait_ge(s_x1d, 1)
                else:
                    sp.wait_ge(s_x1, i + 1)
                sp.dma_start(x1_rows[i * TT:(i + 1) * TT, :], R[:, i, :]).then_inc(s_x1w, 16)

            for i in range(NRAW, 8):
                bload(i, None, (a["w_gate"], a["w_up"])[i % 2][0, :, 2048 * (i // 2):2048 * (i // 2) + 2048], 0)

            sp.wait_ge(r_idx, 1)
            nb = sp.value_load(EBI[0:1, 31:32], min_val=8, max_val=MAXB - 1) + 1

            def gate_up(j, m0):
                e = sp.value_load(EBI[0:1, bass.ds(j, 1)], min_val=0, max_val=NE - 1)
                for i in range(8):
                    bload(i, m0, (a["w_gate"], a["w_up"])[i % 2][bass.ds(e, 1), :, 2048 * (i // 2):2048 * (i // 2) + 2048].rearrange("a p n -> p (a n)"), j)

            def down(j, first):
                e = sp.value_load(EBI[0:1, bass.ds(j - 1, 1)], min_val=0, max_val=NE - 1)
                for n in range(4):
                    w = a["w_down"][bass.ds(e, 1), :, :, 512 * n:512 * n + 512].rearrange("a p c n -> p (a c) n")
                    i = first + n
                    s = (2 + i) % NRAW
                    sp.wait_ge(b_lo[(2 + i) % NHL], (2 + i) // NHL + 1 + 4 * (j - 1))
                    passed(sp)
                    sp.dma_start(RAWB[:, s, :].rearrange("p (c n) -> p c n", c=4), w).then_inc(b_raw[s], 16)

            with sp.Fori(1, MAXB) as j:
                with sp.If(j < nb):
                    gate_up(j, 0)
                    down(j, 8)
            down(nb, 0)

            sp.wait_ge(b_yw, 16 * nb + 16)
            passed(sp)
            sp.wait_ge(b_used, 12 * nb)
            passed(sp)
            for i in range(NT):
                if i >= 2:
                    sp.wait_ge(f_sd, i - 1)
                for c, dst in ((0, YA), (1, YB)):
                    sp.dma_start(dst[:, i % 2, :], y_rows[c * T + i * TT:c * T + (i + 1) * TT, :]).then_inc(f_in[i % 2], 16)
                if i == 1:
                    sp.dma_start(LG2[:, :], a["ln2g"]).then_inc(f_ln, 16)
                    sp.dma_start(LB2[:, :], a["ln2b"]).then_inc(f_ln, 16)
            for i in range(NT):
                sp.wait_ge(f_y, i + 1)
                n = TT if i < NT - 1 else TT - DB
                sp.dma_start(o["yp"][i * TT:i * TT + n, :], R[0:n, i, :]).then_inc(f_out, 16)
            sp.dma_start(o["ys"], R[TT - DB:TT, NT - 1, :]).then_inc(f_out, 16)
            sp.wait_ge(f_out, 16 * (NT + 1))
            sp.wait_ge(s_w_kv, 128)
            sp.wait_ge(h_out, 128)
            sp.wait_ge(c_out, 16)

        @block.gpsimd
        def _(pool):
            def lo(u):
                pool.wait_ge(s_hi, u + 1)
                pool.tensor_tensor(LO[:, u % 2, :], RAW[:, u % 2, :], HI[:, u % 2, :].bitcast(F32), ALU.subtract).then_inc(s_lo, 1)

            pool.memset(ONES[:, :], 1.0).then_inc(s_ones, 1)
            for u in range(NU + 16):
                lo(u)

            pool.wait_ge(s_lg, 32)
            for i in range(NT - 1):
                pool.wait_ge(s_nrm, i + 1)
                pool.tensor_tensor(R[:, i, :], R[:, i, :], LG[:, :], ALU.mult).then_inc(s_x1g, 1)
                pool.wait_ge(s_x1g, i + 1)
                pool.tensor_tensor(R[:, i, :], R[:, i, :], LB[:, :], ALU.add).then_inc(s_x1, 1)
            pool.wait_ge(s_ob, 2 * KC)
            pool.memset(XG[:, :], 0.0).then_inc(s_ones, 1)
            pool.wait_ge(s_ones, 2)
            pool.wait_ge(r_idx, 1)
            pool.wait_ge(s_x1w, 16 * NT)
            nb = pool.value_load(EBI[0:1, 31:32], min_val=8, max_val=MAXB - 1) + 1
            last_token, last_row = pool.to_reg(T - 1), pool.to_reg(2 * T - 1)

            def gather(j, landed):
                pool.tensor_copy(TIXC[:, :], TIX[:, bass.ds(j, 1)]).then_inc(b_ix, 1)
                pool.wait_ge(b_ix, j + 1)
                passed(pool)
                pool.indirect_dma_start(
                    out=XG[:, :], out_offset=None, in_=x1_rows,
                    in_offset=bass.IndirectOffsetOnAxis(ap=TIXC[:, 0:1], axis=0),
                    bounds_check=last_token, oob_is_err=False).then_inc(landed, 16)

            def scatter(j):
                pool.wait_ge(b_y, 4 * j + 2)
                passed(pool)
                pool.tensor_copy(YIXC[:, :], YIX[:, bass.ds(j - 1, 1)]).then_inc(b_iy, 1)
                pool.wait_ge(b_iy, j)
                passed(pool)
                pool.indirect_dma_start(
                    out=y_rows, out_offset=bass.IndirectOffsetOnAxis(ap=YIXC[:, 0:1], axis=0),
                    in_=YO[:, :], in_offset=None,
                    bounds_check=last_row, oob_is_err=False).then_inc(b_yw, 16)

            gather(0, b_yw)
            pool.wait_ge(b_tx, 4)
            gather(1, b_xg)
            with pool.Fori(1, MAXB) as j:
                with pool.If(j < nb):
                    pool.wait_ge(b_tx, 4 * j + 4)
                    passed(pool)
                    gather(j + 1, b_xg)
                    scatter(j)
            scatter(nb)
            pool.wait_ge(b_xg, 16 * nb)
            passed(pool)
            for i in range(NT):
                pool.wait_ge(f_in[i % 2], 32 * (i // 2 + 1))
                pool.tensor_tensor(YA[:, i % 2, :], YA[:, i % 2, :], YB[:, i % 2, :], ALU.add).then_inc(f_ab, 1)

        @block.scalar
        def _(act):
            chain = [0]

            def done(ins):
                chain[0] += 1
                ins.then_inc(s_act, 1)
                act.wait_ge(s_act, chain[0])

            def hi(u):
                act.wait_ge(s_raw[u % 2], 16 * (u // 2 + 1))
                if u >= 2:
                    used(act, u - 2)
                act.activation(HI[:, u % 2, :], RAW[:, u % 2, :], ACT.Copy).then_inc(s_hi, 1)

            def copy_proj(m):
                u, hf = m // 2, m % 2
                act.wait_ge(s_acc, m + 1)
                if u >= 16 and hf == 0:
                    g = [0] * 6 + [1] * 6 + [2 + k // 4 for k in range(16)]
                    act.wait_ge(s_grp, g[u - 16] + 1)
                    if u - 16 in (0, 6):
                        act.wait_ge(s_w_kv, 64 * (1 + (u - 16) // 6))
                scale = 1.0
                if u in range(2, 6) or u in range(8, 12):
                    scale = HD ** -0.5
                if u in HG0:
                    scale = DK ** -0.5
                act.activation(PR[:, u % 16, hf * HALF:(hf + 1) * HALF], acc(m), ACT.Copy, scale=scale).then_inc(s_pr, 1)

            def att_setup(t):
                act.wait_ge(s_vt_t, 2 * t + 1)
                if t:
                    act.wait_ge(s_w_kv, 64 * t)
                act.activation(VT[:, :, :], MB[2].rearrange("p (c n) -> p c n", c=4), ACT.Copy).then_inc(s_vt, 1)
                act.wait_ge(s_vt_t, 2 * t + 2)
                act.activation(SELF[:, :, :], MB[3][0:DB, 0:256].rearrange("p (c n) -> p c n", c=2), ACT.Copy).then_inc(s_vt, 1)

            def att_scores(s):
                l, qb = STEPS[s % 8]
                k0 = 128 if qb == 0 else 0
                act.wait_ge(s_mx, s + 1)
                for j in range(4):
                    ins = act.activation(SC[:, j, k0:256], SC[:, j, k0:256], ACT.Exp, bias=MX[:, 1, j:j + 1],
                                         accum_out=MX[:, 3, j:j + 1])
                done(ins)
                act.activation(MX[:, 2, :], MX[:, 2, :], ACT.Exp).then_inc(s_ex, 1)

            def att_turn(s):
                l, qb = STEPS[s % 8]
                h0 = 1 if qb == 0 else 0
                act.wait_ge(s_tp, s + 1)
                if s >= 1:
                    act.wait_ge(s_pv, s)
                for k in range(h0, 2):
                    ins = act.activation(PT[:, k, :, :], MB[2 + k].rearrange("p (c n) -> p c n", c=4), ACT.Copy)
                ins.then_inc(s_pt, 1)

            def smp(s, t):
                if s == 0:
                    act.wait_ge(s_m[0], t + 1)
                    for k in range(2):
                        ins = act.activation(KTS[:, 4 * k:4 * k + 4, :], MB[2 + k].rearrange("p (c n) -> p c n", c=4), ACT.Copy)
                    ins.then_inc(s_m[1], 1)
                elif s == 1:
                    act.wait_ge(s_m[2], t + 1)
                    act.activation(SST[:, 0:32], MB[0][:, 0:32], ACT.Copy)
                    act.activation(SST[:, 32:64], MB[1][:, 0:32], ACT.Copy).then_inc(s_m[3], 1)
                elif s == 2:
                    act.wait_ge(s_m[5], t + 1)
                    done(act.activation(SSR[:, :], SSR[:, :], ACT.Exp, bias=MXS[0:64, 1:2], accum_out=MXS[0:64, 3:4]))
                    act.activation(MXS[0:64, 2:3], MXS[0:64, 2:3], ACT.Exp).then_inc(s_m[6], 1)
                elif s == 3:
                    act.wait_ge(s_m[8], t + 1)
                    act.activation(PST[:, :], MB[3][:, 0:64], ACT.Copy).then_inc(s_m[9], 1)

            def hg_prep(h):
                q0 = HG0[h]
                act.wait_ge(h_clamp, h + 1)
                f, g = slot(q0 + 1), slot(q0 + 3)
                act.activation(f, f, ACT.Exp, scale=-1.0).then_inc(h_e, 1)
                act.wait_ge(h_f, h + 1)
                if h:
                    act.wait_ge(h_u, h)
                act.activation(PF[:, :], f[:, 0:SEQ], ACT.Ln).then_inc(h_g, 1)

            def runs(tile, n):
                return tile.rearrange("p (b s n) -> p b s n", s=2, n=n)

            def hg_factor(x):
                h, l = x // 8, x % 8
                if l == 0:
                    return
                n = 1 << (l - 1)
                k = l % 2
                act.wait_ge(h_k, h + 1)
                if l >= 2:
                    act.wait_ge(h_upd, 7 * h + l - 1)
                if l >= 3:
                    act.wait_ge(h_lev, 8 * h + l - 1)
                e = runs(EF[:, k, 0:SEQ], n)
                act.activation(e[:, :, 1, :], runs(PF[:, :], n)[:, :, 1, :], ACT.Exp)
                act.activation(e[:, :, 0, :], runs(SF[:, :], n)[:, :, 0, :], ACT.Exp).then_inc(h_fac, 1)

            def hg_final(h):
                act.wait_ge(h_vt, h + 1)
                act.activation(VTK[:, :, :], MB[2].rearrange("p (c n) -> p c n", c=4), ACT.Copy).then_inc(h_vtc, 1)
                act.wait_ge(h_acc, 8 * h + 8)
                act.activation(EF[:, 0, 0:SEQ], PF[:, :], ACT.Exp)
                act.activation(EF[:, 1, 0:SEQ], SF[:, :], ACT.Exp).then_inc(h_fin, 1)

            def hg(s, h):
                if s == 1:
                    act.wait_ge(h_kt, h + 1)
                    act.activation(PF[:, :], MB[2], ACT.Copy).then_inc(h_ktc, 1)
                elif s == 3:
                    act.wait_ge(h_gc, h + 1)
                    act.activation(EF[:, 1, :], EF[:, 1, :], ACT.Exp, scale=-1.0).then_inc(h_ge, 1)
                elif s == 5:
                    act.wait_ge(h_ss, h + 1)
                    act.activation(QF[:, 1, 0:SEQ], MB[1], ACT.Sqrt, bias=EPS_RMS, scale=1.0 / DK)
                    act.activation(QF[:, 1, SEQ:T], MB[2][:, 0:DB], ACT.Sqrt, bias=EPS_RMS, scale=1.0 / DK).then_inc(h_rt, 1)

            for g in range(4):
                act.wait_ge(s_x[g], 16)
                act.activation(XH[:, 4 * g:4 * g + 4, :], Y[:, 4 * g:4 * g + 4, :], ACT.Copy).then_inc(s_xh, 1)
                if g == 0:
                    hi(0)
            for q in range(NQ):
                if q % 2 == 0 and q >= 2:
                    copy_proj(q // 2 - 1)
                if q % 4 == 0 and q // 4 + 1 < NU:
                    hi(q // 4 + 1)
                for what, n in MIX[q]:
                    if what == "att_setup":
                        att_setup(n)
                    elif what == "att_scores":
                        att_scores(n)
                    elif what == "att_turn":
                        att_turn(n)
                    elif what.startswith("smp"):
                        smp(int(what[3:]), n)
                    elif what == "hg_prep":
                        hg_prep(n)
                    elif what == "hg_factor":
                        hg_factor(n)
                    elif what == "hg_final":
                        hg_final(n)
                    elif what in ("hg1", "hg3", "hg5"):
                        hg(int(what[2:]), n)
            copy_proj(2 * NU - 1)

            act.wait_ge(s_acc, 2 * NU)
            hi(NU)
            for c in range(KC):
                if c in (8, 12):
                    act.wait_ge(s_grp, 8 if c == 8 else 10)
                act.activation(XH[:, c, :], Y[:, c, :], ACT.Copy).then_inc(s_yh, 1)
            act.wait_ge(h_out, 128)

            def residual_copies(k):
                act.wait_ge(s_turn, 4 * k + 4)
                for i in range(NT):
                    act.activation(R[:, i, 512 * k:512 * k + 512], BANK[0:TT, 2 + i, :], ACT.Copy).then_inc(s_rcp, 1)

            for n in range(KC):
                if n + 1 < KC:
                    hi(NU + n + 1)
                if n % 4 == 0 and n:
                    residual_copies(n // 4 - 1)
            residual_copies(3)
            act.wait_ge(s_var, 1)
            act.activation(MV[0:TT, :, 2:3], MV[0:TT, :, 1:2], ACT.Sqrt, bias=EPS_LN[0:TT, :]).then_inc(s_sd, 1)
            act.wait_ge(s_rcp, 4 * NT)
            act.wait_ge(s_rs, 1)
            for i in (0, NT - 1, *range(1, NT - 1)):
                act.activation(R[:, i, :], R[:, i, :], ACT.Identity, scale=MV[0:TT, i, 2:3], bias=MV[0:TT, i, 3:4]).then_inc(s_nd if i == NT - 1 else s_nrm, 1)

            def bhi(i, m0, j):
                s, r = (i % NHL, i % NRAW) if m0 is None else ((2 + i) % NHL, (2 + i) % NRAW)
                if m0 is None:
                    act.wait_ge(b_raw[r], 16 * (i // NRAW + 1))
                    if i >= NHL:
                        act.wait_ge(b_used, i - NHL + 1)
                else:
                    act.wait_ge(b_raw[r], 16 * ((8 + i) // NRAW + 1) + 32 * (j - 1))
                    act.wait_ge(b_used, 12 * j + i - 6)
                act.activation(HIB[:, s, :], RAWB[:, r, :], ACT.Copy).then_inc(b_hi, 1)

            for i in range(AHEAD):
                bhi(i, None, 0)

            act.wait_ge(r_e, 1)
            act.activation(G4[1][:, :, :], G4[1][:, :, :], ACT.Exp).then_inc(r_x, 1)
            act.wait_ge(r_e, 2)
            act.activation(C5[2][:, :], C5[2][:, :], ACT.Exp).then_inc(r_x, 1)

            act.wait_ge(r_idx, 1)
            nb = act.value_load(EBI[0:1, 31:32], min_val=8, max_val=MAXB - 1) + 1

            def silu(j):
                act.wait_ge(b_used, 12 * j + 4 if not isinstance(j, int) else 8)
                act.activation(SG[:, :], BANK[:, 0, :], ACT.Silu).then_inc(b_sg, 1)

            def token_hi(g, j):
                act.wait_ge(b_tx, 4 * j + g + 1)
                act.activation(XGH[:, 4 * g:4 * g + 4, :], BANK[:, 2 + g % 2, :].rearrange("p (c n) -> p c n", c=4), ACT.Copy).then_inc(b_xh, 1)

            def h_hi(j):
                act.wait_ge(b_th, j + 1)
                act.activation(HTH[:, :, :], BANK[:, 6, :].rearrange("p (c n) -> p c n", c=4), ACT.Copy).then_inc(b_hh, 1)

            def out_copy(n, i, j):
                act.wait_ge(b_used, 12 * j - 3 + i)
                act.activation(YO[:, 512 * n:512 * n + 512], BANK[:, 4 + n % 2, :], ACT.Copy).then_inc(b_y, 1)

            act.sem_inc(b_y, 2)
            for g in range(4):
                token_hi(g, 0)
            for i in range(AHEAD, 8):
                bhi(i, None, 0)
            silu(0)
            for g in range(4):
                token_hi(g, 1)
            for i in range(2):
                bhi(i, 0, 1)
            with act.Fori(1, MAXB) as j:
                with act.If(j < nb):
                    h_hi(j - 1)
                    for i in range(2, 10):
                        bhi(i, 0, j)
                    silu(j)
                    token_hi(0, j + 1)
                    bhi(10, 0, j)
                    act.wait_ge(b_yw, 16 * j)
                    out_copy(0, 8, j)
                    token_hi(1, j + 1)
                    bhi(11, 0, j)
                    out_copy(1, 9, j)
                    token_hi(2, j + 1)
                    bhi(0, 0, j + 1)
                    out_copy(2, 10, j)
                    token_hi(3, j + 1)
                    bhi(1, 0, j + 1)
                    out_copy(3, 11, j)
            h_hi(nb - 1)
            bhi(2, 0, nb)
            act.wait_ge(b_yw, 16 * nb)
            out_copy(0, 0, nb)
            bhi(3, 0, nb)
            for n in range(1, 4):
                out_copy(n, n, nb)

            for i in range(NT):
                act.wait_ge(f_st, i + 1)
                done(act.activation(YA[:, i % 2, :], R[:, i, :], ACT.Square, bias=MV[0:TT, i, 0:1], accum_out=MV[0:TT, i, 1:2]))
                act.activation(MV[0:TT, i, 2:3], MV[0:TT, i, 1:2], ACT.Sqrt, bias=EPS_LN[0:TT, :], scale=1.0 / D).then_inc(f_sd, 1)
                act.wait_ge(f_rs, i + 1)
                act.activation(R[:, i, :], R[:, i, :], ACT.Identity, scale=MV[0:TT, i, 2:3], bias=MV[0:TT, i, 3:4]).then_inc(f_nm, 1)

        @block.vector
        def _(dve):
            chain = [0]

            def done(ins):
                chain[0] += 1
                ins.then_inc(s_dve, 1)
                dve.wait_ge(s_dve, chain[0])

            dve.memset(EPS_LN, LN_EPS)
            dve.memset(EPS_RMS, RMS_EPS)
            for g in range(4):
                dve.wait_ge(s_xh, g + 1)
                dve.tensor_tensor(XL[:, 4 * g:4 * g + 4, :], Y[:, 4 * g:4 * g + 4, :], XH[:, 4 * g:4 * g + 4, :].bitcast(F32), ALU.subtract).then_inc(s_xl, 1)
            dve.wait_ge(s_const, 160)
            done(dve.tensor_tensor(LBT, LBP, LBP, ALU.subtract))
            done(dve.tensor_scalar(LBT, LBT, 1.0, None, ALU.add))
            done(dve.reciprocal(OML, LBT))
            done(dve.tensor_tensor(LBT, LBT, OML, ALU.mult))
            done(dve.tensor_tensor(LB0, LBT, LBT, ALU.subtract))
            done(dve.tensor_scalar(OML, LB0, -1.0, 1.0, ALU.mult, ALU.add))

            def att_scores(s):
                t, (l, qb) = s // 8, STEPS[s % 8]
                k0 = 128 if qb == 0 else 0
                dve.wait_ge(s_sc, s + 1)
                if s >= 1:
                    dve.wait_ge(s_tp, s)
                for j in range(4):
                    h = 8 * t + 4 * l + j
                    src = MB[j // 2].rearrange("p (c n) -> p c n", c=2)[:, j % 2, k0:256]
                    ins = dve.scalar_tensor_tensor(SC[:, j, k0:256], NDIST[:, k0:256], SLOPE[h], src, ALU.mult, ALU.add)
                done(ins)
                done(dve.tensor_reduce(MX[:, 0, :], SC[:, :, k0:256], AX.X, ALU.max))
                sk = SINK[:, 8 * t + 4 * l:8 * t + 4 * l + 4]
                done(dve.tensor_tensor(MX[:, 0, :], MX[:, 0, :], sk, ALU.max))
                dve.tensor_scalar(MX[:, 1, :], MX[:, 0, :], -1.0, None, ALU.mult)
                dve.tensor_tensor(MX[:, 2, :], sk, MX[:, 0, :], ALU.subtract).then_inc(s_mx, 1)
                dve.wait_ge(s_ex, s + 1)
                done(dve.tensor_tensor(MX[:, 3, :], MX[:, 3, :], MX[:, 2, :], ALU.add))
                done(dve.reciprocal(MX[:, 3, :], MX[:, 3, :]))
                for j in range(4):
                    ins = dve.tensor_scalar(SC[:, j, k0:256], SC[:, j, k0:256], MX[:, 3, j:j + 1], None, ALU.mult)
                ins.then_inc(s_p, 1)

            def att_pv(s):
                t, (l, qb) = s // 8, STEPS[s % 8]
                dve.wait_ge(s_pv, s + 1)
                b = 64 * l
                dve.tensor_copy(Y[b:b + 64, 4 * t:4 * t + 4, 128 * qb:128 * qb + 128],
                                MB[4][b:b + 64, :].rearrange("p (c n) -> p c n", c=4)).then_inc(s_yc, 1)

            def smp(s, t):
                if s == 2:
                    dve.wait_ge(s_m[4], t + 1)
                    done(dve.tensor_tensor(SSR[:, :], MB[1][0:64, 0:128], NDS[:, t, :], ALU.add))
                    done(dve.tensor_reduce(MXS[0:64, 0:1], SSR[:, :], AX.X, ALU.max))
                    sk = SINKC[0:64, t:t + 1]
                    done(dve.tensor_tensor(MXS[0:64, 0:1], MXS[0:64, 0:1], sk, ALU.max))
                    dve.tensor_scalar(MXS[0:64, 1:2], MXS[0:64, 0:1], -1.0, None, ALU.mult)
                    dve.tensor_tensor(MXS[0:64, 2:3], sk, MXS[0:64, 0:1], ALU.subtract).then_inc(s_m[5], 1)
                    dve.wait_ge(s_m[6], t + 1)
                    done(dve.tensor_tensor(MXS[0:64, 3:4], MXS[0:64, 3:4], MXS[0:64, 2:3], ALU.add))
                    done(dve.reciprocal(MXS[0:64, 3:4], MXS[0:64, 3:4]))
                    dve.tensor_scalar(SSR[:, :], SSR[:, :], MXS[0:64, 3:4], None, ALU.mult).then_inc(s_m[7], 1)
                elif s == 4:
                    dve.wait_ge(s_m[10], t + 1)
                    dve.tensor_copy(Y[:, 4 * t:4 * t + 4, SEQ:T],
                                    MB[4][:, 0:32].rearrange("p (b g) -> p g b", b=DB)).then_inc(s_grp, 1)

            def hg_prep(h):
                q0 = HG0[h]
                f = slot(q0 + 1)
                dve.wait_ge(s_pr, 2 * q0 + 8)
                if h == 0:
                    dve.wait_ge(s_w_kv, 128)
                dve.tensor_scalar(f, f, -44.0, None, ALU.max).then_inc(h_clamp, 1)
                dve.wait_ge(h_e, h + 1)
                done(dve.tensor_scalar(f, f, 1.0, None, ALU.add))
                done(dve.reciprocal(f, f))
                done(dve.tensor_scalar(f, f, OML[:, h:h + 1], LB0[:, h:h + 1], ALU.mult, ALU.add))
                dve.tensor_copy(FS[h % 2], f[:, SEQ:T]).then_inc(h_f, 1)

            def hg_k(h):
                f = slot(HG0[h] + 1)
                if h:
                    dve.wait_ge(h_out, 32 * h)
                done(dve.memset(SF[:, :], 0.0))
                dve.wait_ge(h_g, h + 1)
                dve.tensor_scalar(f, f, -1.0, 1.0, ALU.mult, ALU.add).then_inc(h_k, 1)

            def runs(tile, n):
                return tile.rearrange("p (b s n) -> p b s n", s=2, n=n)

            def hg_factor(x):
                h, l = x // 8, x % 8
                q, k = slot(HG0[h]), slot(HG0[h] + 1)
                if l == 0:
                    return
                z = l % 2
                dve.wait_ge(h_fac, 7 * h + l)
                if l >= 3:
                    dve.wait_ge(h_lev, 8 * h + l - 1)
                n = 1 << (l - 1)
                w, e = runs(QF[:, z, 0:SEQ], n), runs(EF[:, z, 0:SEQ], n)
                dve.tensor_tensor(w[:, :, 1, :], runs(q[:, 0:SEQ], n)[:, :, 1, :], e[:, :, 1, :], ALU.mult)
                dve.tensor_tensor(w[:, :, 0, :], runs(k[:, 0:SEQ], n)[:, :, 0, :], e[:, :, 0, :], ALU.mult).then_inc(h_mul, 1)
                p, s = runs(PF[:, :], n), runs(SF[:, :], n)
                nb = SEQ // (2 * n)
                done(dve.tensor_tensor(s[:, :, 0, :], s[:, :, 0, :], p[:, :, 1, n - 1:n].to_broadcast([128, nb, n]), ALU.add))
                ins = dve.tensor_tensor(p[:, :, 1, :], p[:, :, 1, :], p[:, :, 0, n - 1:n].to_broadcast([128, nb, n]), ALU.add)
                ins.then_inc(h_upd, 1)

            def hg_level(x):
                h, l = x // 8, x % 8
                dve.wait_ge(h_lev, 8 * h + l + 1)
                if l == 0:
                    m = MASK[:, l:l + 1, :].to_broadcast([128, 4, 128])
                    dve.tensor_tensor(AT[:, :, :], MB[0].rearrange("p (c n) -> p c n", c=4), m, ALU.mult).then_inc(h_acc, 1)
                else:
                    n = 1 << (l - 1)
                    m = runs(MASK[:, l, :], n)[:, :, 1, :].unsqueeze(1).to_broadcast([128, 4, 64 // n, n])
                    t4 = TMP[:, 0:256].rearrange("p (c b n) -> p c b n", c=4, n=n)
                    done(dve.tensor_tensor(t4, MB[l % 2][:, 0:256].rearrange("p (c b n) -> p c b n", c=4, n=n), m, ALU.mult))
                    at = runs(AT[:, :, :].rearrange("p c n -> p (c n)"), n)[:, :, 1, :]
                    dve.tensor_tensor(at, at, TMP[:, 0:256].rearrange("p (b n) -> p b n", n=n), ALU.add).then_inc(h_acc, 1)

            def hg(s, h):
                q0 = HG0[h]
                q, k, v, g = (slot(q0 + c) for c in range(4))
                if s == 0:
                    dve.wait_ge(h_fin, h + 1)
                    dve.tensor_copy(DEC, EF[:, 0, 127:SEQ:128])
                    dve.tensor_tensor(QF[:, 0, 0:SEQ], q[:, 0:SEQ], EF[:, 0, 0:SEQ], ALU.mult)
                    dve.tensor_tensor(EF[:, 1, 0:SEQ], k[:, 0:SEQ], EF[:, 1, 0:SEQ], ALU.mult).then_inc(h_ks, 1)
                elif s in (1, 2):
                    c = s - 1
                    if c == 0:
                        dve.wait_ge(h_s0, 16 * (h + 1))
                    b0 = 4 * c
                    st = S0[:, b0:b0 + 4, :]
                    dve.wait_ge(h_vb, 2 * h + c + 1)
                    t4 = TMP[:, 0:SEQ].rearrange("p (c n) -> p c n", c=4)
                    dve.tensor_tensor(t4, MB[4].rearrange("p (c n) -> p c n", c=4),
                                      k[:, SEQ + b0:SEQ + b0 + 4].unsqueeze(2).to_broadcast([128, 4, 128]), ALU.mult)
                    done(dve.tensor_tensor(st, st, FS[h % 2][:, b0:b0 + 4].unsqueeze(2).to_broadcast([128, 4, 128]), ALU.mult))
                    dve.tensor_tensor(st, st, t4, ALU.add).then_inc(h_sn, 1)
                elif s == 3:
                    dve.wait_ge(h_kt, h + 1)
                    dve.tensor_scalar(EF[:, 1, :], g, -80.0, None, ALU.max).then_inc(h_gc, 1)
                    dve.wait_ge(h_u, h + 1)
                    done(dve.tensor_copy(SF[:, 0:128], MB[3][:, 0:128]))
                    for c in range(1, 4):
                        ins = dve.scalar_tensor_tensor(SF[:, 128 * c:128 * c + 128], SF[:, 128 * c - 128:128 * c], DEC[:, c:c + 1],
                                                       MB[3][:, 128 * c:128 * c + 128], ALU.mult, ALU.add)
                        if c < 3:
                            done(ins)
                    ins.then_inc(h_st, 1)
                elif s == 4:
                    dve.wait_ge(h_o, h + 1)
                    dve.tensor_copy(TMP[:, 0:SEQ], MB[0])
                    done(dve.tensor_copy(TMP[:, SEQ:T], MB[4][:, 0:DB]))
                    dve.tensor_tensor(EF[:, 0, :], TMP[:, :], TMP[:, :], ALU.mult).then_inc(h_sq, 1)
                    dve.wait_ge(h_ge, h + 1)
                    done(dve.tensor_scalar(EF[:, 1, :], EF[:, 1, :], 1.0, None, ALU.add))
                    done(dve.reciprocal(EF[:, 1, :], EF[:, 1, :]))
                    done(dve.scalar_tensor_tensor(g, g, GAIN, EF[:, 1, :], ALU.mult, ALU.mult))
                elif s == 5:
                    dve.wait_ge(h_rt, h + 1)
                    done(dve.reciprocal(QF[:, 1, :], QF[:, 1, :]))
                    done(dve.tensor_tensor(TMP[:, :], TMP[:, :], QF[:, 1, :], ALU.mult))
                    dve.tensor_tensor(Y[:, 8 + h, :], TMP[:, :], g, ALU.mult).then_inc(s_grp, 1)

            def conv(j):
                cc, ch, cb = (slot(CV0[j] + k) for k in range(3))
                dve.wait_ge(s_pr, 2 * CV0[j] + 6)
                y = Y[:, 12 + j, :]
                w = [CW[:, 3 * j + k:3 * j + k + 1] for k in range(3)]
                done(dve.tensor_tensor(cc, cc, ch, ALU.mult))
                dve.tensor_copy(CVO[:, j, 0:2], cc[:, SEQ - 2:SEQ])
                so = CVO[:, j, 2:18].rearrange("p (b r) -> p b r", r=2)
                dve.tensor_copy(so[:, :, 0], HIST[:, j, :, 1])
                dve.tensor_copy(so[:, :, 1], cc[:, SEQ:T])
                done(dve.tensor_scalar(y, cc, w[2], None, ALU.mult))
                dve.scalar_tensor_tensor(y[:, 1:SEQ], cc[:, 0:SEQ - 1], w[1], y[:, 1:SEQ], ALU.mult, ALU.add)
                done(dve.scalar_tensor_tensor(y[:, SEQ:T], HIST[:, j, :, 1], w[1], y[:, SEQ:T], ALU.mult, ALU.add))
                dve.scalar_tensor_tensor(y[:, 2:SEQ], cc[:, 0:SEQ - 2], w[0], y[:, 2:SEQ], ALU.mult, ALU.add)
                done(dve.scalar_tensor_tensor(y[:, SEQ:T], HIST[:, j, :, 0], w[0], y[:, SEQ:T], ALU.mult, ALU.add))
                dve.tensor_tensor(y, y, cb, ALU.mult).then_inc(s_grp, 1)

            for q in range(NQ):
                for what, n in MIX[q]:
                    if what == "att_scores":
                        att_scores(n)
                    elif what == "att_pv":
                        att_pv(n)
                    elif what.startswith("smp"):
                        smp(int(what[3:]), n)
                    elif what == "hg_prep":
                        hg_prep(n)
                    elif what == "hg_k":
                        hg_k(n)
                    elif what == "hg_factor":
                        hg_factor(n)
                    elif what == "hg_level":
                        hg_level(n)
                    elif what in ("hg0", "hg1", "hg2", "hg3", "hg4", "hg5"):
                        hg(int(what[2:]), n)
                    elif what == "conv":
                        conv(n)
            for c in range(KC):
                if c == 2:
                    conv(3)
                dve.wait_ge(s_yh, c + 1)
                dve.tensor_tensor(XL[:, c, :], Y[:, c, :], XH[:, c, :].bitcast(F32), ALU.subtract).then_inc(s_yl, 1)

            def column_stats(k):
                for i in range(NT):
                    dve.wait_ge(s_rcp, NT * k + i + 1)
                    ins = dve.bn_stats(ST[0:TT, i, k, :], R[:, i, 512 * k:512 * k + 512])
                return ins

            for n in range(KC):
                for hf in range(2):
                    m = 2 * n + hf
                    dve.wait_ge(s_ob, m + 1)
                    if hf == 0:
                        dve.wait_ge(s_r[n % NRT], 16 * (n // NRT + 1))
                    r = RT[:, n % NRT, hf * HALF:(hf + 1) * HALF]
                    dve.scalar_tensor_tensor(r, r, ALPHA, BANK[:, m % 2, 0:HALF], ALU.mult, ALU.add).then_inc(s_rt, 1)
                    if hf == 0 and n % 4 == 0 and n:
                        column_stats(n // 4 - 1)
                if n == 0:
                    dve.wait_ge(s_wr, 32)
                    done(dve.tensor_tensor(GW[:, :, :], WR[:, :, :], GB1[:, 0, :].unsqueeze(2).to_broadcast([128, KC, 20]), ALU.mult))
                    dve.tensor_tensor(WR[:, :, :], WR[:, :, :], GB1[:, 1, :].unsqueeze(2).to_broadcast([128, KC, 20]), ALU.mult).then_inc(s_gw, 1)
            done(column_stats(3))
            for i in range(NT):
                ins = dve.bn_aggr(MV[0:TT, i, 0:2], ST[0:TT, i, :, :].rearrange("p n s -> p (n s)"))
            ins.then_inc(s_var, 1)

            dve.wait_ge(s_log, 4)
            dve.wait_ge(s_rc, 128)
            tt, ts = dve.tensor_tensor, dve.tensor_scalar

            def bc(x, *shape):
                return x.to_broadcast(list(shape))

            def col(x):
                return x[:, :].unsqueeze(2)

            done(tt(RB[:, :], RB[:, :], BANK[0:TT, 7, 420:440], ALU.add))
            done(dve.tensor_reduce(LO_G[:, :, :].rearrange("p i n -> p (i n)"), BANK[0:TT, 7, 0:400].rearrange("p (k x) -> p x k", k=4), AX.X, ALU.add))
            dve.wait_ge(s_var, 1)
            done(tt(OH[:, 0, :, 0:20], bc(BANK[0:TT, 7, 400:420].unsqueeze(1), TT, NT, 20), bc(MV[0:TT, :, 0:1], TT, NT, 20), ALU.mult))
            done(tt(LO_G[:, :, :], LO_G[:, :, :], OH[:, 0, :, 0:20], ALU.subtract))
            dve.wait_ge(s_sd, 1)
            done(dve.reciprocal(MV[0:TT, :, 2:3], MV[0:TT, :, 2:3]))
            dve.scalar_tensor_tensor(MV[0:TT, :, 3:4], MV[0:TT, :, 0:1], -1.0, MV[0:TT, :, 2:3], ALU.mult, ALU.mult).then_inc(s_rs, 1)
            done(tt(LO_G[:, :, :], LO_G[:, :, :], bc(MV[0:TT, :, 2:3], TT, NT, 20), ALU.mult))
            done(tt(LO_G[:, :, :], LO_G[:, :, :], bc(RB[:, :].unsqueeze(1), TT, NT, 20), ALU.add))
            gl, el = LO_G[:, :, 0:4], LO_G[:, :, 4:20]
            gm, gs, dif, w1, w2, v1, v2 = (C5[k] for k in range(7))
            done(dve.tensor_reduce(gm[:, :], gl, AX.X, ALU.max))
            done(tt(G4[0][:, :, :], gl, bc(col(gm), TT, NT, 4), ALU.is_equal))
            tt(G4[1][:, :, :], gl, bc(col(gm), TT, NT, 4), ALU.subtract).then_inc(r_e, 1)

            def first(hot, iota, n, tmp):
                io = bc(iota[:, :].unsqueeze(1), TT, NT, n)
                done(dve.scalar_tensor_tensor(hot, io, float(n), hot, ALU.subtract, ALU.mult))
                done(dve.tensor_reduce(tmp[:, :], hot, AX.X, ALU.min))
                done(ts(tmp[:, :], tmp[:, :], float(n), None, ALU.add))
                done(tt(hot, io, bc(col(tmp), TT, NT, n), ALU.is_equal))

            first(G4[0][:, :, :], IO4, 4, C5[7])
            ghot = G4[0][:, :, :]
            em, hot1, hot2, em2, rk, sel = (E16[k] for k in range(6))
            g16 = ghot.unsqueeze(3).to_broadcast([TT, NT, 4, 4])
            done(ts(hot2[:, :, :].rearrange("p i (g e) -> p i g e", g=4), g16, -NEG, NEG, ALU.mult, ALU.add))
            done(tt(em[:, :, :].rearrange("p i (g e) -> p i g e", g=4), el.rearrange("p i (g e) -> p i g e", g=4), g16, ALU.mult))
            done(tt(em[:, :, :], em[:, :, :], hot2[:, :, :], ALU.add))
            done(dve.tensor_reduce(v1[:, :], em[:, :, :], AX.X, ALU.max))
            done(tt(hot1[:, :, :], em[:, :, :], bc(col(v1), TT, NT, 16), ALU.is_equal))
            first(hot1[:, :, :], IO16, 16, C5[7])
            done(dve.scalar_tensor_tensor(em2[:, :, :], hot1[:, :, :], NEG, em[:, :, :], ALU.mult, ALU.add))
            done(dve.tensor_reduce(v2[:, :], em2[:, :, :], AX.X, ALU.max))
            done(tt(hot2[:, :, :], em2[:, :, :], bc(col(v2), TT, NT, 16), ALU.is_equal))
            first(hot2[:, :, :], IO16, 16, C5[7])
            tt(rk[:, :, :], hot1[:, :, :], hot2[:, :, :], ALU.add).then_inc(r_hot, 1)
            tt(dif[:, :], v2[:, :], v1[:, :], ALU.subtract).then_inc(r_e, 1)
            dve.wait_ge(r_x, 2)
            done(dve.tensor_reduce(gs[:, :], G4[1][:, :, :], AX.X, ALU.add))
            done(dve.reciprocal(gs[:, :], gs[:, :]))
            done(ts(w1[:, :], dif[:, :], 1.0, None, ALU.add))
            done(dve.reciprocal(w1[:, :], w1[:, :]))
            done(tt(w2[:, :], w1[:, :], dif[:, :], ALU.mult))
            done(tt(w1[:, :], w1[:, :], gs[:, :], ALU.mult))
            done(tt(w2[:, :], w2[:, :], gs[:, :], ALU.mult))
            dve.wait_ge(s_nd, 1)
            dve.wait_ge(s_lg, 32)
            done(tt(R[:, NT - 1, :], R[:, NT - 1, :], LG[:, :], ALU.mult))
            tt(R[:, NT - 1, :], R[:, NT - 1, :], LB[:, :], ALU.add).then_inc(s_x1d, 1)
            dve.wait_ge(r_rank, 1)
            before = BANK[0:TT, 0, 0:80].rearrange("p (i e) -> p i e", i=NT)
            total = BANK[0:TT, 1, 0:80].rearrange("p (i e) -> p i e", i=NT)
            cnt, nblk, bstart, tmp16 = (NB16[k] for k in range(4))
            done(dve.tensor_copy(em[:, :, :], total))
            done(dve.tensor_copy(sel[:, :, :], before))
            for i in range(1, NT):
                done(tt(em2[:, i, :], em[:, i - 1, :], em2[:, i - 1, :], ALU.add) if i > 1 else dve.tensor_copy(em2[:, 1, :], em[:, 0, :]))
                done(tt(sel[:, i, :], sel[:, i, :], em2[:, i, :], ALU.add))
            done(tt(cnt[:, :], em[:, NT - 1, :], em2[:, NT - 1, :], ALU.add))
            done(ts(nblk[:, :], cnt[:, :], 0.5, None, ALU.is_ge))
            for b in range(1, NT):
                done(dve.scalar_tensor_tensor(nblk[:, :], cnt[:, :], CAP * b + 0.5, nblk[:, :], ALU.is_ge, ALU.add))
            done(ts(nblk[:, 0:1], nblk[:, 0:1], 1.0, None, ALU.max))
            done(dve.memset(bstart[:, 0:1], 0.0))
            for e in range(1, NE):
                done(tt(bstart[:, e:e + 1], bstart[:, e - 1:e], nblk[:, e - 1:e], ALU.add))
            done(tt(EBC[:, :, :], bc(bstart[:, :].unsqueeze(1), TT, MAXB + 1, 16), bc(IO24[:, :].unsqueeze(2), TT, MAXB + 1, 16), ALU.is_le))
            done(dve.memset(EBF[:, :], 0.0))
            done(dve.tensor_reduce(EBF[:, 0:MAXB + 1], EBC[:, :, :], AX.X, ALU.add))
            done(ts(EBF[:, 0:MAXB + 1], EBF[:, 0:MAXB + 1], -1.0, None, ALU.add))
            done(dve.scalar_tensor_tensor(EBF[:, 31:32], bstart[:, 15:16], -1.0, nblk[:, 15:16], ALU.add, ALU.add))
            dve.tensor_copy(EBI[:, :], EBF[0:1, :])
            for c, hot, w in ((0, hot1, w1), (1, hot2, w2)):
                r, b, bb, row = C5[8], C5[9], C5[10], C5[11 + c]
                done(tt(em[:, :, :], hot[:, :, :], sel[:, :, :], ALU.mult))
                done(dve.tensor_reduce(r[:, :], em[:, :, :], AX.X, ALU.add))
                done(tt(em[:, :, :], hot[:, :, :], bc(bstart[:, :].unsqueeze(1), TT, NT, 16), ALU.mult))
                done(dve.tensor_reduce(b[:, :], em[:, :, :], AX.X, ALU.add))
                done(ts(bb[:, :], r[:, :], CAP - 0.5, None, ALU.is_ge))
                for k in range(2, NT):
                    done(dve.scalar_tensor_tensor(bb[:, :], r[:, :], CAP * k - 0.5, bb[:, :], ALU.is_ge, ALU.add))
                done(tt(b[:, :], b[:, :], bb[:, :], ALU.add))
                done(dve.scalar_tensor_tensor(r[:, :], bb[:, :], -float(CAP), r[:, :], ALU.mult, ALU.add))
                done(ts(row[:, :], TID[:, :], float(c * T), None, ALU.add))
                tt(OH[:, c, :, :], bc(IO128[:, :].unsqueeze(1), TT, NT, 128), bc(col(r), TT, NT, 128), ALU.is_equal)
                one = TB[:, c, :, 0, :]
                done(tt(one, bc(IO24[:, :].unsqueeze(1), TT, NT, MAXB + 1), bc(col(b), TT, NT, MAXB + 1), ALU.is_equal))
                done(tt(TB[:, c, :, 1, :], one, bc(col(w), TT, NT, MAXB + 1), ALU.mult))
                done(tt(TB[:, c, :, 2, :], one, bc(col(row), TT, NT, MAXB + 1), ALU.mult))
                tt(one, one, bc(TID[:, :].unsqueeze(2), TT, NT, MAXB + 1), ALU.mult).then_inc(r_tab, 1)
                dve.wait_ge(r_tab, c + 1)
            dve.wait_ge(r_tabm, 1)
            done(dve.tensor_copy(TABF[:, :, :], BANK[:, 2, 0:3 * (MAXB + 1)].rearrange("p (k j) -> p k j", k=3)))
            for k, dst, skip in ((0, TIX, SKP[:, 0:1]), (2, YIX, SKIP)):
                v = TABF[:, k, :]
                done(ts(TABZ[:, :], v, 0.0, skip, ALU.is_equal, ALU.mult))
                done(ts(v, v, -1.0, 0.0, ALU.add, ALU.max))
                done(tt(TABZ[:, :], TABZ[:, :], v, ALU.add))
                if k == 0:
                    done(dve.tensor_copy(dst[:, :], TABZ[:, :]))
                else:
                    dve.tensor_copy(dst[:, :], TABZ[:, :]).then_inc(r_idx, 1)

            dve.wait_ge(r_idx, 1)
            nb = dve.value_load(EBI[0:1, 31:32], min_val=8, max_val=MAXB - 1) + 1

            def blo(i, m0, j):
                s, r = (i % NHL, i % NRAW) if m0 is None else ((2 + i) % NHL, (2 + i) % NRAW)
                dve.wait_ge(b_hi, i + 1 if m0 is None else 12 * j + i - 3)
                dve.tensor_tensor(LOB[:, s, :], RAWB[:, r, :], HIB[:, s, :].bitcast(F32), ALU.subtract).then_inc(b_lo[s], 1)

            def h_made(j):
                dve.wait_ge(b_sg, j + 1)
                if not isinstance(j, int) or j >= 1:
                    dve.wait_ge(b_th, j)
                dve.scalar_tensor_tensor(H[:, :], SG[:, :], TABF[:, 1, bass.ds(j, 1)], BANK[:, 1, :], ALU.mult, ALU.mult).then_inc(b_h, 1)

            def token_lo(g, j):
                dve.wait_ge(b_xh, 4 * j + g + 1)
                dve.tensor_tensor(XGL[:, 4 * g:4 * g + 4, :], BANK[:, 2 + g % 2, :].rearrange("p (c n) -> p c n", c=4),
                                  XGH[:, 4 * g:4 * g + 4, :].bitcast(F32), ALU.subtract).then_inc(b_xl, 1)

            def h_lo(j):
                dve.wait_ge(b_hh, j + 1)
                dve.tensor_tensor(HTL[:, :, :], BANK[:, 6, :].rearrange("p (c n) -> p c n", c=4), HTH[:, :, :].bitcast(F32),
                                  ALU.subtract).then_inc(b_hl, 1)

            for i in range(AHEAD):
                blo(i, None, 0)
            for g in range(4):
                token_lo(g, 0)
            for i in range(AHEAD, 8):
                blo(i, None, 0)
            h_made(0)
            for g in range(4):
                token_lo(g, 1)
            for i in range(2):
                blo(i, 0, 1)
            with dve.Fori(1, MAXB) as j:
                with dve.If(j < nb):
                    h_lo(j - 1)
                    for i in range(2, 10):
                        blo(i, 0, j)
                    h_made(j)
                    token_lo(0, j + 1)
                    blo(10, 0, j)
                    token_lo(1, j + 1)
                    blo(11, 0, j)
                    token_lo(2, j + 1)
                    blo(0, 0, j + 1)
                    token_lo(3, j + 1)
                    blo(1, 0, j + 1)
            h_lo(nb - 1)
            for n in range(2, 4):
                blo(n, 0, nb)

            mu, sd, sq = (lambda i: MV[0:TT, i, 0:1]), (lambda i: MV[0:TT, i, 2:3]), (lambda i: MV[0:TT, i, 3:4])

            def added(i):
                dve.wait_ge(f_ab, i + 1)
                r = R[:, i, :]
                done(dve.scalar_tensor_tensor(r, r, ALPHA, YA[:, i % 2, :], ALU.mult, ALU.add, accum_out=sq(i)))
                dve.tensor_scalar(mu(i), sq(i), -1.0 / D, None, ALU.mult).then_inc(f_st, 1)

            def scaled(i):
                if i == 0:
                    dve.wait_ge(f_ln, 32)
                dve.wait_ge(f_nm, i + 1)
                done(tt(R[:, i, :], R[:, i, :], LG2[:, :], ALU.mult))
                tt(R[:, i, :], R[:, i, :], LB2[:, :], ALU.add).then_inc(f_y, 1)

            def rstd(i):
                dve.wait_ge(f_sd, i + 1)
                done(dve.reciprocal(sd(i), sd(i)))
                dve.tensor_tensor(sq(i), mu(i), sd(i), ALU.mult).then_inc(f_rs, 1)

            added(0)
            for i in range(NT):
                if i + 1 < NT:
                    added(i + 1)
                rstd(i)
                if i >= 1:
                    scaled(i - 1)
            scaled(NT - 1)

        @block.tensor
        def _(pe):
            def quarter(u, hf, kq):
                m = 2 * u + hf
                if hf == 0 and kq == 0:
                    pe.wait_ge(s_hi, u + 1)
                    pe.wait_ge(s_lo, u + 1)
                if kq == 0 and m >= 3:
                    pe.wait_ge(s_pr, m - 2)
                hw = HI[:, u % 2, :].rearrange("p (c n) -> p c n", c=KC)
                lw = LO[:, u % 2, :].rearrange("p (c n) -> p c n", c=KC)
                cols = slice(hf * HALF, (hf + 1) * HALF)
                for c in range(8 * kq, 8 * kq + 8):
                    if u == 0 and hf == 0 and c % 4 == 0:
                        pe.wait_ge(s_xl, c // 4 + 1)
                    pe.matmul(acc(m), hw[:, c, :], XH[:, c, cols], start=(c == 0), stop=False)
                    pe.matmul(acc(m), hw[:, c, :], XL[:, c, cols], start=False, stop=False)
                    ins = pe.matmul(acc(m), lw[:, c, :], XH[:, c, cols], start=False, stop=(c == KC - 1))
                if kq == 1:
                    ins.then_inc(s_acc, 1)

            def att_setup(t):
                u0 = ATT0[t]
                pe.wait_ge(s_pr, 2 * u0 + 12)
                pe.wait_ge(s_const, 160)
                if t:
                    pe.wait_ge(s_grp, t)
                for c in range(4):
                    ins = pe.transpose(MB[2][:, 128 * c:128 * c + 128], slot(u0 + 1)[:, 128 * c:128 * c + 128], IDENT[:, :])
                ins.then_inc(s_vt_t, 1)
                for k in range(2):
                    ins = pe.transpose(MB[3][0:DB, 128 * k:128 * k + 128], slot(u0 + k)[:, SEQ:T], IDENT[:, :])
                ins.then_inc(s_vt_t, 1)

            def att_scores(s):
                t, (l, qb) = s // 8, STEPS[s % 8]
                u0, b = ATT0[t], 64 * l
                k0 = 128 if qb == 0 else 0
                if s >= 1:
                    pe.wait_ge(s_mx, s)
                for j in range(4):
                    dst = MB[j // 2].rearrange("p (c n) -> p c n", c=2)[:, j % 2, k0:256]
                    ins = pe.matmul(dst, slot(u0 + 2 + j)[b:b + 64, 128 * qb:128 * qb + 128],
                                    slot(u0)[b:b + 64, 128 * qb - 128 + k0:128 * qb + 128], start=True, stop=True)
                ins.then_inc(s_sc, 1)

            def att_turn(s):
                t, (l, qb) = s // 8, STEPS[s % 8]
                pe.wait_ge(s_p, s + 1)
                if s >= 1:
                    pe.wait_ge(s_pt, s)
                pe.wait_ge(s_vt, 2 * t + 2)
                for k in range(1 if qb == 0 else 0, 2):
                    for j in range(4):
                        ins = pe.transpose(MB[2 + k][:, 128 * j:128 * j + 128], SC[:, j, 128 * k:128 * k + 128], IDENT[:, :])
                ins.then_inc(s_tp, 1)

            def att_pv(s):
                t, (l, qb) = s // 8, STEPS[s % 8]
                b = 64 * l
                pe.wait_ge(s_pt, s + 1)
                if s >= 1:
                    pe.wait_ge(s_yc, s)
                ks = [1] if qb == 0 else [0, 1]
                for k in ks:
                    ins = pe.matmul(MB[4][b:b + 64, :], VT[:, qb - 1 + k, b:b + 64], PT[:, k, :, :],
                                    start=(k == ks[0]), stop=(k == 1))
                ins.then_inc(s_pv, 1)

            def smp(s, t):
                u0 = ATT0[t]
                if s == 0:
                    pe.wait_ge(s_kc, 32 * (t + 1))
                    pe.wait_ge(s_self, 32 * (t + 1))
                    pe.wait_ge(s_pt, 8 * t + 8)
                    for b in range(DB):
                        ins = pe.transpose(MB[2 + b // 4][:, 128 * (b % 4):128 * (b % 4) + 128], KCA[:, b, :], IDENT[:, :])
                    ins.then_inc(s_m[0], 1)
                elif s == 1:
                    pe.wait_ge(s_m[1], t + 1)
                    pe.wait_ge(s_mx, 8 * t + 8)
                    for b in range(DB):
                        for l in range(2):
                            s0 = (u0 + 2) % 16
                            ins = pe.matmul(MB[l][:, 4 * b:4 * b + 4], KTS[64 * l:64 * l + 64, b, :],
                                            PR[64 * l:64 * l + 64, s0:s0 + 4, SEQ + b], start=True, stop=True)
                    ins.then_inc(s_m[2], 1)
                elif s == 2:
                    pe.wait_ge(s_m[3], t + 1)
                    pe.transpose(MB[1][0:64, 0:128], SST[:, :], IDENT[:, :]).then_inc(s_m[4], 1)
                elif s == 3:
                    pe.wait_ge(s_m[7], t + 1)
                    pe.transpose(MB[3][:, 0:64], SSR[:, :], IDENT[0:64, 0:64]).then_inc(s_m[8], 1)
                elif s == 4:
                    pe.wait_ge(s_m[9], t + 1)
                    pe.wait_ge(s_yc, 8 * t + 8)
                    for b in range(DB):
                        for l in range(2):
                            c = 32 * l + 4 * b
                            ins = pe.matmul(MB[4][64 * l:64 * l + 64, 4 * b:4 * b + 4], VCA[:, b, 64 * l:64 * l + 64],
                                            PST[:, c:c + 4], start=True, stop=True)
                    ins.then_inc(s_m[10], 1)

            def hg_level(x):
                h, l = x // 8, x % 8
                q, k = slot(HG0[h]), slot(HG0[h] + 1)
                z = l % 2
                if l == 0:
                    pe.wait_ge(h_k, h + 1)
                else:
                    pe.wait_ge(h_mul, 7 * h + l)
                if l >= 2:
                    pe.wait_ge(h_acc, 8 * h + l - 1)
                for c in range(4):
                    cols = slice(128 * c, 128 * c + 128)
                    if l == 0:
                        ins = pe.matmul(MB[0][:, cols], k[:, cols], q[:, cols], start=True, stop=True)
                    else:
                        n = 1 << (l - 1)
                        qq = QF[:, z, cols].rearrange("p (b s n) -> p b s n", s=2, n=n)[:, :, 1, :]
                        ins = pe.matmul(MB[l % 2][:, 64 * c:64 * c + 64], QF[:, z, cols], qq, start=True, stop=True)
                ins.then_inc(h_lev, 1)
                if l == 4:
                    v = slot(HG0[h] + 2)
                    for c in range(4):
                        ins = pe.transpose(MB[2][:, 128 * c:128 * c + 128], v[:, 128 * c:128 * c + 128], IDENT[:, :])
                    ins.then_inc(h_vt, 1)

            def spread(h, c):
                v = slot(HG0[h] + 2)
                if c:
                    pe.wait_ge(h_sn, 2 * h + c)
                for b in range(4):
                    t = SEQ + 4 * c + b
                    ins = pe.transpose(MB[4][:, 128 * b:128 * b + 128], v[:, t:t + 1].to_broadcast([128, 128]), IDENT[:, :])
                ins.then_inc(h_vb, 1)

            def hg(s, h):
                q = slot(HG0[h])
                if s == 0:
                    spread(h, 0)
                elif s == 1:
                    pe.wait_ge(h_ks, h + 1)
                    pe.wait_ge(h_vtc, h + 1)
                    for c in range(4):
                        ins = pe.transpose(MB[2][:, 128 * c:128 * c + 128], EF[:, 1, 128 * c:128 * c + 128], IDENT[:, :])
                    ins.then_inc(h_kt, 1)
                elif s == 2:
                    spread(h, 1)
                    pe.wait_ge(h_ktc, h + 1)
                    for c in range(4):
                        ins = pe.matmul(MB[3][:, 128 * c:128 * c + 128], PF[:, 128 * c:128 * c + 128], VTK[:, c, :], start=True, stop=True)
                    ins.then_inc(h_u, 1)
                elif s == 4:
                    pe.wait_ge(h_st, h + 1)
                    pe.wait_ge(h_sn, 2 * h + 2)
                    pe.wait_ge(h_acc, 8 * h + 8)
                    for c in range(4):
                        cols = slice(128 * c, 128 * c + 128)
                        pe.matmul(MB[0][:, cols], VTK[:, c, :], AT[:, c, :], start=True, stop=(c == 0))
                        if c:
                            pe.matmul(MB[0][:, cols], SF[:, 128 * c - 128:128 * c], QF[:, 0, cols], start=False, stop=True)
                    for b in range(DB):
                        ins = pe.matmul(MB[4][:, b:b + 1], S0[:, b, :], q[:, SEQ + b:SEQ + b + 1], start=True, stop=True)
                    ins.then_inc(h_o, 1)
                elif s == 5:
                    pe.wait_ge(h_sq, h + 1)
                    pe.wait_ge(s_ones, 1)
                    pe.matmul(MB[1], ONES[:, :], EF[:, 0, 0:SEQ], start=True, stop=True)
                    pe.matmul(MB[2][:, 0:DB], ONES[:, :], EF[:, 0, SEQ:T], start=True, stop=True).then_inc(h_ss, 1)

            for q in range(NQ):
                quarter(q // 4, q % 4 // 2, q % 2)
                for what, n in MIX[q]:
                    if what == "att_setup":
                        att_setup(n)
                    elif what == "att_scores":
                        att_scores(n)
                    elif what == "att_turn":
                        att_turn(n)
                    elif what == "att_pv":
                        att_pv(n)
                    elif what.startswith("smp"):
                        smp(int(what[3:]), n)
                    elif what == "hg_level":
                        hg_level(n)
                    elif what in ("hg0", "hg1", "hg2", "hg4", "hg5"):
                        hg(int(what[2:]), n)

            def turn(n):
                pe.wait_ge(s_rt, 2 * n + 2)
                if n == 0:
                    pe.wait_ge(s_grp, 10)
                elif n % 4 == 0:
                    pe.wait_ge(s_rcp, NT * (n // 4))
                for i in range(NT):
                    ins = pe.transpose(BANK[0:TT, 2 + i, 128 * (n % 4):128 * (n % 4) + 128], RT[:, n % NRT, i * TT:(i + 1) * TT], IDENT[:, :])
                ins.then_inc(s_turn, 1)

            def router(k):
                if k == 0:
                    pe.wait_ge(s_gw, 1)
                    for j, w in ((400, GW), (420, WR)):
                        for c in range(KC):
                            pe.matmul(BANK[0:TT, 7, j:j + 20], ONES[:, 0:TT], w[:, c, :], start=(c == 0), stop=(c == KC - 1))
                for i in range(NT):
                    for c in range(4):
                        ins = pe.matmul(BANK[0:TT, 7, 100 * k + 20 * i:100 * k + 20 * i + 20], RT[:, (4 * k + c) % NRT, i * TT:(i + 1) * TT],
                                        GW[:, 4 * k + c, :], start=(c == 0), stop=(c == 3))
                ins.then_inc(s_log, 1)

            for n in range(KC):
                u = NU + n
                pe.wait_ge(s_hi, u + 1)
                pe.wait_ge(s_lo, u + 1)
                if n == 0:
                    pe.wait_ge(s_pr, 2 * NU)
                hw = HI[:, u % 2, :].rearrange("p (c n) -> p c n", c=KC)
                lw = LO[:, u % 2, :].rearrange("p (c n) -> p c n", c=KC)
                for hf in range(2):
                    m = 2 * n + hf
                    if m >= 2:
                        pe.wait_ge(s_rt, m - 1)
                    b = BANK[:, m % 2, 0:HALF]
                    cols = slice(hf * HALF, (hf + 1) * HALF)
                    for c in range(KC):
                        if m == 0:
                            pe.wait_ge(s_yl, c + 1)
                        pe.matmul(b, hw[:, c, :], XH[:, c, cols], start=(c == 0), stop=False)
                        pe.matmul(b, hw[:, c, :], XL[:, c, cols], start=False, stop=False)
                        ins = pe.matmul(b, lw[:, c, :], XH[:, c, cols], start=False, stop=(c == KC - 1))
                    ins.then_inc(s_ob, 1)
                    if hf == 0 and n >= 1:
                        turn(n - 1)
                        if n % 4 == 0:
                            router(n // 4 - 1)
            turn(KC - 1)
            router(3)
            pe.wait_ge(r_hot, 1)
            pe.wait_ge(s_rc, 128)
            hot = E16[4][:, :, :].rearrange("p i e -> p (i e)")
            pe.matmul(BANK[0:TT, 0, 0:80], TRI[:, :], hot, start=True, stop=True)
            pe.matmul(BANK[0:TT, 1, 0:80], ONES[0:TT, 0:TT], hot, start=True, stop=True).then_inc(r_rank, 1)
            pe.wait_ge(r_tab, 2)
            for c in range(2):
                for i in range(NT):
                    ins = pe.matmul(BANK[:, 2, 0:3 * (MAXB + 1)], OH[:, c, i, :], TB[:, c, i, :, :].rearrange("p k j -> p (k j)"),
                                    start=(c == 0 and i == 0), stop=(c == 1 and i == NT - 1))
            ins.then_inc(r_tabm, 1)

            pe.wait_ge(r_idx, 1)
            nb = pe.value_load(EBI[0:1, 31:32], min_val=8, max_val=MAXB - 1) + 1

            def tokens(g, j):
                if g == 0:
                    pe.wait_ge(b_yw, 16) if isinstance(j, int) and j == 0 else pe.wait_ge(b_xg, 16 * j)
                if not isinstance(j, int) or 4 * j + g >= 2:
                    pe.wait_ge(b_xl, 4 * j + g - 1)
                for c in range(4):
                    ins = pe.transpose(BANK[:, 2 + g % 2, 128 * c:128 * c + 128], XG[:, 4 * g + c:D:KC], IDENT[:, :])
                ins.then_inc(b_tx, 1)

            def ready(i, m0, j):
                s = i % NHL if m0 is None else (2 + i) % NHL
                pe.wait_ge(b_lo[s], i // NHL + 1 if m0 is None else (8 + i) // NHL + 1 + 4 * (j - 1))
                return HIB[:, s, :].rearrange("p (c n) -> p c n", c=4), LOB[:, s, :].rearrange("p (c n) -> p c n", c=4)

            def gate_up(j, m0):
                pe.wait_ge(b_xl, 4 * j + 4)
                if m0 is not None:
                    pe.wait_ge(b_h, j)
                for i in range(8):
                    hw, lw = ready(i, m0, j)
                    b = BANK[:, i % 2, :]
                    for c in range(4):
                        cc = 4 * (i // 2) + c
                        pe.matmul(b, XGH[:, cc, :], hw[:, c, :], start=(cc == 0), stop=False)
                        pe.matmul(b, XGL[:, cc, :], hw[:, c, :], start=False, stop=False)
                        ins = pe.matmul(b, XGH[:, cc, :], lw[:, c, :], start=False, stop=(cc == KC - 1))
                    ins.then_inc(b_used, 1)

            def turn_h(j):
                pe.wait_ge(b_h, j + 1)
                if not isinstance(j, int):
                    pe.wait_ge(b_hl, j)
                for c in range(4):
                    ins = pe.transpose(BANK[:, 6, 128 * c:128 * c + 128], H[:, c:512:4], IDENT[:, :])
                ins.then_inc(b_th, 1)

            def down(n, i, j):
                if n == 0:
                    pe.wait_ge(b_hl, j)
                pe.wait_ge(b_y, 4 * (j - 1) + n + 1)
                hw, lw = ready(i, 0, j)
                b = BANK[:, 4 + n % 2, :]
                for c in range(4):
                    pe.matmul(b, HTH[:, c, :], hw[:, c, :], start=(c == 0), stop=False)
                    pe.matmul(b, HTL[:, c, :], hw[:, c, :], start=False, stop=False)
                    ins = pe.matmul(b, HTH[:, c, :], lw[:, c, :], start=False, stop=(c == 3))
                ins.then_inc(b_used, 1)

            for g in range(4):
                tokens(g, 0)
            gate_up(0, None)
            for g in range(4):
                tokens(g, 1)
            turn_h(0)
            with pe.Fori(1, MAXB) as j:
                with pe.If(j < nb):
                    gate_up(j, 0)
                    for n in range(4):
                        tokens(n, j + 1)
                        down(n, 8 + n, j)
                    turn_h(j)
            for n in range(4):
                down(n, n, nb)


def kernel(x_prompt, x_sample, state_conv, state_hgrn, cache_k_win, cache_v_win,
           w_in, w_out, conv_w, hg_lb_param, hg_gain, attn_sinks, ln1_g, ln1_b,
           w_group, b_group, w_router, b_router, w_gate, w_up, w_down, ln2_g, ln2_b):
    import concourse.bacc as bacc
    from concourse.bass_utils import run_bass_kernel_spmd as run

    A = np.asarray
    x = np.concatenate([A(x_prompt)[0], A(x_sample)[:, 0]], axis=0)
    arrays = {
        "xT": x.reshape(T, KC, 128).transpose(2, 1, 0).reshape(128, KC * T),
        "w_in": A(w_in)[0][:, feature_order()].reshape(KC, 128, NU, 128).transpose(2, 1, 0, 3).reshape(NU, 128, 2048),
        "w_out": A(w_out)[0][mix_order()].reshape(KC, 128, KC, 128).transpose(2, 1, 0, 3).reshape(KC, 128, 2048),
        "w_gate": A(w_gate)[0].reshape(NE, 128, KC * 512),
        "w_up": A(w_up)[0].reshape(NE, 128, KC * 512),
        "w_down": A(w_down)[0].reshape(NE, 128, 4, D),
        "wr": np.concatenate([A(w_group)[0], A(w_router)[0]], axis=1).reshape(KC, 128, 20).transpose(1, 0, 2),
        "gb1": np.stack([A(ln1_g)[0].reshape(KC, 128).T, A(ln1_b)[0].reshape(KC, 128).T], axis=1),
        "rb": np.broadcast_to(np.concatenate([A(b_group)[0], A(b_router)[0]]), (TT, 20)),
        "sink": np.broadcast_to(A(attn_sinks)[0], (128, 16)),
        "sinkc": np.broadcast_to(A(attn_sinks)[0].reshape(2, 2, 1, 4), (2, 2, DB, 4)).reshape(2, 64).T,
        "gain": A(hg_gain)[0].reshape(128, 1),
        "lbp": A(hg_lb_param)[0].reshape(4, 128).T,
        "cw": A(conv_w)[0].reshape(3, 4, 128).transpose(2, 1, 0).reshape(128, 12),
        "hist": A(state_conv)[0].reshape(DB, 2, 4, 128).transpose(3, 2, 0, 1).reshape(128, 64),
        "s0": A(state_hgrn)[0].transpose(1, 2, 0, 3),
        "cache_k": A(cache_k_win)[0].reshape(DB, WIN, 256),
        "cache_v": A(cache_v_win)[0].reshape(DB, WIN, 256),
        "ln1g": np.broadcast_to(A(ln1_g)[0], (TT, D)),
        "ln1b": np.broadcast_to(A(ln1_b)[0], (TT, D)),
        "ln2g": np.broadcast_to(A(ln2_g)[0], (TT, D)),
        "ln2b": np.broadcast_to(A(ln2_b)[0], (TT, D)),
    }
    f = np.float32
    i, j = np.arange(128)[:, None], np.arange(256)[None, :]
    dist = i + WIN - j
    s, t = np.arange(128)[:, None], np.arange(128)[None, :]
    levels = [s == t] + [(s // (2 * n) == t // (2 * n)) & (s % (2 * n) < n) & (t % (2 * n) >= n) for n in (1, 2, 4, 8, 16, 32, 64)]
    row = np.arange(64)[:, None]
    head = 8 * np.arange(2)[None, :] + 4 * (row // 32) + row % 4
    slope = np.array(SLOPE, f)[head]
    arrays |= {
        "ident": np.eye(128, dtype=f),
        "ndist": np.where((dist >= 0) & (dist < WIN), -dist, NEG).astype(f),
        "mask": np.stack(levels, axis=1).astype(np.float16),
        "nds": (-slope[:, :, None] * (127 - np.arange(128))[None, None, :].astype(f)).astype(f),
        "tri": (np.arange(TT)[:, None] < np.arange(TT)[None, :]).astype(f),
        "io128": np.broadcast_to(np.arange(128, dtype=f), (TT, 128)),
        "io24": np.broadcast_to(np.arange(MAXB + 1, dtype=f), (TT, MAXB + 1)),
        "io4": np.broadcast_to(np.arange(4, dtype=f), (TT, 4)),
        "io16": np.broadcast_to(np.arange(16, dtype=f), (TT, 16)),
        "tid": (np.arange(TT)[:, None] + TT * np.arange(NT)[None, :] + 1).astype(f),
        "skp": np.where(np.arange(128)[:, None] > 0, SKIP, 0.0).astype(f),
    }
    outs = {"yp": (SEQ, D), "ys": (DB, D), "cs": (128, 4, 18), "hp": (4, 128, 128), "hs": (4, 128, DB, 128),
            "kp": (2, 128, 128), "vp": (2, 128, 128), "ks": (2, 128, DB, 128), "vs": (2, 128, DB, 128)}

    nc = bacc.Bacc("TRN2", target_bir_lowering=False, num_devices=1)
    arrays = {n: np.ascontiguousarray(v) for n, v in arrays.items()}
    a = {n: nc.dram_tensor(f"in_{n}", v.shape, mybir.dt.from_np(v.dtype), kind="ExternalInput").ap() for n, v in arrays.items()}
    o = {n: nc.dram_tensor(f"out_{n}", sh, F32, kind="ExternalOutput").ap() for n, sh in outs.items()}
    build(nc, a, o)
    r = run(nc, [{f"in_{n}": v for n, v in arrays.items()}], core_ids=[0]).results[0]
    r = {n: r[f"out_{n}"] for n in outs}

    cs = r["cs"].transpose(2, 1, 0).reshape(18, 512)
    return (
        r["yp"].reshape(1, SEQ, D),
        r["ys"].reshape(DB, 1, D),
        cs[0:2].reshape(1, 1, 2, 512),
        cs[2:18].reshape(1, DB, 2, 512),
        r["hp"].reshape(1, 1, 4, 128, 128),
        r["hs"].transpose(2, 0, 1, 3).reshape(1, DB, 4, 128, 128),
        r["kp"].transpose(2, 0, 1).reshape(1, 1, WIN, 4, HD),
        r["ks"].transpose(2, 1, 0, 3).reshape(1, DB, WIN, 4, HD),
        r["vp"].transpose(1, 0, 2).reshape(1, 1, WIN, 4, HD),
        r["vs"].transpose(2, 1, 0, 3).reshape(1, DB, WIN, 4, HD),
    )
```

```python
import math
from contextlib import ExitStack

import numpy as np
import concourse.bass as bass
from concourse import mybir

F32 = mybir.dt.float32
F32R = mybir.dt.float32r
F16 = mybir.dt.float16
I32 = mybir.dt.int32
ALU = mybir.AluOpType
ACT = mybir.ActivationFunctionType
AX = mybir.AxisListType

D = 2048
SEQ, DB = 512, 8
T = SEQ + DB
HALF = T // 2
NT, TT = 5, T // 5
KC = D // 128
NU = 40
HD, WIN = 64, 128
NE, EPG, NG = 16, 4, 4
CAP = 128
MAXB = (2 * T - NE) // CAP + NE
DK = 128
ALPHA = 2.0 ** 0.25
LN_EPS, RMS_EPS = 1e-5, 1e-6
SLOPE = [2.0 ** (-8.0 * (h + 1) / 16) for h in range(16)]
NEG = -3e38
AHEAD = 3
SKIP = 4096.0

ATT0 = [0, 6]
HG0 = [12 + 4 * h for h in range(4)]
CV0 = [28 + 3 * j for j in range(4)]


def feature_order():
    cc, ch, cb = 512, 1024, 0
    hq, hf, hi, hg = 1536, 2048, 2560, 3072
    aq, ak, av = 3584, 4608, 4864
    out = []
    for t in range(2):
        out += [np.arange(ak + 128 * t, ak + 128 * t + 128), np.arange(av + 128 * t, av + 128 * t + 128)]
        for j in range(4):
            out.append(np.concatenate([np.arange(aq + 64 * h, aq + 64 * h + 64) for h in (8 * t + j, 8 * t + 4 + j)]))
    for h in range(4):
        out += [np.arange(b + 128 * h, b + 128 * h + 128) for b in (hq, hf, hi, hg)]
    for j in range(4):
        out += [np.arange(b + 128 * j, b + 128 * j + 128) for b in (cc, ch, cb)]
    return np.concatenate(out)


def mix_order():
    out = []
    for t in range(2):
        for j in range(4):
            out.append(np.concatenate([np.arange(1024 + 64 * h, 1024 + 64 * h + 64) for h in (8 * t + j, 8 * t + 4 + j)]))
    out += [np.arange(512 + 128 * h, 512 + 128 * h + 128) for h in range(4)]
    out += [np.arange(128 * j, 128 * j + 128) for j in range(4)]
    return np.concatenate(out)


NQ = 4 * NU
STEPS = [(l, qb) for l in range(2) for qb in range(4)]


def schedule():
    at = {q: [] for q in range(NQ + 40)}
    for t in range(2):
        b = (24, 56)[t]
        at[b].append(("att_setup", t))
        for i in range(8):
            at[b + 1 + 3 * i].append(("att_scores", 8 * t + i))
            at[b + 4 + 3 * i].append(("att_turn", 8 * t + i))
            at[b + 5 + 3 * i].append(("att_pv", 8 * t + i))
        for s, q in enumerate((26, 27, 28, 30, 31)):
            at[b + q].append((f"smp{s}", t))
    for h in range(4):
        b = 90 + 17 * h
        at[b - (6 if h else 3)].append(("hg_prep", h))
        at[b - 2].append(("hg_k", h))
        for l in range(8):
            at[b + l].append(("hg_factor", 8 * h + l))
            at[b + l + 1].append(("hg_level", 8 * h + l))
        at[b + 8].append(("hg_final", h))
        for s in range(6):
            at[b + 9 + s + (s > 3)].append((f"hg{s}", h))
    for j, q in enumerate((139, 150, NQ - 3)):
        at[q].append(("conv", j))
    return at


def build(nc, a, o):
    MIX = schedule()
    x1_rows = nc.dram_tensor("x1_rows", [T, D], F32, kind="Internal").ap()
    y_rows = nc.dram_tensor("y_rows", [2 * T, D], F32, kind="Internal").ap()

    base = (nc.sbuf_base + 63) // 64 * 64

    def sb(name, shape, dt, off):
        return nc.alloc_sbuf_tensor_at(name, shape, dt, offset=base + off)

    IDENT = sb("IDENT", [128, 128], F32, 0)
    ONES = sb("ONES", [128, 128], F32, 512)
    NDIST = sb("NDIST", [128, 256], F32, 1024)
    MASK = sb("MASK", [128, 8, 128], F16, 2048)
    NDS = sb("NDS", [64, 2, 128], F32, 4096)
    SM = sb("SM", [128, 512], F32, 5120)
    O_RING = 7168
    RAW = sb("RAW", [128, 2, 2048], F32, O_RING)
    HI = sb("HI", [128, 2, 2048], F32R, O_RING + 16384)
    LO = sb("LO", [128, 2, 2048], F32R, O_RING + 32768)
    O_XT = O_RING + 49152
    XH = sb("XH", [128, KC, T], F32R, O_XT)
    XL = sb("XL", [128, KC, T], F32R, O_XT + 33280)
    O_Y = O_XT + 66560
    Y = sb("Y", [128, KC, T], F32, O_Y)
    O_PR = O_Y + 33280
    PR = sb("PR", [128, 16, T], F32, O_PR)
    O_T = O_PR + 33280
    SC = sb("SC", [128, 4, 256], F32, O_T)
    PT = sb("PT", [128, 2, 4, 128], F32, O_T + 4096)
    VT = sb("VT", [128, 4, 128], F32, O_T + 8192)
    KCA = sb("KCA", [128, DB, 128], F32, O_T + 10240)
    VCA = sb("VCA", [128, DB, 128], F32, O_T + 14336)
    SELF = sb("SELF", [DB, 2, 128], F32, O_T + 18432)
    KTS = sb("KTS", [128, DB, 128], F32, O_T)
    SST = sb("SST", [128, 64], F32, O_T + 19456)
    SSR = sb("SSR", [64, 128], F32, O_T + 19712)
    PST = sb("PST", [128, 64], F32, O_T + 20224)
    PF = sb("PF", [128, SEQ], F32, O_T)
    SF = sb("SF", [128, SEQ], F32, O_T + 2048)
    AT = sb("AT", [128, 4, 128], F32, O_T + 4096)
    TMP = sb("TMP", [128, T], F32, O_T + 6144)
    VTK = sb("VTK", [128, 4, 128], F32, O_T + 8256)
    EF = sb("EF", [128, 2, T], F32, O_T + 10304)
    QF = sb("QF", [128, 2, T], F32, O_T + 14464)
    S0 = sb("S0", [128, DB, 128], F32, O_T + 18624)
    CVO = sb("CVO", [128, 4, 18], F32, O_T + 22720)
    R = sb("R", [TT, NT, D], F32, O_PR)
    NRT = 8
    NXD = 2
    RT = sb("RT", [128, NRT, T], F32, O_Y)
    LG = sb("LG", [TT, D], F32, O_Y + NRT * T * 4)
    LB = sb("LB", [TT, D], F32, O_Y + NRT * T * 4 + 8192)
    WR = sb("WR", [128, KC, 20], F32, 2048)
    GB1 = sb("GB1", [128, 2, KC], F32, 2048 + KC * 80)
    GW = sb("GW", [128, KC, 20], F32, 2048 + KC * 88)
    O_RT = O_PR + 40960
    rt = [O_RT]

    def small(name, shape, dt=F32):
        n = int(np.prod(shape[1:])) * 4
        off = rt[0]
        rt[0] += (n + 31) // 32 * 32
        return sb(name, shape, dt, off)

    NRAW, NHL = 6, 3
    RAWB = sb("RAWB", [128, NRAW, 2048], F32, O_RING)
    HIB = sb("HIB", [128, NHL, 2048], F32R, O_RING + 49152)
    LOB = sb("LOB", [128, NHL, 2048], F32R, O_RING + 73728)
    O_M = O_RING + 98304
    XG = sb("XG", [128, D], F32, O_M)
    XGH = sb("XGH", [128, KC, 128], F32R, O_M + 8192)
    XGL = sb("XGL", [128, KC, 128], F32R, O_M + 16384)
    YO = sb("YO", [128, D], F32, O_M + 24576)
    H = sb("H", [128, 512], F32, O_M + 32768)
    SG = sb("SG", [128, 512], F32, O_M + 34816)
    HTH = sb("HTH", [128, 4, 128], F32R, O_M + 36864)
    HTL = sb("HTL", [128, 4, 128], F32R, O_M + 38912)
    LG2 = sb("LG2", [TT, D], F32, O_RING)
    LB2 = sb("LB2", [TT, D], F32, O_RING + 8192)
    YA = sb("YA", [TT, NT, D], F32, O_RING + 49152)
    YB = sb("YB", [TT, NT, D], F32, O_RING + 49152 + NT * 8192)

    BANK = nc.alloc_psum_tensor("BANK", [128, 8, 512], F32)

    SINK = SM[:, 0:16]
    GAIN = SM[:, 16:17]
    LBP = SM[:, 20:24]
    LB0 = SM[:, 24:28]
    OML = SM[:, 28:32]
    LBT = SM[:, 32:36]
    EPS_LN = SM[:, 36:37]
    EPS_RMS = SM[:, 37:38]
    SINKC = SM[:, 38:40]
    CW = SM[:, 40:52]
    HIST = SM[:, 64:128].rearrange("p (j b r) -> p j b r", j=4, b=DB)
    MX = SM[:, 128:144].rearrange("p (k j) -> p k j", j=4)
    MXS = SM[:, 144:150]
    DEC = SM[:, 152:156]
    FS = [SM[:, 160:168], SM[:, 168:176]]
    ST = SM[:, 192:312].rearrange("p (i n s) -> p i n s", i=NT, n=4)
    MV = SM[:, 320:340].rearrange("p (i s) -> p i s", i=NT)

    with ExitStack() as ctx:
        def sem(name):
            return ctx.enter_context(nc.semaphore(name))

        s_const = sem("const_in")
        s_ones = sem("ones_set")
        s_x = [sem(f"x_in{g}") for g in range(8)]
        s_xh = sem("x_hi")
        s_xl = sem("x_lo")
        s_raw = [sem(f"weights_in{s}") for s in range(2)]
        s_hi = sem("weights_hi")
        s_lo = sem("weights_lo")
        s_lo0 = sem("first_weights_lo")
        s_acc = sem("proj_ready")
        s_pr = sem("proj_copied")
        s_grp = sem("group_done")
        s_act = sem("act_chain")
        s_dve = sem("dve_chain")
        s_vt_t = sem("v_turned")
        s_vt = sem("v_copied")
        s_sc = sem("scores_ready")
        s_mx = sem("max_ready")
        s_ex = sem("exp_ready")
        s_p = sem("probs_ready")
        s_tp = sem("probs_turned")
        s_pt = sem("probs_t_copied")
        s_pv = sem("pv_ready")
        s_yc = sem("pv_copied")
        s_kc = sem("cache_in")
        s_self = sem("self_rows_in")
        s_w_kv = sem("kv_states_out")
        s_m = [sem(f"sample_{n}") for n in ("kt", "kt_copied", "scores", "scores_copied", "turned", "max", "exp", "probs", "pt", "pt_copied", "out")]
        h_clamp = sem("hg_clamped")
        h_e = sem("hg_exp")
        h_f = sem("hg_f")
        h_g = sem("hg_logf")
        h_fac = sem("hg_factors_exp")
        h_mul = sem("hg_factors_ready")
        h_k = sem("hg_k_ready")
        h_gc = sem("hg_gate_clamped")
        h_ge = sem("hg_gate_exp")
        h_upd = sem("hg_sums_updated")
        h_lev = sem("hg_level_ready")
        h_acc = sem("hg_level_added")
        h_vt = sem("hg_v_turned")
        h_vtc = sem("hg_v_copied")
        h_fin = sem("hg_final_exp")
        h_ks = sem("hg_k_to_end")
        h_kt = sem("hg_k_turned")
        h_ktc = sem("hg_k_copied")
        h_u = sem("hg_u_ready")
        h_st = sem("hg_states_ready")
        h_s0 = sem("hg_state_in")
        h_vb = sem("hg_v_spread")
        h_sn = sem("hg_sample_states")
        h_o = sem("hg_out_ready")
        h_sq = sem("hg_squares")
        h_ss = sem("hg_square_sums")
        h_rt = sem("hg_root")
        h_out = sem("hg_states_out")
        c_out = sem("conv_states_out")
        s_yh = sem("mix_hi")
        s_yl = sem("mix_lo")
        s_r = [sem(f"residual_in{k}") for k in range(NRT)]
        s_ob = sem("out_ready")
        s_rt = sem("out_added")
        s_turn = sem("residual_turned")
        s_rcp = sem("residual_copied")
        s_gw = sem("router_scaled")
        s_lg = sem("ln1_in")
        s_wr = sem("router_in")
        s_var = sem("ln_var")
        s_sd = sem("ln_sd")
        s_rs = sem("ln_rstd")
        s_nrm = sem("ln_normed")
        s_nd = sem("ln_normed_last")
        s_x1g = sem("x1_gained")
        s_x1 = sem("x1_ready_pool")
        s_x1d = sem("x1_ready_dve")
        s_x1w = sem("x1_out")
        s_log = sem("logits_ready")
        s_rc = sem("route_consts")
        r_e = sem("route_exp_in")
        r_x = sem("route_exp")
        r_hot = sem("route_hot")
        r_rank = sem("route_rank")
        r_tab = sem("route_onehots")
        r_tabm = sem("route_table")
        r_tix = sem("route_tokens")
        r_idx = sem("route_indices")
        b_raw = [sem(f"expert_in{s}") for s in range(NRAW)]
        b_hi = sem("expert_hi")
        b_lo = [sem(f"expert_lo{s}") for s in range(NHL)]
        b_used = sem("expert_used")
        b_xg = sem("tokens_in")
        b_tx = sem("tokens_turned")
        b_ix = sem("gather_indices")
        b_iy = sem("scatter_indices")
        b_xh = sem("tokens_hi")
        b_xl = sem("tokens_lo")
        b_sg = sem("silu_ready")
        b_h = sem("h_ready")
        b_th = sem("h_turned")
        b_hh = sem("h_hi")
        b_hl = sem("h_lo")
        b_y = sem("down_copied")
        b_yw = sem("block_out")
        s_passed = sem("waits_passed")
        f_in = [sem(f"y_in{i}") for i in range(NT)]
        f_ln = sem("ln2_in")
        f_ab = sem("y_rows_added")
        f_g = sem("y_gained")
        f_st = sem("ln2_mean")
        f_sd = sem("ln2_sd")
        f_rs = sem("ln2_rstd")
        f_nm = sem("ln2_normed")
        f_y = sem("y_ready_pool")
        f_yd = sem("y_ready_dve")
        f_out = sem("y_out")

        TRI = small("TRI", [TT, TT])
        IOS = small("IOS", [TT, 128])
        THB = small("THB", [TT, MAXB + 2])
        IO24 = small("IO24", [TT, MAXB + 1])
        IO4 = small("IO4", [TT, 4])
        IO16 = small("IO16", [TT, 16])
        CUTS = small("CUTS", [TT, NT])
        VAL = small("VAL", [TT, 2, NT, 3])
        LIM = small("LIM", [128, 1])
        RB = small("RB", [TT, 20])
        LO_G = small("LO_G", [TT, NT, 20])
        T20 = small("T20", [TT, NT, 20])
        G4 = [small(f"G4_{k}", [TT, NT, 4]) for k in range(3)]
        EM, RK, SEL = (small(n, [TT, NT, 16]) for n in ("EM", "RK", "SEL"))
        HOT = small("HOT", [TT, 2, NT, 16])
        PM = small("PM", [TT, 2, NT, 16])
        GM, GS, DIF, V1, V2, TMIN = (small(n, [TT, NT]) for n in ("GM", "GS", "DIF", "V1", "V2", "TMIN"))
        CT = small("CT", [TT, 16, NT])
        PX = [small(f"PX{k}", [TT, 24]) for k in range(2)]
        POS = small("POS", [TT, 2, NT])
        NBK = small("NBK", [TT, 2 * NT])
        GE = small("GE", [TT, 2 * NT, MAXB + 2])
        ONE = small("ONE", [TT, 2 * NT, MAXB + 1])
        OH = sb("OH", [TT, 2, NT, 128], F32, O_M + 24576)
        TB = sb("TB", [TT, 2, NT, 3, MAXB + 1], F32, O_M + 24576 + 5120)
        TABF = small("TABF", [128, 3, MAXB + 1])
        TIX = small("TIX", [128, MAXB + 1], I32)
        YIX = small("YIX", [128, MAXB + 1], I32)
        TIXC = small("TIXC", [128, 1], I32)
        YIXC = small("YIXC", [128, 1], I32)
        EBC = small("EBC", [TT, MAXB + 1, 16])
        EBF = small("EBF", [TT, 32])
        EBI = small("EBI", [1, 32], I32)

        def used(eng, u):
            if u < NU:
                eng.wait_ge(s_acc, 2 * u + 2)
            else:
                eng.wait_ge(s_ob, 2 * (u - NU) + 2)

        block = ctx.enter_context(nc.Block())

        def acc(m):
            return BANK[:, m % 3, 0:HALF]

        MB = [BANK[:, 3 + k, :] for k in range(5)]

        def slot(u):
            return PR[:, u % 16, :]

        def passed(eng):
            eng.sem_inc(s_passed, 1)

        @block.sync
        def _(sp):
            def unit(u, w):
                if u >= 2:
                    sp.wait_ge(s_lo, u - 1)
                sp.dma_start(RAW[:, u % 2, :], w).then_inc(s_raw[u % 2], 16)

            xr = a["xT"].rearrange("p (g n) -> p g n", g=8)
            unit(0, a["w_in"][0])
            for g in range(8):
                sp.dma_start(Y[:, 2 * g:2 * g + 2, :], xr[:, g, :]).then_inc(s_x[g], 16)
            unit(1, a["w_in"][1])
            for t, s in ((IDENT, "ident"), (NDIST, "ndist"), (MASK, "mask"), (NDS, "nds")):
                sp.dma_start(t[:], a[s]).then_inc(s_const, 16)
            for t, s in ((SINK, "sink"), (SINKC[0:64, :], "sinkc"), (GAIN, "gain"), (LBP, "lbp"), (CW, "cw"), (SM[:, 64:128], "hist")):
                sp.dma_start(t, a[s]).then_inc(s_const, 16)
            kc = a["cache_k"].rearrange("b s n -> s b n")
            vc = a["cache_v"].rearrange("b s n -> s b n")

            def caches(t):
                if t:
                    sp.wait_ge(s_grp, t)
                    sp.wait_ge(s_w_kv, 64 * t)
                for dst, src in ((KCA, kc), (VCA, vc)):
                    sp.dma_start(dst[0:127, :, :], src[1:128, :, 128 * t:128 * t + 128]).then_inc(s_kc, 16)

            def att_setup(t):
                sp.wait_ge(s_vt, 2 * t + 2)
                sp.dma_start(KCA[127:128, :, :], SELF[:, 0, :]).then_inc(s_self, 16)
                sp.dma_start(VCA[127:128, :, :], SELF[:, 1, :]).then_inc(s_self, 16)
                k_slot = slot(ATT0[t])
                sp.dma_start(o["kp"][t], k_slot[:, SEQ - WIN:SEQ]).then_inc(s_w_kv, 16)
                sp.dma_start(o["vp"][t], VT[:, 3, :]).then_inc(s_w_kv, 16)

            def smp0(t):
                sp.wait_ge(s_kc, 32 * (t + 1))
                sp.wait_ge(s_self, 32 * (t + 1))
                sp.dma_start(o["ks"][t], KCA[:, :, :]).then_inc(s_w_kv, 16)
                sp.dma_start(o["vs"][t], VCA[:, :, :]).then_inc(s_w_kv, 16)

            def hg_states(h):
                if h:
                    sp.wait_ge(h_out, 32 * h)
                    sp.wait_ge(h_o, h)
                sp.dma_start(S0[:, :, :], a["s0"][h]).then_inc(h_s0, 16)

            def hg3(h):
                sp.wait_ge(h_st, h + 1)
                sp.dma_start(o["hp"][h], SF[:, 384:512]).then_inc(h_out, 16)
                sp.wait_ge(h_sn, 2 * h + 2)
                sp.dma_start(o["hs"][h], S0[:, :, :]).then_inc(h_out, 16)

            caches(0)
            for q in range(NQ):
                if q % 4 == 0 and q // 4 + 2 < NU:
                    unit(q // 4 + 2, a["w_in"][q // 4 + 2])
                for what, n in MIX[q]:
                    if what == "att_setup":
                        if n == 1:
                            caches(1)
                        att_setup(n)
                    elif what == "smp0":
                        smp0(n)
                    elif what == "hg_k":
                        if n == 0:
                            sp.wait_ge(s_grp, 2)
                            sp.wait_ge(s_w_kv, 128)
                        hg_states(n)
                    elif what == "hg3":
                        hg3(n)
            for k in range(2):
                unit(NU + k, a["w_out"][k])
            sp.wait_ge(s_grp, 10)
            sp.wait_ge(h_out, 128)
            sp.dma_start(o["cs"], CVO[:, :, :]).then_inc(c_out, 16)
            sp.wait_ge(c_out, 16)

            def residual(m):
                if m < NRT:
                    sp.wait_ge(s_yl, m + 1)
                else:
                    sp.wait_ge(s_log, (m - NRT) // 4 + 1)
                sp.dma_start(RT[:, m % NRT, :], a["xT"][:, T * m:T * m + T]).then_inc(s_r[m % NRT], 16)

            for m in range(4):
                residual(m)

            def bload(i, m0, w, j):
                s = (2 + i) % NRAW if m0 is not None else i % NRAW
                if m0 is None:
                    if i >= NRAW:
                        sp.wait_ge(b_lo[(i - NRAW) % NHL], (i - NRAW) // NHL + 1)
                else:
                    sp.wait_ge(b_lo[(2 + i) % NHL], (2 + i) // NHL + 1 + 4 * (j - 1))
                    passed(sp)
                sp.dma_start(RAWB[:, s, :], w).then_inc(b_raw[s], 16)

            for n in range(KC):
                if n + 2 < KC:
                    unit(NU + n + 2, a["w_out"][n + 2])
                if n + 4 < KC:
                    residual(n + 4)
                if n == 0:
                    sp.wait_ge(s_yl, KC)
                    sp.dma_start(WR[:, :, :], a["wr"]).then_inc(s_wr, 16)
                    sp.dma_start(GB1[:, :, :], a["gb1"]).then_inc(s_wr, 16)
                    sp.dma_start(LG[:, :], a["ln1g"]).then_inc(s_lg, 16)
                    sp.dma_start(LB[:, :], a["ln1b"]).then_inc(s_lg, 16)
                    for t, s in ((TRI, "tri"), (IOS, "ios"), (THB, "thb"), (IO24, "io24"), (IO4, "io4"), (IO16, "io16"), (CUTS, "cuts"), (VAL, "val"), (LIM, "lim"), (RB, "rb")):
                        sp.dma_start(t[:], a[s]).then_inc(s_rc, 16)
            sp.wait_ge(s_lo, NU + 16)
            for i in range(NRAW):
                if i == 2:
                    sp.wait_ge(s_ob, 2 * KC)
                bload(i, None, (a["w_gate"], a["w_up"])[i % 2][0, :, 2048 * (i // 2):2048 * (i // 2) + 2048], 0)
            for i in range(NT):
                if i >= NT - NXD:
                    sp.wait_ge(s_x1d, i - NT + NXD + 1)
                else:
                    sp.wait_ge(s_x1, i + 1)
                sp.dma_start(x1_rows[i * TT:(i + 1) * TT, :], R[:, i, :]).then_inc(s_x1w, 16)

            sp.wait_ge(b_yw, 16)
            for i in range(NRAW, 8):
                bload(i, None, (a["w_gate"], a["w_up"])[i % 2][0, :, 2048 * (i // 2):2048 * (i // 2) + 2048], 0)

            sp.wait_ge(r_idx, 1)
            nb = sp.value_load(EBI[0:1, 31:32], min_val=8, max_val=MAXB - 1) + 1

            def gate_up(j, m0):
                e = sp.value_load(EBI[0:1, bass.ds(j, 1)], min_val=0, max_val=NE - 1)
                for i in range(8):
                    bload(i, m0, (a["w_gate"], a["w_up"])[i % 2][bass.ds(e, 1), :, 2048 * (i // 2):2048 * (i // 2) + 2048].rearrange("a p n -> p (a n)"), j)

            def down(j, first):
                e = sp.value_load(EBI[0:1, bass.ds(j - 1, 1)], min_val=0, max_val=NE - 1)
                for n in range(4):
                    w = a["w_down"][bass.ds(e, 1), :, :, 512 * n:512 * n + 512].rearrange("a p c n -> p (a c) n")
                    i = first + n
                    s = (2 + i) % NRAW
                    sp.wait_ge(b_lo[(2 + i) % NHL], (2 + i) // NHL + 1 + 4 * (j - 1))
                    passed(sp)
                    sp.dma_start(RAWB[:, s, :].rearrange("p (c n) -> p c n", c=4), w).then_inc(b_raw[s], 16)

            with sp.Fori(1, MAXB) as j:
                with sp.If(j < nb):
                    gate_up(j, 0)
                    down(j, 8)
            down(nb, 0)

            sp.wait_ge(b_lo[2], 4 * nb)
            passed(sp)
            sp.dma_start(LG2[:, :], a["ln2g"]).then_inc(f_ln, 16)
            sp.dma_start(LB2[:, :], a["ln2b"]).then_inc(f_ln, 16)

            sp.wait_ge(b_used, 12 * nb)
            passed(sp)
            sp.wait_ge(b_xg, 16 * nb)
            passed(sp)
            sp.wait_ge(b_xl, 4 * nb + 4)
            passed(sp)
            sp.wait_ge(b_yw, 16 * nb + 16)
            passed(sp)
            for i in range(NT):
                for c, dst in ((0, YA), (1, YB)):
                    sp.dma_start(dst[:, i, :], y_rows[c * T + i * TT:c * T + (i + 1) * TT, :]).then_inc(f_in[i], 16)
            for i in (0, 1, 2, 4, 3):
                if i in (2, 3):
                    sp.wait_ge(f_y, i - 1)
                else:
                    sp.wait_ge(f_yd, 3 if i == 4 else i + 1)
                n = TT if i < NT - 1 else TT - DB
                sp.dma_start(o["yp"][i * TT:i * TT + n, :], R[0:n, i, :]).then_inc(f_out, 16)
            sp.dma_start(o["ys"], R[TT - DB:TT, NT - 1, :]).then_inc(f_out, 16)
            sp.wait_ge(f_out, 16 * (NT + 1))
            sp.wait_ge(s_w_kv, 128)
            sp.wait_ge(h_out, 128)
            sp.wait_ge(c_out, 16)

        @block.gpsimd
        def _(pool):
            def lo(u):
                pool.wait_ge(s_hi, u + 1)
                pool.tensor_tensor(LO[:, u % 2, :], RAW[:, u % 2, :], HI[:, u % 2, :].bitcast(F32), ALU.subtract).then_inc(s_lo, 1)

            pool.memset(ONES[:, :], 1.0).then_inc(s_ones, 1)
            pool.wait_ge(s_hi, 1)
            for k in range(4):
                cols = slice(512 * k, 512 * k + 512)
                pool.tensor_tensor(LO[:, 0, cols], RAW[:, 0, cols], HI[:, 0, cols].bitcast(F32), ALU.subtract).then_inc(s_lo if k == 3 else s_lo0, 1)
            for u in range(1, NU + 16):
                lo(u)

            pool.wait_ge(s_ob, 2 * KC)
            pool.memset(XG[:, :], 0.0).then_inc(s_ones, 1)
            pool.wait_ge(s_lg, 32)
            for i in range(NT - NXD):
                pool.wait_ge(s_nrm, i + 1)
                pool.tensor_tensor(R[:, i, :], R[:, i, :], LG[:, :], ALU.mult).then_inc(s_x1g, 1)
                pool.wait_ge(s_x1g, i + 1)
                pool.tensor_tensor(R[:, i, :], R[:, i, :], LB[:, :], ALU.add).then_inc(s_x1, 1)
            pool.wait_ge(s_ones, 2)
            last_token, last_row = pool.to_reg(T - 1), pool.to_reg(2 * T - 1)

            def gather(j, landed):
                pool.tensor_copy(TIXC[:, :], TIX[:, bass.ds(j, 1)]).then_inc(b_ix, 1)
                pool.wait_ge(b_ix, j + 1)
                passed(pool)
                pool.indirect_dma_start(
                    out=XG[:, :], out_offset=None, in_=x1_rows,
                    in_offset=bass.IndirectOffsetOnAxis(ap=TIXC[:, 0:1], axis=0),
                    bounds_check=last_token, oob_is_err=False).then_inc(landed, 16)

            def scatter(j):
                pool.wait_ge(b_y, 4 * j + 2)
                passed(pool)
                pool.tensor_copy(YIXC[:, :], YIX[:, bass.ds(j - 1, 1)]).then_inc(b_iy, 1)
                pool.wait_ge(b_iy, j)
                passed(pool)
                pool.indirect_dma_start(
                    out=y_rows, out_offset=bass.IndirectOffsetOnAxis(ap=YIXC[:, 0:1], axis=0),
                    in_=YO[:, :], in_offset=None,
                    bounds_check=last_row, oob_is_err=False).then_inc(b_yw, 16)

            pool.wait_ge(r_tix, 1)
            pool.wait_ge(s_x1w, 16 * NT)
            gather(0, b_yw)
            pool.wait_ge(r_idx, 1)
            nb = pool.value_load(EBI[0:1, 31:32], min_val=8, max_val=MAXB - 1) + 1
            pool.wait_ge(b_tx, 4)
            gather(1, b_xg)
            with pool.Fori(1, MAXB) as j:
                with pool.If(j < nb):
                    pool.wait_ge(b_tx, 4 * j + 4)
                    passed(pool)
                    gather(j + 1, b_xg)
                    scatter(j)
            scatter(nb)
            pool.wait_ge(b_xg, 16 * nb)
            passed(pool)
            for i in range(2, NT):
                pool.wait_ge(f_in[i], 32)
                pool.tensor_tensor(YA[:, i, :], YA[:, i, :], YB[:, i, :], ALU.add).then_inc(f_ab, 1)
            pool.wait_ge(f_ln, 32)
            for i in (2, 3):
                pool.wait_ge(f_g, i + 1)
                pool.tensor_tensor(R[:, i, :], R[:, i, :], LB2[:, :], ALU.add).then_inc(f_y, 1)

        @block.scalar
        def _(act):
            chain = [0]

            def done(ins):
                chain[0] += 1
                ins.then_inc(s_act, 1)
                act.wait_ge(s_act, chain[0])

            def hi(u):
                act.wait_ge(s_raw[u % 2], 16 * (u // 2 + 1))
                if u >= 2:
                    used(act, u - 2)
                act.activation(HI[:, u % 2, :], RAW[:, u % 2, :], ACT.Copy).then_inc(s_hi, 1)

            def copy_proj(m):
                u, hf = m // 2, m % 2
                act.wait_ge(s_acc, m + 1)
                if u >= 16 and hf == 0:
                    g = [0] * 6 + [1] * 6 + [2 + k // 4 for k in range(16)]
                    act.wait_ge(s_grp, g[u - 16] + 1)
                    if u - 16 in (0, 6):
                        act.wait_ge(s_w_kv, 64 * (1 + (u - 16) // 6))
                scale = 1.0
                if u in range(2, 6) or u in range(8, 12):
                    scale = HD ** -0.5
                if u in HG0:
                    scale = DK ** -0.5
                act.activation(PR[:, u % 16, hf * HALF:(hf + 1) * HALF], acc(m), ACT.Copy, scale=scale).then_inc(s_pr, 1)

            def att_setup(t):
                act.wait_ge(s_vt_t, 2 * t + 1)
                if t:
                    act.wait_ge(s_w_kv, 64 * t)
                act.activation(VT[:, :, :], MB[2].rearrange("p (c n) -> p c n", c=4), ACT.Copy).then_inc(s_vt, 1)
                act.wait_ge(s_vt_t, 2 * t + 2)
                act.activation(SELF[:, :, :], MB[3][0:DB, 0:256].rearrange("p (c n) -> p c n", c=2), ACT.Copy).then_inc(s_vt, 1)

            def att_scores(s):
                l, qb = STEPS[s % 8]
                k0 = 128 if qb == 0 else 0
                act.wait_ge(s_mx, s + 1)
                for j in range(4):
                    ins = act.activation(SC[:, j, k0:256], SC[:, j, k0:256], ACT.Exp, bias=MX[:, 1, j:j + 1],
                                         accum_out=MX[:, 3, j:j + 1])
                done(ins)
                act.activation(MX[:, 2, :], MX[:, 2, :], ACT.Exp).then_inc(s_ex, 1)

            def att_turn(s):
                l, qb = STEPS[s % 8]
                h0 = 1 if qb == 0 else 0
                act.wait_ge(s_tp, s + 1)
                if s >= 1:
                    act.wait_ge(s_pv, s)
                for k in range(h0, 2):
                    ins = act.activation(PT[:, k, :, :], MB[2 + k].rearrange("p (c n) -> p c n", c=4), ACT.Copy)
                ins.then_inc(s_pt, 1)

            def smp(s, t):
                if s == 0:
                    act.wait_ge(s_m[0], t + 1)
                    for k in range(2):
                        ins = act.activation(KTS[:, 4 * k:4 * k + 4, :], MB[2 + k].rearrange("p (c n) -> p c n", c=4), ACT.Copy)
                    ins.then_inc(s_m[1], 1)
                elif s == 1:
                    act.wait_ge(s_m[2], t + 1)
                    act.activation(SST[:, 0:32], MB[0][:, 0:32], ACT.Copy)
                    act.activation(SST[:, 32:64], MB[1][:, 0:32], ACT.Copy).then_inc(s_m[3], 1)
                elif s == 2:
                    act.wait_ge(s_m[5], t + 1)
                    done(act.activation(SSR[:, :], SSR[:, :], ACT.Exp, bias=MXS[0:64, 1:2], accum_out=MXS[0:64, 3:4]))
                    act.activation(MXS[0:64, 2:3], MXS[0:64, 2:3], ACT.Exp).then_inc(s_m[6], 1)
                elif s == 3:
                    act.wait_ge(s_m[8], t + 1)
                    act.activation(PST[:, :], MB[3][:, 0:64], ACT.Copy).then_inc(s_m[9], 1)

            def hg_prep(h):
                q0 = HG0[h]
                act.wait_ge(h_clamp, h + 1)
                f, g = slot(q0 + 1), slot(q0 + 3)
                act.activation(f, f, ACT.Exp, scale=-1.0).then_inc(h_e, 1)
                act.wait_ge(h_f, h + 1)
                if h:
                    act.wait_ge(h_u, h)
                act.activation(PF[:, :], f[:, 0:SEQ], ACT.Ln).then_inc(h_g, 1)

            def runs(tile, n):
                return tile.rearrange("p (b s n) -> p b s n", s=2, n=n)

            def hg_factor(x):
                h, l = x // 8, x % 8
                if l == 0:
                    return
                n = 1 << (l - 1)
                k = l % 2
                act.wait_ge(h_k, h + 1)
                if l >= 2:
                    act.wait_ge(h_upd, 7 * h + l - 1)
                if l >= 3:
                    act.wait_ge(h_lev, 8 * h + l - 1)
                e = runs(EF[:, k, 0:SEQ], n)
                act.activation(e[:, :, 1, :], runs(PF[:, :], n)[:, :, 1, :], ACT.Exp)
                act.activation(e[:, :, 0, :], runs(SF[:, :], n)[:, :, 0, :], ACT.Exp).then_inc(h_fac, 1)

            def hg_final(h):
                act.wait_ge(h_vt, h + 1)
                act.activation(VTK[:, :, :], MB[2].rearrange("p (c n) -> p c n", c=4), ACT.Copy).then_inc(h_vtc, 1)
                act.wait_ge(h_acc, 8 * h + 8)
                act.activation(EF[:, 0, 0:SEQ], PF[:, :], ACT.Exp)
                act.activation(EF[:, 1, 0:SEQ], SF[:, :], ACT.Exp).then_inc(h_fin, 1)

            def hg(s, h):
                if s == 1:
                    act.wait_ge(h_kt, h + 1)
                    act.activation(PF[:, :], MB[2], ACT.Copy).then_inc(h_ktc, 1)
                elif s == 3:
                    act.wait_ge(h_gc, h + 1)
                    act.activation(EF[:, 1, :], EF[:, 1, :], ACT.Exp, scale=-1.0).then_inc(h_ge, 1)
                elif s == 5:
                    act.wait_ge(h_ss, h + 1)
                    act.activation(QF[:, 1, 0:SEQ], MB[1], ACT.Sqrt, bias=EPS_RMS, scale=1.0 / DK)
                    act.activation(QF[:, 1, SEQ:T], MB[2][:, 0:DB], ACT.Sqrt, bias=EPS_RMS, scale=1.0 / DK).then_inc(h_rt, 1)

            hi(0)
            for g in range(8):
                act.wait_ge(s_x[g], 16)
                act.activation(XH[:, 2 * g:2 * g + 2, :], Y[:, 2 * g:2 * g + 2, :], ACT.Copy).then_inc(s_xh, 1)
            for q in range(NQ):
                if q % 2 == 0 and q >= 2:
                    copy_proj(q // 2 - 1)
                if q % 4 == 0 and q // 4 + 1 < NU:
                    hi(q // 4 + 1)
                for what, n in MIX[q]:
                    if what == "att_setup":
                        att_setup(n)
                    elif what == "att_scores":
                        att_scores(n)
                    elif what == "att_turn":
                        att_turn(n)
                    elif what.startswith("smp"):
                        smp(int(what[3:]), n)
                    elif what == "hg_prep":
                        hg_prep(n)
                    elif what == "hg_factor":
                        hg_factor(n)
                    elif what == "hg_final":
                        hg_final(n)
                    elif what in ("hg1", "hg3", "hg5"):
                        hg(int(what[2:]), n)
            hi(NU)
            copy_proj(2 * NU - 1)

            act.wait_ge(s_acc, 2 * NU)
            for c in range(KC):
                if c in (8, 12):
                    act.wait_ge(s_grp, 8 if c == 8 else 10)
                act.activation(XH[:, c, :], Y[:, c, :], ACT.Copy).then_inc(s_yh, 1)
            act.wait_ge(h_out, 128)

            def residual_copies(k):
                act.wait_ge(s_turn, 4 * k + 4)
                for i in range(NT):
                    act.activation(R[:, i, 512 * k:512 * k + 512], BANK[0:TT, 2 + i, :], ACT.Copy).then_inc(s_rcp, 1)

            for n in range(KC):
                if n + 1 < KC:
                    hi(NU + n + 1)
                if n % 4 == 0 and n:
                    residual_copies(n // 4 - 1)
            residual_copies(3)
            act.wait_ge(s_var, 1)
            act.activation(MV[0:TT, :, 2:3], MV[0:TT, :, 1:2], ACT.Sqrt, bias=EPS_LN[0:TT, :]).then_inc(s_sd, 1)
            act.wait_ge(s_rcp, 4 * NT)
            act.wait_ge(s_rs, 1)

            def normed(i):
                act.activation(R[:, i, :], R[:, i, :], ACT.Identity, scale=MV[0:TT, i, 2:3], bias=MV[0:TT, i, 3:4]).then_inc(s_nrm if i < NT - NXD else s_nd, 1)

            normed(0)
            normed(1)
            act.wait_ge(r_e, 1)
            act.activation(G4[1][:, :, :], G4[1][:, :, :], ACT.Exp).then_inc(r_x, 1)
            act.wait_ge(r_e, 2)
            act.activation(DIF[:, :], DIF[:, :], ACT.Exp).then_inc(r_x, 1)
            for i in range(2, NT):
                normed(i)

            def bhi(i, m0, j):
                s, r = (i % NHL, i % NRAW) if m0 is None else ((2 + i) % NHL, (2 + i) % NRAW)
                if m0 is None:
                    act.wait_ge(b_raw[r], 16 * (i // NRAW + 1))
                    if i >= NHL:
                        act.wait_ge(b_used, i - NHL + 1)
                else:
                    act.wait_ge(b_raw[r], 16 * ((8 + i) // NRAW + 1) + 32 * (j - 1))
                    act.wait_ge(b_used, 12 * j + i - 6)
                act.activation(HIB[:, s, :], RAWB[:, r, :], ACT.Copy).then_inc(b_hi, 1)

            for i in range(AHEAD):
                bhi(i, None, 0)

            act.wait_ge(r_idx, 1)
            nb = act.value_load(EBI[0:1, 31:32], min_val=8, max_val=MAXB - 1) + 1

            def silu(j):
                act.wait_ge(b_used, 12 * j + 4 if not isinstance(j, int) else 8)
                act.activation(SG[:, :], BANK[:, 0, :], ACT.Silu).then_inc(b_sg, 1)

            def token_hi(g, j):
                act.wait_ge(b_tx, 4 * j + g + 1)
                act.activation(XGH[:, 4 * g:4 * g + 4, :], BANK[:, 2 + g % 2, :].rearrange("p (c n) -> p c n", c=4), ACT.Copy).then_inc(b_xh, 1)

            def h_hi(j):
                act.wait_ge(b_th, j + 1)
                act.activation(HTH[:, :, :], BANK[:, 6, :].rearrange("p (c n) -> p c n", c=4), ACT.Copy).then_inc(b_hh, 1)

            def out_copy(n, i, j):
                act.wait_ge(b_used, 12 * j - 3 + i)
                act.activation(YO[:, 512 * n:512 * n + 512], BANK[:, 4 + n % 2, :], ACT.Copy).then_inc(b_y, 1)

            act.sem_inc(b_y, 2)
            for g in range(4):
                token_hi(g, 0)
            for i in range(AHEAD, 8):
                bhi(i, None, 0)
            silu(0)
            for g in range(4):
                token_hi(g, 1)
            for i in range(2):
                bhi(i, 0, 1)
            with act.Fori(1, MAXB) as j:
                with act.If(j < nb):
                    h_hi(j - 1)
                    for i in range(2, 10):
                        bhi(i, 0, j)
                    silu(j)
                    token_hi(0, j + 1)
                    bhi(10, 0, j)
                    act.wait_ge(b_yw, 16 * j)
                    out_copy(0, 8, j)
                    token_hi(1, j + 1)
                    bhi(11, 0, j)
                    out_copy(1, 9, j)
                    token_hi(2, j + 1)
                    bhi(0, 0, j + 1)
                    out_copy(2, 10, j)
                    token_hi(3, j + 1)
                    bhi(1, 0, j + 1)
                    out_copy(3, 11, j)
            h_hi(nb - 1)
            bhi(2, 0, nb)
            act.wait_ge(b_yw, 16 * nb)
            out_copy(0, 0, nb)
            bhi(3, 0, nb)
            for n in range(1, 4):
                out_copy(n, n, nb)

            for i in range(NT):
                act.wait_ge(f_st, i + 1)
                done(act.activation(YA[:, i, :], R[:, i, :], ACT.Square, bias=MV[0:TT, i, 0:1], accum_out=MV[0:TT, i, 1:2]))
                act.activation(MV[0:TT, i, 2:3], MV[0:TT, i, 1:2], ACT.Sqrt, bias=EPS_LN[0:TT, :], scale=1.0 / D).then_inc(f_sd, 1)
                act.wait_ge(f_rs, i + 1)
                act.activation(R[:, i, :], R[:, i, :], ACT.Identity, scale=MV[0:TT, i, 2:3], bias=MV[0:TT, i, 3:4]).then_inc(f_nm, 1)

        @block.vector
        def _(dve):
            chain = [0]

            def done(ins):
                chain[0] += 1
                ins.then_inc(s_dve, 1)
                dve.wait_ge(s_dve, chain[0])

            dve.memset(EPS_LN, LN_EPS)
            dve.memset(EPS_RMS, RMS_EPS)
            for g in range(8):
                dve.wait_ge(s_xh, g + 1)
                dve.tensor_tensor(XL[:, 2 * g:2 * g + 2, :], Y[:, 2 * g:2 * g + 2, :], XH[:, 2 * g:2 * g + 2, :].bitcast(F32), ALU.subtract).then_inc(s_xl, 1)
            dve.wait_ge(s_const, 160)
            done(dve.tensor_tensor(LBT, LBP, LBP, ALU.subtract))
            done(dve.tensor_scalar(LBT, LBT, 1.0, None, ALU.add))
            done(dve.reciprocal(OML, LBT))
            done(dve.tensor_tensor(LBT, LBT, OML, ALU.mult))
            done(dve.tensor_tensor(LB0, LBT, LBT, ALU.subtract))
            done(dve.tensor_scalar(OML, LB0, -1.0, 1.0, ALU.mult, ALU.add))

            def att_scores(s):
                t, (l, qb) = s // 8, STEPS[s % 8]
                k0 = 128 if qb == 0 else 0
                dve.wait_ge(s_sc, s + 1)
                if s >= 1:
                    dve.wait_ge(s_tp, s)
                for j in range(4):
                    h = 8 * t + 4 * l + j
                    src = MB[j // 2].rearrange("p (c n) -> p c n", c=2)[:, j % 2, k0:256]
                    ins = dve.scalar_tensor_tensor(SC[:, j, k0:256], NDIST[:, k0:256], SLOPE[h], src, ALU.mult, ALU.add)
                done(ins)
                done(dve.tensor_reduce(MX[:, 0, :], SC[:, :, k0:256], AX.X, ALU.max))
                sk = SINK[:, 8 * t + 4 * l:8 * t + 4 * l + 4]
                done(dve.tensor_tensor(MX[:, 0, :], MX[:, 0, :], sk, ALU.max))
                dve.tensor_scalar(MX[:, 1, :], MX[:, 0, :], -1.0, None, ALU.mult)
                dve.tensor_tensor(MX[:, 2, :], sk, MX[:, 0, :], ALU.subtract).then_inc(s_mx, 1)
                dve.wait_ge(s_ex, s + 1)
                done(dve.tensor_tensor(MX[:, 3, :], MX[:, 3, :], MX[:, 2, :], ALU.add))
                done(dve.reciprocal(MX[:, 3, :], MX[:, 3, :]))
                for j in range(4):
                    ins = dve.tensor_scalar(SC[:, j, k0:256], SC[:, j, k0:256], MX[:, 3, j:j + 1], None, ALU.mult)
                ins.then_inc(s_p, 1)

            def att_pv(s):
                t, (l, qb) = s // 8, STEPS[s % 8]
                dve.wait_ge(s_pv, s + 1)
                b = 64 * l
                dve.tensor_copy(Y[b:b + 64, 4 * t:4 * t + 4, 128 * qb:128 * qb + 128],
                                MB[4][b:b + 64, :].rearrange("p (c n) -> p c n", c=4)).then_inc(s_yc, 1)

            def smp(s, t):
                if s == 2:
                    dve.wait_ge(s_m[4], t + 1)
                    done(dve.tensor_tensor(SSR[:, :], MB[1][0:64, 0:128], NDS[:, t, :], ALU.add))
                    done(dve.tensor_reduce(MXS[0:64, 0:1], SSR[:, :], AX.X, ALU.max))
                    sk = SINKC[0:64, t:t + 1]
                    done(dve.tensor_tensor(MXS[0:64, 0:1], MXS[0:64, 0:1], sk, ALU.max))
                    dve.tensor_scalar(MXS[0:64, 1:2], MXS[0:64, 0:1], -1.0, None, ALU.mult)
                    dve.tensor_tensor(MXS[0:64, 2:3], sk, MXS[0:64, 0:1], ALU.subtract).then_inc(s_m[5], 1)
                    dve.wait_ge(s_m[6], t + 1)
                    done(dve.tensor_tensor(MXS[0:64, 3:4], MXS[0:64, 3:4], MXS[0:64, 2:3], ALU.add))
                    done(dve.reciprocal(MXS[0:64, 3:4], MXS[0:64, 3:4]))
                    dve.tensor_scalar(SSR[:, :], SSR[:, :], MXS[0:64, 3:4], None, ALU.mult).then_inc(s_m[7], 1)
                elif s == 4:
                    dve.wait_ge(s_m[10], t + 1)
                    dve.tensor_copy(Y[:, 4 * t:4 * t + 4, SEQ:T],
                                    MB[4][:, 0:32].rearrange("p (b g) -> p g b", b=DB)).then_inc(s_grp, 1)

            def hg_prep(h):
                q0 = HG0[h]
                f = slot(q0 + 1)
                dve.wait_ge(s_pr, 2 * q0 + 8)
                if h == 0:
                    dve.wait_ge(s_w_kv, 128)
                dve.tensor_scalar(f, f, -44.0, None, ALU.max).then_inc(h_clamp, 1)
                dve.wait_ge(h_e, h + 1)
                done(dve.tensor_scalar(f, f, 1.0, None, ALU.add))
                done(dve.reciprocal(f, f))
                done(dve.tensor_scalar(f, f, OML[:, h:h + 1], LB0[:, h:h + 1], ALU.mult, ALU.add))
                dve.tensor_copy(FS[h % 2], f[:, SEQ:T]).then_inc(h_f, 1)

            def hg_k(h):
                f = slot(HG0[h] + 1)
                if h:
                    dve.wait_ge(h_out, 32 * h)
                done(dve.memset(SF[:, :], 0.0))
                dve.wait_ge(h_g, h + 1)
                dve.tensor_scalar(f, f, -1.0, 1.0, ALU.mult, ALU.add).then_inc(h_k, 1)

            def runs(tile, n):
                return tile.rearrange("p (b s n) -> p b s n", s=2, n=n)

            def hg_factor(x):
                h, l = x // 8, x % 8
                q, k = slot(HG0[h]), slot(HG0[h] + 1)
                if l == 0:
                    return
                z = l % 2
                dve.wait_ge(h_fac, 7 * h + l)
                if l >= 3:
                    dve.wait_ge(h_lev, 8 * h + l - 1)
                n = 1 << (l - 1)
                w, e = runs(QF[:, z, 0:SEQ], n), runs(EF[:, z, 0:SEQ], n)
                dve.tensor_tensor(w[:, :, 1, :], runs(q[:, 0:SEQ], n)[:, :, 1, :], e[:, :, 1, :], ALU.mult)
                dve.tensor_tensor(w[:, :, 0, :], runs(k[:, 0:SEQ], n)[:, :, 0, :], e[:, :, 0, :], ALU.mult).then_inc(h_mul, 1)
                p, s = runs(PF[:, :], n), runs(SF[:, :], n)
                nb = SEQ // (2 * n)
                done(dve.tensor_tensor(s[:, :, 0, :], s[:, :, 0, :], p[:, :, 1, n - 1:n].to_broadcast([128, nb, n]), ALU.add))
                ins = dve.tensor_tensor(p[:, :, 1, :], p[:, :, 1, :], p[:, :, 0, n - 1:n].to_broadcast([128, nb, n]), ALU.add)
                ins.then_inc(h_upd, 1)

            def hg_level(x):
                h, l = x // 8, x % 8
                dve.wait_ge(h_lev, 8 * h + l + 1)
                if l == 0:
                    m = MASK[:, l:l + 1, :].to_broadcast([128, 4, 128])
                    dve.tensor_tensor(AT[:, :, :], MB[0].rearrange("p (c n) -> p c n", c=4), m, ALU.mult).then_inc(h_acc, 1)
                else:
                    n = 1 << (l - 1)
                    m = runs(MASK[:, l, :], n)[:, :, 1, :].unsqueeze(1).to_broadcast([128, 4, 64 // n, n])
                    t4 = TMP[:, 0:256].rearrange("p (c b n) -> p c b n", c=4, n=n)
                    done(dve.tensor_tensor(t4, MB[l % 2][:, 0:256].rearrange("p (c b n) -> p c b n", c=4, n=n), m, ALU.mult))
                    at = runs(AT[:, :, :].rearrange("p c n -> p (c n)"), n)[:, :, 1, :]
                    dve.tensor_tensor(at, at, TMP[:, 0:256].rearrange("p (b n) -> p b n", n=n), ALU.add).then_inc(h_acc, 1)

            def hg(s, h):
                q0 = HG0[h]
                q, k, v, g = (slot(q0 + c) for c in range(4))
                if s == 0:
                    dve.wait_ge(h_fin, h + 1)
                    dve.tensor_copy(DEC, EF[:, 0, 127:SEQ:128])
                    dve.tensor_tensor(QF[:, 0, 0:SEQ], q[:, 0:SEQ], EF[:, 0, 0:SEQ], ALU.mult)
                    dve.tensor_tensor(EF[:, 1, 0:SEQ], k[:, 0:SEQ], EF[:, 1, 0:SEQ], ALU.mult).then_inc(h_ks, 1)
                elif s in (1, 2):
                    c = s - 1
                    if c == 0:
                        dve.wait_ge(h_s0, 16 * (h + 1))
                    b0 = 4 * c
                    st = S0[:, b0:b0 + 4, :]
                    dve.wait_ge(h_vb, 2 * h + c + 1)
                    t4 = TMP[:, 0:SEQ].rearrange("p (c n) -> p c n", c=4)
                    dve.tensor_tensor(t4, MB[4].rearrange("p (c n) -> p c n", c=4),
                                      k[:, SEQ + b0:SEQ + b0 + 4].unsqueeze(2).to_broadcast([128, 4, 128]), ALU.mult)
                    done(dve.tensor_tensor(st, st, FS[h % 2][:, b0:b0 + 4].unsqueeze(2).to_broadcast([128, 4, 128]), ALU.mult))
                    dve.tensor_tensor(st, st, t4, ALU.add).then_inc(h_sn, 1)
                elif s == 3:
                    dve.wait_ge(h_kt, h + 1)
                    dve.tensor_scalar(EF[:, 1, :], g, -80.0, None, ALU.max).then_inc(h_gc, 1)
                    dve.wait_ge(h_u, h + 1)
                    done(dve.tensor_copy(SF[:, 0:128], MB[3][:, 0:128]))
                    for c in range(1, 4):
                        ins = dve.scalar_tensor_tensor(SF[:, 128 * c:128 * c + 128], SF[:, 128 * c - 128:128 * c], DEC[:, c:c + 1],
                                                       MB[3][:, 128 * c:128 * c + 128], ALU.mult, ALU.add)
                        if c < 3:
                            done(ins)
                    ins.then_inc(h_st, 1)
                elif s == 4:
                    dve.wait_ge(h_o, h + 1)
                    dve.tensor_copy(TMP[:, 0:SEQ], MB[0])
                    done(dve.tensor_copy(TMP[:, SEQ:T], MB[4][:, 0:DB]))
                    dve.tensor_tensor(EF[:, 0, :], TMP[:, :], TMP[:, :], ALU.mult).then_inc(h_sq, 1)
                    dve.wait_ge(h_ge, h + 1)
                    done(dve.tensor_scalar(EF[:, 1, :], EF[:, 1, :], 1.0, None, ALU.add))
                    done(dve.reciprocal(EF[:, 1, :], EF[:, 1, :]))
                    done(dve.scalar_tensor_tensor(g, g, GAIN, EF[:, 1, :], ALU.mult, ALU.mult))
                elif s == 5:
                    dve.wait_ge(h_rt, h + 1)
                    done(dve.reciprocal(QF[:, 1, :], QF[:, 1, :]))
                    done(dve.tensor_tensor(TMP[:, :], TMP[:, :], QF[:, 1, :], ALU.mult))
                    dve.tensor_tensor(Y[:, 8 + h, :], TMP[:, :], g, ALU.mult).then_inc(s_grp, 1)

            def conv(j):
                cc, ch, cb = (slot(CV0[j] + k) for k in range(3))
                dve.wait_ge(s_pr, 2 * CV0[j] + 6)
                y = Y[:, 12 + j, :]
                w = [CW[:, 3 * j + k:3 * j + k + 1] for k in range(3)]
                done(dve.tensor_tensor(cc, cc, ch, ALU.mult))
                dve.tensor_copy(CVO[:, j, 0:2], cc[:, SEQ - 2:SEQ])
                so = CVO[:, j, 2:18].rearrange("p (b r) -> p b r", r=2)
                dve.tensor_copy(so[:, :, 0], HIST[:, j, :, 1])
                dve.tensor_copy(so[:, :, 1], cc[:, SEQ:T])
                done(dve.tensor_scalar(y, cc, w[2], None, ALU.mult))
                dve.scalar_tensor_tensor(y[:, 1:SEQ], cc[:, 0:SEQ - 1], w[1], y[:, 1:SEQ], ALU.mult, ALU.add)
                done(dve.scalar_tensor_tensor(y[:, SEQ:T], HIST[:, j, :, 1], w[1], y[:, SEQ:T], ALU.mult, ALU.add))
                dve.scalar_tensor_tensor(y[:, 2:SEQ], cc[:, 0:SEQ - 2], w[0], y[:, 2:SEQ], ALU.mult, ALU.add)
                done(dve.scalar_tensor_tensor(y[:, SEQ:T], HIST[:, j, :, 0], w[0], y[:, SEQ:T], ALU.mult, ALU.add))
                dve.tensor_tensor(y, y, cb, ALU.mult).then_inc(s_grp, 1)

            for q in range(NQ):
                for what, n in MIX[q]:
                    if what == "att_scores":
                        att_scores(n)
                    elif what == "att_pv":
                        att_pv(n)
                    elif what.startswith("smp"):
                        smp(int(what[3:]), n)
                    elif what == "hg_prep":
                        hg_prep(n)
                    elif what == "hg_k":
                        hg_k(n)
                    elif what == "hg_factor":
                        hg_factor(n)
                    elif what == "hg_level":
                        hg_level(n)
                    elif what in ("hg0", "hg1", "hg2", "hg3", "hg4", "hg5"):
                        hg(int(what[2:]), n)
                    elif what == "conv":
                        conv(n)
            for c in range(KC):
                if c == 2:
                    conv(3)
                dve.wait_ge(s_yh, c + 1)
                dve.tensor_tensor(XL[:, c, :], Y[:, c, :], XH[:, c, :].bitcast(F32), ALU.subtract).then_inc(s_yl, 1)

            def column_stats(k):
                for i in range(NT):
                    dve.wait_ge(s_rcp, NT * k + i + 1)
                    ins = dve.bn_stats(ST[0:TT, i, k, :], R[:, i, 512 * k:512 * k + 512])
                return ins

            for n in range(KC):
                for hf in range(2):
                    m = 2 * n + hf
                    dve.wait_ge(s_ob, m + 1)
                    if hf == 0:
                        dve.wait_ge(s_r[n % NRT], 16 * (n // NRT + 1))
                    r = RT[:, n % NRT, hf * HALF:(hf + 1) * HALF]
                    dve.scalar_tensor_tensor(r, r, ALPHA, BANK[:, m % 2, 0:HALF], ALU.mult, ALU.add).then_inc(s_rt, 1)
                    if hf == 0 and n % 4 == 0 and n:
                        column_stats(n // 4 - 1)
                if n == 0:
                    dve.wait_ge(s_wr, 32)
                    done(dve.tensor_tensor(GW[:, :, :], WR[:, :, :], GB1[:, 0, :].unsqueeze(2).to_broadcast([128, KC, 20]), ALU.mult))
                    dve.tensor_tensor(WR[:, :, :], WR[:, :, :], GB1[:, 1, :].unsqueeze(2).to_broadcast([128, KC, 20]), ALU.mult).then_inc(s_gw, 1)
            done(column_stats(3))
            for i in range(NT):
                ins = dve.bn_aggr(MV[0:TT, i, 0:2], ST[0:TT, i, :, :].rearrange("p n s -> p (n s)"))
            ins.then_inc(s_var, 1)

            dve.wait_ge(s_log, 4)
            dve.wait_ge(s_rc, 160)
            tt, ts = dve.tensor_tensor, dve.tensor_scalar

            def bc(x, *shape):
                return x.to_broadcast(list(shape))

            def col(x):
                return x[:, :].unsqueeze(2)

            done(tt(RB[:, :], RB[:, :], BANK[0:TT, 7, 420:440], ALU.add))
            done(dve.tensor_reduce(LO_G[:, :, :].rearrange("p i n -> p (i n)"), BANK[0:TT, 7, 0:400].rearrange("p (k x) -> p x k", k=4), AX.X, ALU.add))
            dve.wait_ge(s_var, 1)
            done(tt(T20[:, :, :], bc(BANK[0:TT, 7, 400:420].unsqueeze(1), TT, NT, 20), bc(MV[0:TT, :, 0:1], TT, NT, 20), ALU.mult))
            done(tt(LO_G[:, :, :], LO_G[:, :, :], T20[:, :, :], ALU.subtract))
            dve.wait_ge(s_sd, 1)
            done(dve.reciprocal(MV[0:TT, :, 2:3], MV[0:TT, :, 2:3]))
            dve.scalar_tensor_tensor(MV[0:TT, :, 3:4], MV[0:TT, :, 0:1], -1.0, MV[0:TT, :, 2:3], ALU.mult, ALU.mult).then_inc(s_rs, 1)
            done(tt(LO_G[:, :, :], LO_G[:, :, :], bc(MV[0:TT, :, 2:3], TT, NT, 20), ALU.mult))
            done(tt(LO_G[:, :, :], LO_G[:, :, :], bc(RB[:, :].unsqueeze(1), TT, NT, 20), ALU.add))
            gl, el = LO_G[:, :, 0:4], LO_G[:, :, 4:20]
            done(dve.tensor_reduce(GM[:, :], gl, AX.X, ALU.max))
            done(tt(G4[0][:, :, :], gl, bc(col(GM), TT, NT, 4), ALU.is_equal))
            tt(G4[1][:, :, :], gl, bc(col(GM), TT, NT, 4), ALU.subtract).then_inc(r_e, 1)

            def first(hot, iota, n):
                io = bc(iota[:, :].unsqueeze(1), TT, NT, n)
                done(tt(hot, io, hot, ALU.mult))
                done(dve.tensor_reduce(TMIN[:, :], hot, AX.X, ALU.min))
                done(tt(hot, io, bc(col(TMIN), TT, NT, n), ALU.is_equal))

            first(G4[0][:, :, :], IO4, 4)
            hot1, hot2 = HOT[:, 0], HOT[:, 1]
            done(ts(G4[2][:, :, :], G4[0][:, :, :], 0.5, -NEG, ALU.subtract, ALU.mult))
            done(tt(EM[:, :, :].rearrange("p i (g e) -> p i g e", g=4), el.rearrange("p i (g e) -> p i g e", g=4),
                    G4[2][:, :, :].unsqueeze(3).to_broadcast([TT, NT, 4, 4]), ALU.min))
            done(dve.tensor_reduce(V1[:, :], EM[:, :, :], AX.X, ALU.max))
            done(tt(hot1, EM[:, :, :], bc(col(V1), TT, NT, 16), ALU.is_equal))
            first(hot1, IO16, 16)
            done(dve.scalar_tensor_tensor(EM[:, :, :], hot1, NEG, EM[:, :, :], ALU.mult, ALU.add))
            done(dve.tensor_reduce(V2[:, :], EM[:, :, :], AX.X, ALU.max))
            done(tt(hot2, EM[:, :, :], bc(col(V2), TT, NT, 16), ALU.is_equal))
            first(hot2, IO16, 16)
            tt(RK[:, :, :], hot1, hot2, ALU.add).then_inc(r_hot, 1)
            tt(DIF[:, :], V2[:, :], V1[:, :], ALU.subtract).then_inc(r_e, 1)
            dve.memset(PX[0][:, 0:8], 0.0)
            dve.memset(PX[1][:, 0:8], 0.0)
            done(dve.memset(EBF[:, :], 0.0))
            dve.wait_ge(r_rank, 1)
            before = BANK[0:TT, 0, 0:80].rearrange("p (i e) -> p i e", i=NT)
            done(tt(CT[:, :, :], bc(BANK[0:TT, 1, 0:16].unsqueeze(2), TT, 16, NT), bc(CUTS[:, :].unsqueeze(1), TT, 16, NT), ALU.is_ge))
            done(dve.tensor_reduce(PX[0][:, 8:24], CT[:, :, :], AX.X, ALU.add))
            done(ts(PX[0][:, 8:9], PX[0][:, 8:9], 1.0, None, ALU.max))
            for k in range(4):
                n = 1 << k
                done(tt(PX[1 - k % 2][:, 8:24], PX[k % 2][:, 8:24], PX[k % 2][:, 8 - n:24 - n], ALU.add))
            bstart = PX[0][:, 7:23]
            done(dve.scalar_tensor_tensor(SEL[:, :, :], bc(bstart.unsqueeze(1), TT, NT, 16), float(CAP), before, ALU.mult, ALU.add))
            done(tt(PM[:, :, :, :], HOT[:, :, :, :], SEL[:, :, :].unsqueeze(1).to_broadcast([TT, 2, NT, 16]), ALU.mult))
            pos = POS[:, :, :].rearrange("p c i -> p (c i)")
            done(dve.tensor_reduce(pos, PM[:, :, :, :].rearrange("p c i e -> p (c i) e"), AX.X, ALU.add))
            done(tt(GE[:, :, :], bc(pos.unsqueeze(2), TT, 2 * NT, MAXB + 2), bc(THB[:, :].unsqueeze(1), TT, 2 * NT, MAXB + 2), ALU.is_ge))
            tt(ONE[:, :, :], GE[:, :, 0:MAXB + 1], GE[:, :, 1:MAXB + 2], ALU.subtract)
            done(dve.tensor_reduce(NBK[:, :], GE[:, :, :], AX.X, ALU.add))
            dve.wait_ge(r_x, 2)
            done(dve.tensor_reduce(GS[:, :], G4[1][:, :, :], AX.X, ALU.add))
            dve.scalar_tensor_tensor(pos, NBK[:, :], -float(CAP), pos, ALU.mult, ALU.add)
            done(dve.scalar_tensor_tensor(GS[:, :], DIF[:, :], 1.0, GS[:, :], ALU.add, ALU.mult))
            done(dve.reciprocal(GS[:, :], GS[:, :]))
            dve.tensor_copy(VAL[:, 0, :, 1], GS[:, :])
            done(tt(VAL[:, 1, :, 1], GS[:, :], DIF[:, :], ALU.mult))
            tt(TB[:, :, :, :, :].rearrange("p c i k j -> p (c i) k j"), ONE[:, :, :].unsqueeze(2).to_broadcast([TT, 2 * NT, 3, MAXB + 1]),
               VAL[:, :, :, :].rearrange("p c i k -> p (c i) k").unsqueeze(3).to_broadcast([TT, 2 * NT, 3, MAXB + 1]), ALU.mult)
            tt(OH[:, :, :, :].rearrange("p c i n -> p (c i) n"), bc(IOS[:, :].unsqueeze(1), TT, 2 * NT, 128), bc(pos.unsqueeze(2), TT, 2 * NT, 128),
               ALU.is_equal).then_inc(r_tab, 1)
            dve.wait_ge(s_lg, 32)
            for i in range(NT - NXD, NT):
                dve.wait_ge(s_nd, i - NT + NXD + 1)
                done(tt(R[:, i, :], R[:, i, :], LG[:, :], ALU.mult))
                tt(R[:, i, :], R[:, i, :], LB[:, :], ALU.add).then_inc(s_x1d, 1)
            dve.wait_ge(r_tabm, 1)
            tab = BANK[:, 2, 0:3 * (MAXB + 1)].rearrange("p (k j) -> p k j", k=3)
            ts(TIX[:, :], tab[:, 0, :], SKIP, LIM[:, 0:1], ALU.add, ALU.min).then_inc(r_tix, 1)
            ts(YIX[:, :], tab[:, 2, :], SKIP, None, ALU.add)
            dve.tensor_copy(TABF[:, :, :], tab)
            done(tt(EBC[:, :, :], bc(bstart.unsqueeze(1), TT, MAXB + 1, 16), bc(IO24[:, :].unsqueeze(2), TT, MAXB + 1, 16), ALU.is_le))
            done(dve.tensor_reduce(EBF[:, 0:MAXB + 1], EBC[:, :, :], AX.X, ALU.add))
            ts(EBF[:, 31:32], PX[0][:, 23:24], -1.0, None, ALU.add)
            done(ts(EBF[:, 0:MAXB + 1], EBF[:, 0:MAXB + 1], -1.0, None, ALU.add))
            done(dve.tensor_copy(EBI[:, :], EBF[0:1, :]))
            dve.sem_inc(r_idx, 1)

            dve.wait_ge(r_idx, 1)
            nb = dve.value_load(EBI[0:1, 31:32], min_val=8, max_val=MAXB - 1) + 1

            def blo(i, m0, j):
                s, r = (i % NHL, i % NRAW) if m0 is None else ((2 + i) % NHL, (2 + i) % NRAW)
                dve.wait_ge(b_hi, i + 1 if m0 is None else 12 * j + i - 3)
                dve.tensor_tensor(LOB[:, s, :], RAWB[:, r, :], HIB[:, s, :].bitcast(F32), ALU.subtract).then_inc(b_lo[s], 1)

            def h_made(j):
                dve.wait_ge(b_sg, j + 1)
                if not isinstance(j, int) or j >= 1:
                    dve.wait_ge(b_th, j)
                dve.scalar_tensor_tensor(H[:, :], SG[:, :], TABF[:, 1, bass.ds(j, 1)], BANK[:, 1, :], ALU.mult, ALU.mult).then_inc(b_h, 1)

            def token_lo(g, j):
                dve.wait_ge(b_xh, 4 * j + g + 1)
                dve.tensor_tensor(XGL[:, 4 * g:4 * g + 4, :], BANK[:, 2 + g % 2, :].rearrange("p (c n) -> p c n", c=4),
                                  XGH[:, 4 * g:4 * g + 4, :].bitcast(F32), ALU.subtract).then_inc(b_xl, 1)

            def h_lo(j):
                dve.wait_ge(b_hh, j + 1)
                dve.tensor_tensor(HTL[:, :, :], BANK[:, 6, :].rearrange("p (c n) -> p c n", c=4), HTH[:, :, :].bitcast(F32),
                                  ALU.subtract).then_inc(b_hl, 1)

            for i in range(AHEAD):
                blo(i, None, 0)
            for g in range(4):
                token_lo(g, 0)
            for i in range(AHEAD, 8):
                blo(i, None, 0)
            h_made(0)
            for g in range(4):
                token_lo(g, 1)
            for i in range(2):
                blo(i, 0, 1)
            with dve.Fori(1, MAXB) as j:
                with dve.If(j < nb):
                    h_lo(j - 1)
                    for i in range(2, 10):
                        blo(i, 0, j)
                    h_made(j)
                    token_lo(0, j + 1)
                    blo(10, 0, j)
                    token_lo(1, j + 1)
                    blo(11, 0, j)
                    token_lo(2, j + 1)
                    blo(0, 0, j + 1)
                    token_lo(3, j + 1)
                    blo(1, 0, j + 1)
            h_lo(nb - 1)
            for n in range(2, 4):
                blo(n, 0, nb)

            mu, sd, sq = (lambda i: MV[0:TT, i, 0:1]), (lambda i: MV[0:TT, i, 2:3]), (lambda i: MV[0:TT, i, 3:4])

            def rows_added(i):
                dve.wait_ge(f_in[i], 32)
                done(tt(YA[:, i, :], YA[:, i, :], YB[:, i, :], ALU.add))

            def added(i):
                if i >= 2:
                    dve.wait_ge(f_ab, i - 1)
                r = R[:, i, :]
                done(dve.scalar_tensor_tensor(r, r, ALPHA, YA[:, i, :], ALU.mult, ALU.add, accum_out=sq(i)))
                dve.tensor_scalar(mu(i), sq(i), -1.0 / D, None, ALU.mult).then_inc(f_st, 1)

            def rstd(i):
                dve.wait_ge(f_sd, i + 1)
                done(dve.reciprocal(sd(i), sd(i)))
                dve.tensor_tensor(sq(i), mu(i), sd(i), ALU.mult).then_inc(f_rs, 1)

            def gained(i):
                dve.wait_ge(f_nm, i + 1)
                return tt(R[:, i, :], R[:, i, :], LG2[:, :], ALU.mult).then_inc(f_g, 1)

            def shifted(i):
                dve.wait_ge(f_g, i + 1)
                tt(R[:, i, :], R[:, i, :], LB2[:, :], ALU.add).then_inc(f_yd, 1)

            rows_added(0)
            added(0)
            rows_added(1)
            added(1)
            rstd(0)
            dve.wait_ge(f_ln, 32)
            gained(0)
            rstd(1)
            shifted(0)
            added(2)
            gained(1)
            rstd(2)
            shifted(1)
            added(3)
            added(4)
            rstd(3)
            gained(2)
            gained(3)
            rstd(4)
            gained(4)
            shifted(4)

        @block.tensor
        def _(pe):
            def products(bank, hw, lw, hf, c, ready):
                cols = slice(hf * HALF, (hf + 1) * HALF)
                pe.matmul(bank, hw[:, c, :], XH[:, c, cols], start=(c == 0), stop=False)
                pe.matmul(bank, hw[:, c, :], XL[:, c, cols], start=False, stop=False)
                ins = pe.matmul(bank, lw[:, c, :], XH[:, c, cols], start=False, stop=(c == KC - 1))
                if c == KC - 1:
                    ins.then_inc(ready, 1)

            def first_unit():
                hw = HI[:, 0, :].rearrange("p (c n) -> p c n", c=KC)
                lw = LO[:, 0, :].rearrange("p (c n) -> p c n", c=KC)
                pe.wait_ge(s_hi, 1)
                for c in range(KC):
                    if c % 4 == 0:
                        pe.wait_ge(s_lo0, c // 4 + 1) if c < 12 else pe.wait_ge(s_lo, 1)
                    if c % 2 == 0:
                        pe.wait_ge(s_xl, c // 2 + 1)
                    for hf in range(2):
                        products(acc(hf), hw, lw, hf, c, s_acc)

            def quarter(u, hf, kq):
                m = 2 * u + hf
                if hf == 0 and kq == 0:
                    pe.wait_ge(s_hi, u + 1)
                    pe.wait_ge(s_lo, u + 1)
                if kq == 0 and m >= 3:
                    pe.wait_ge(s_pr, m - 2)
                hw = HI[:, u % 2, :].rearrange("p (c n) -> p c n", c=KC)
                lw = LO[:, u % 2, :].rearrange("p (c n) -> p c n", c=KC)
                for c in range(8 * kq, 8 * kq + 8):
                    products(acc(m), hw, lw, hf, c, s_acc)

            def att_setup(t):
                u0 = ATT0[t]
                pe.wait_ge(s_pr, 2 * u0 + 12)
                pe.wait_ge(s_const, 160)
                if t:
                    pe.wait_ge(s_grp, t)
                for c in range(4):
                    ins = pe.transpose(MB[2][:, 128 * c:128 * c + 128], slot(u0 + 1)[:, 128 * c:128 * c + 128], IDENT[:, :])
                ins.then_inc(s_vt_t, 1)
                for k in range(2):
                    ins = pe.transpose(MB[3][0:DB, 128 * k:128 * k + 128], slot(u0 + k)[:, SEQ:T], IDENT[:, :])
                ins.then_inc(s_vt_t, 1)

            def att_scores(s):
                t, (l, qb) = s // 8, STEPS[s % 8]
                u0, b = ATT0[t], 64 * l
                k0 = 128 if qb == 0 else 0
                if s >= 1:
                    pe.wait_ge(s_mx, s)
                for j in range(4):
                    dst = MB[j // 2].rearrange("p (c n) -> p c n", c=2)[:, j % 2, k0:256]
                    ins = pe.matmul(dst, slot(u0 + 2 + j)[b:b + 64, 128 * qb:128 * qb + 128],
                                    slot(u0)[b:b + 64, 128 * qb - 128 + k0:128 * qb + 128], start=True, stop=True)
                ins.then_inc(s_sc, 1)

            def att_turn(s):
                t, (l, qb) = s // 8, STEPS[s % 8]
                pe.wait_ge(s_p, s + 1)
                if s >= 1:
                    pe.wait_ge(s_pt, s)
                pe.wait_ge(s_vt, 2 * t + 2)
                for k in range(1 if qb == 0 else 0, 2):
                    for j in range(4):
                        ins = pe.transpose(MB[2 + k][:, 128 * j:128 * j + 128], SC[:, j, 128 * k:128 * k + 128], IDENT[:, :])
                ins.then_inc(s_tp, 1)

            def att_pv(s):
                t, (l, qb) = s // 8, STEPS[s % 8]
                b = 64 * l
                pe.wait_ge(s_pt, s + 1)
                if s >= 1:
                    pe.wait_ge(s_yc, s)
                ks = [1] if qb == 0 else [0, 1]
                for k in ks:
                    ins = pe.matmul(MB[4][b:b + 64, :], VT[:, qb - 1 + k, b:b + 64], PT[:, k, :, :],
                                    start=(k == ks[0]), stop=(k == 1))
                ins.then_inc(s_pv, 1)

            def smp(s, t):
                u0 = ATT0[t]
                if s == 0:
                    pe.wait_ge(s_kc, 32 * (t + 1))
                    pe.wait_ge(s_self, 32 * (t + 1))
                    pe.wait_ge(s_pt, 8 * t + 8)
                    for b in range(DB):
                        ins = pe.transpose(MB[2 + b // 4][:, 128 * (b % 4):128 * (b % 4) + 128], KCA[:, b, :], IDENT[:, :])
                    ins.then_inc(s_m[0], 1)
                elif s == 1:
                    pe.wait_ge(s_m[1], t + 1)
                    pe.wait_ge(s_mx, 8 * t + 8)
                    for b in range(DB):
                        for l in range(2):
                            s0 = (u0 + 2) % 16
                            ins = pe.matmul(MB[l][:, 4 * b:4 * b + 4], KTS[64 * l:64 * l + 64, b, :],
                                            PR[64 * l:64 * l + 64, s0:s0 + 4, SEQ + b], start=True, stop=True)
                    ins.then_inc(s_m[2], 1)
                elif s == 2:
                    pe.wait_ge(s_m[3], t + 1)
                    pe.transpose(MB[1][0:64, 0:128], SST[:, :], IDENT[:, :]).then_inc(s_m[4], 1)
                elif s == 3:
                    pe.wait_ge(s_m[7], t + 1)
                    pe.transpose(MB[3][:, 0:64], SSR[:, :], IDENT[0:64, 0:64]).then_inc(s_m[8], 1)
                elif s == 4:
                    pe.wait_ge(s_m[9], t + 1)
                    pe.wait_ge(s_yc, 8 * t + 8)
                    for b in range(DB):
                        for l in range(2):
                            c = 32 * l + 4 * b
                            ins = pe.matmul(MB[4][64 * l:64 * l + 64, 4 * b:4 * b + 4], VCA[:, b, 64 * l:64 * l + 64],
                                            PST[:, c:c + 4], start=True, stop=True)
                    ins.then_inc(s_m[10], 1)

            def hg_level(x):
                h, l = x // 8, x % 8
                q, k = slot(HG0[h]), slot(HG0[h] + 1)
                z = l % 2
                if l == 0:
                    pe.wait_ge(h_k, h + 1)
                else:
                    pe.wait_ge(h_mul, 7 * h + l)
                if l >= 2:
                    pe.wait_ge(h_acc, 8 * h + l - 1)
                for c in range(4):
                    cols = slice(128 * c, 128 * c + 128)
                    if l == 0:
                        ins = pe.matmul(MB[0][:, cols], k[:, cols], q[:, cols], start=True, stop=True)
                    else:
                        n = 1 << (l - 1)
                        qq = QF[:, z, cols].rearrange("p (b s n) -> p b s n", s=2, n=n)[:, :, 1, :]
                        ins = pe.matmul(MB[l % 2][:, 64 * c:64 * c + 64], QF[:, z, cols], qq, start=True, stop=True)
                ins.then_inc(h_lev, 1)
                if l == 4:
                    v = slot(HG0[h] + 2)
                    for c in range(4):
                        ins = pe.transpose(MB[2][:, 128 * c:128 * c + 128], v[:, 128 * c:128 * c + 128], IDENT[:, :])
                    ins.then_inc(h_vt, 1)

            def spread(h, c):
                v = slot(HG0[h] + 2)
                if c:
                    pe.wait_ge(h_sn, 2 * h + c)
                for b in range(4):
                    t = SEQ + 4 * c + b
                    ins = pe.transpose(MB[4][:, 128 * b:128 * b + 128], v[:, t:t + 1].to_broadcast([128, 128]), IDENT[:, :])
                ins.then_inc(h_vb, 1)

            def hg(s, h):
                q = slot(HG0[h])
                if s == 0:
                    spread(h, 0)
                elif s == 1:
                    pe.wait_ge(h_ks, h + 1)
                    pe.wait_ge(h_vtc, h + 1)
                    for c in range(4):
                        ins = pe.transpose(MB[2][:, 128 * c:128 * c + 128], EF[:, 1, 128 * c:128 * c + 128], IDENT[:, :])
                    ins.then_inc(h_kt, 1)
                elif s == 2:
                    spread(h, 1)
                    pe.wait_ge(h_ktc, h + 1)
                    for c in range(4):
                        ins = pe.matmul(MB[3][:, 128 * c:128 * c + 128], PF[:, 128 * c:128 * c + 128], VTK[:, c, :], start=True, stop=True)
                    ins.then_inc(h_u, 1)
                elif s == 4:
                    pe.wait_ge(h_st, h + 1)
                    pe.wait_ge(h_sn, 2 * h + 2)
                    pe.wait_ge(h_acc, 8 * h + 8)
                    for c in range(4):
                        cols = slice(128 * c, 128 * c + 128)
                        pe.matmul(MB[0][:, cols], VTK[:, c, :], AT[:, c, :], start=True, stop=(c == 0))
                        if c:
                            pe.matmul(MB[0][:, cols], SF[:, 128 * c - 128:128 * c], QF[:, 0, cols], start=False, stop=True)
                    for b in range(DB):
                        ins = pe.matmul(MB[4][:, b:b + 1], S0[:, b, :], q[:, SEQ + b:SEQ + b + 1], start=True, stop=True)
                    ins.then_inc(h_o, 1)
                elif s == 5:
                    pe.wait_ge(h_sq, h + 1)
                    pe.wait_ge(s_ones, 1)
                    pe.matmul(MB[1], ONES[:, :], EF[:, 0, 0:SEQ], start=True, stop=True)
                    pe.matmul(MB[2][:, 0:DB], ONES[:, :], EF[:, 0, SEQ:T], start=True, stop=True).then_inc(h_ss, 1)

            for q in range(NQ):
                if q == 0:
                    first_unit()
                elif q >= 4:
                    quarter(q // 4, q % 4 // 2, q % 2)
                for what, n in MIX[q]:
                    if what == "att_setup":
                        att_setup(n)
                    elif what == "att_scores":
                        att_scores(n)
                    elif what == "att_turn":
                        att_turn(n)
                    elif what == "att_pv":
                        att_pv(n)
                    elif what.startswith("smp"):
                        smp(int(what[3:]), n)
                    elif what == "hg_level":
                        hg_level(n)
                    elif what in ("hg0", "hg1", "hg2", "hg4", "hg5"):
                        hg(int(what[2:]), n)

            def turn(n):
                pe.wait_ge(s_rt, 2 * n + 2)
                if n == 0:
                    pe.wait_ge(s_grp, 10)
                elif n % 4 == 0:
                    pe.wait_ge(s_rcp, NT * (n // 4))
                for i in range(NT):
                    ins = pe.transpose(BANK[0:TT, 2 + i, 128 * (n % 4):128 * (n % 4) + 128], RT[:, n % NRT, i * TT:(i + 1) * TT], IDENT[:, :])
                ins.then_inc(s_turn, 1)

            def router(k):
                if k == 0:
                    pe.wait_ge(s_gw, 1)
                    for j, w in ((400, GW), (420, WR)):
                        for c in range(KC):
                            pe.matmul(BANK[0:TT, 7, j:j + 20], ONES[:, 0:TT], w[:, c, :], start=(c == 0), stop=(c == KC - 1))
                for i in range(NT):
                    for c in range(4):
                        ins = pe.matmul(BANK[0:TT, 7, 100 * k + 20 * i:100 * k + 20 * i + 20], RT[:, (4 * k + c) % NRT, i * TT:(i + 1) * TT],
                                        GW[:, 4 * k + c, :], start=(c == 0), stop=(c == 3))
                ins.then_inc(s_log, 1)

            for n in range(KC):
                u = NU + n
                pe.wait_ge(s_hi, u + 1)
                pe.wait_ge(s_lo, u + 1)
                if n == 0:
                    pe.wait_ge(s_pr, 2 * NU)
                hw = HI[:, u % 2, :].rearrange("p (c n) -> p c n", c=KC)
                lw = LO[:, u % 2, :].rearrange("p (c n) -> p c n", c=KC)
                if n == 0:
                    for c in range(KC):
                        pe.wait_ge(s_yl, c + 1)
                        for hf in range(2):
                            products(BANK[:, hf, 0:HALF], hw, lw, hf, c, s_ob)
                    continue
                for hf in range(2):
                    pe.wait_ge(s_rt, 2 * n + hf - 1)
                    for c in range(KC):
                        products(BANK[:, hf, 0:HALF], hw, lw, hf, c, s_ob)
                    if hf == 0 and n >= 1:
                        turn(n - 1)
                        if n % 4 == 0:
                            router(n // 4 - 1)
            turn(KC - 1)
            router(3)
            pe.wait_ge(r_hot, 1)
            pe.wait_ge(s_rc, 160)
            hot = RK[:, :, :].rearrange("p i e -> p (i e)")
            pe.matmul(BANK[0:TT, 0, 0:80], TRI[:, :], hot, start=True, stop=False)
            for s in range(1, NT):
                pe.matmul(BANK[0:TT, 0, 16 * s:80], ONES[0:TT, 0:TT], hot[:, 0:80 - 16 * s], start=False, stop=(s == NT - 1))
            for i in range(NT):
                ins = pe.matmul(BANK[0:TT, 1, 0:16], ONES[0:TT, 0:TT], RK[:, i, :], start=(i == 0), stop=(i == NT - 1))
            ins.then_inc(r_rank, 1)
            pe.wait_ge(r_tab, 1)
            for c in range(2):
                for i in range(NT):
                    ins = pe.matmul(BANK[:, 2, 0:3 * (MAXB + 1)], OH[:, c, i, :], TB[:, c, i, :, :].rearrange("p k j -> p (k j)"),
                                    start=(c == 0 and i == 0), stop=(c == 1 and i == NT - 1))
            ins.then_inc(r_tabm, 1)

            pe.wait_ge(r_idx, 1)
            nb = pe.value_load(EBI[0:1, 31:32], min_val=8, max_val=MAXB - 1) + 1

            def tokens(g, j):
                if g == 0:
                    pe.wait_ge(b_yw, 16) if isinstance(j, int) and j == 0 else pe.wait_ge(b_xg, 16 * j)
                if not isinstance(j, int) or 4 * j + g >= 2:
                    pe.wait_ge(b_xl, 4 * j + g - 1)
                for c in range(4):
                    ins = pe.transpose(BANK[:, 2 + g % 2, 128 * c:128 * c + 128], XG[:, 4 * g + c:D:KC], IDENT[:, :])
                ins.then_inc(b_tx, 1)

            def ready(i, m0, j):
                s = i % NHL if m0 is None else (2 + i) % NHL
                pe.wait_ge(b_lo[s], i // NHL + 1 if m0 is None else (8 + i) // NHL + 1 + 4 * (j - 1))
                return HIB[:, s, :].rearrange("p (c n) -> p c n", c=4), LOB[:, s, :].rearrange("p (c n) -> p c n", c=4)

            def gate_up(j, m0):
                pe.wait_ge(b_xl, 4 * j + 4)
                if m0 is not None:
                    pe.wait_ge(b_h, j)
                for i in range(8):
                    hw, lw = ready(i, m0, j)
                    b = BANK[:, i % 2, :]
                    for c in range(4):
                        cc = 4 * (i // 2) + c
                        pe.matmul(b, XGH[:, cc, :], hw[:, c, :], start=(cc == 0), stop=False)
                        pe.matmul(b, XGL[:, cc, :], hw[:, c, :], start=False, stop=False)
                        ins = pe.matmul(b, XGH[:, cc, :], lw[:, c, :], start=False, stop=(cc == KC - 1))
                    ins.then_inc(b_used, 1)

            def turn_h(j):
                pe.wait_ge(b_h, j + 1)
                if not isinstance(j, int):
                    pe.wait_ge(b_hl, j)
                for c in range(4):
                    ins = pe.transpose(BANK[:, 6, 128 * c:128 * c + 128], H[:, c:512:4], IDENT[:, :])
                ins.then_inc(b_th, 1)

            def down(n, i, j):
                if n == 0:
                    pe.wait_ge(b_hl, j)
                pe.wait_ge(b_y, 4 * (j - 1) + n + 1)
                hw, lw = ready(i, 0, j)
                b = BANK[:, 4 + n % 2, :]
                for c in range(4):
                    pe.matmul(b, HTH[:, c, :], hw[:, c, :], start=(c == 0), stop=False)
                    pe.matmul(b, HTL[:, c, :], hw[:, c, :], start=False, stop=False)
                    ins = pe.matmul(b, HTH[:, c, :], lw[:, c, :], start=False, stop=(c == 3))
                ins.then_inc(b_used, 1)

            for g in range(4):
                tokens(g, 0)
            gate_up(0, None)
            for g in range(4):
                tokens(g, 1)
            turn_h(0)
            with pe.Fori(1, MAXB) as j:
                with pe.If(j < nb):
                    gate_up(j, 0)
                    for n in range(4):
                        tokens(n, j + 1)
                        down(n, 8 + n, j)
                    turn_h(j)
            for n in range(4):
                down(n, n, nb)


def kernel(x_prompt, x_sample, state_conv, state_hgrn, cache_k_win, cache_v_win,
           w_in, w_out, conv_w, hg_lb_param, hg_gain, attn_sinks, ln1_g, ln1_b,
           w_group, b_group, w_router, b_router, w_gate, w_up, w_down, ln2_g, ln2_b):
    import concourse.bacc as bacc
    from concourse.bass_utils import run_bass_kernel_spmd as run

    A = np.asarray
    x = np.concatenate([A(x_prompt)[0], A(x_sample)[:, 0]], axis=0)
    arrays = {
        "xT": x.reshape(T, KC, 128).transpose(2, 1, 0).reshape(128, KC * T),
        "w_in": A(w_in)[0][:, feature_order()].reshape(KC, 128, NU, 128).transpose(2, 1, 0, 3).reshape(NU, 128, 2048),
        "w_out": A(w_out)[0][mix_order()].reshape(KC, 128, KC, 128).transpose(2, 1, 0, 3).reshape(KC, 128, 2048),
        "w_gate": A(w_gate)[0].reshape(NE, 128, KC * 512),
        "w_up": A(w_up)[0].reshape(NE, 128, KC * 512),
        "w_down": A(w_down)[0].reshape(NE, 128, 4, D),
        "wr": np.concatenate([A(w_group)[0], A(w_router)[0]], axis=1).reshape(KC, 128, 20).transpose(1, 0, 2),
        "gb1": np.stack([A(ln1_g)[0].reshape(KC, 128).T, A(ln1_b)[0].reshape(KC, 128).T], axis=1),
        "rb": np.broadcast_to(np.concatenate([A(b_group)[0], A(b_router)[0]]), (TT, 20)),
        "sink": np.broadcast_to(A(attn_sinks)[0], (128, 16)),
        "sinkc": np.broadcast_to(A(attn_sinks)[0].reshape(2, 2, 1, 4), (2, 2, DB, 4)).reshape(2, 64).T,
        "gain": A(hg_gain)[0].reshape(128, 1),
        "lbp": A(hg_lb_param)[0].reshape(4, 128).T,
        "cw": A(conv_w)[0].reshape(3, 4, 128).transpose(2, 1, 0).reshape(128, 12),
        "hist": A(state_conv)[0].reshape(DB, 2, 4, 128).transpose(3, 2, 0, 1).reshape(128, 64),
        "s0": A(state_hgrn)[0].transpose(1, 2, 0, 3),
        "cache_k": A(cache_k_win)[0].reshape(DB, WIN, 256),
        "cache_v": A(cache_v_win)[0].reshape(DB, WIN, 256),
        "ln1g": np.broadcast_to(A(ln1_g)[0], (TT, D)),
        "ln1b": np.broadcast_to(A(ln1_b)[0], (TT, D)),
        "ln2g": np.broadcast_to(A(ln2_g)[0], (TT, D)),
        "ln2b": np.broadcast_to(A(ln2_b)[0], (TT, D)),
    }
    f = np.float32
    i, j = np.arange(128)[:, None], np.arange(256)[None, :]
    dist = i + WIN - j
    s, t = np.arange(128)[:, None], np.arange(128)[None, :]
    levels = [s == t] + [(s // (2 * n) == t // (2 * n)) & (s % (2 * n) < n) & (t % (2 * n) >= n) for n in (1, 2, 4, 8, 16, 32, 64)]
    row = np.arange(64)[:, None]
    head = 8 * np.arange(2)[None, :] + 4 * (row // 32) + row % 4
    slope = np.array(SLOPE, f)[head]
    tok = np.broadcast_to(np.arange(TT)[:, None, None] + TT * np.arange(NT)[None, None, :], (TT, 2, NT))
    arrays |= {
        "ident": np.eye(128, dtype=f),
        "ndist": np.where((dist >= 0) & (dist < WIN), -dist, NEG).astype(f),
        "mask": np.stack(levels, axis=1).astype(np.float16),
        "nds": (-slope[:, :, None] * (127 - np.arange(128))[None, None, :].astype(f)).astype(f),
        "tri": (np.arange(TT)[:, None] < np.arange(TT)[None, :]).astype(f),
        "ios": np.broadcast_to(np.arange(128, dtype=f) - CAP, (TT, 128)),
        "thb": np.broadcast_to(CAP * np.arange(MAXB + 2, dtype=f), (TT, MAXB + 2)),
        "io24": np.broadcast_to(np.arange(MAXB + 1, dtype=f), (TT, MAXB + 1)),
        "io4": np.broadcast_to(np.arange(4, dtype=f) - 4, (TT, 4)),
        "io16": np.broadcast_to(np.arange(16, dtype=f) - 16, (TT, 16)),
        "cuts": np.broadcast_to(CAP * np.arange(NT, dtype=f) + f(0.5), (TT, NT)),
        "val": np.stack([tok - SKIP, 0 * tok, tok + T * np.arange(2)[:, None] - SKIP], axis=-1).astype(f),
        "lim": np.where(np.arange(128)[:, None] > 0, SKIP, T - 1.0).astype(f),
    }
    outs = {"yp": (SEQ, D), "ys": (DB, D), "cs": (128, 4, 18), "hp": (4, 128, 128), "hs": (4, 128, DB, 128),
            "kp": (2, 128, 128), "vp": (2, 128, 128), "ks": (2, 128, DB, 128), "vs": (2, 128, DB, 128)}

    nc = bacc.Bacc("TRN2", target_bir_lowering=False, num_devices=1)
    arrays = {n: np.ascontiguousarray(v) for n, v in arrays.items()}
    a = {n: nc.dram_tensor(f"in_{n}", v.shape, mybir.dt.from_np(v.dtype), kind="ExternalInput").ap() for n, v in arrays.items()}
    o = {n: nc.dram_tensor(f"out_{n}", sh, F32, kind="ExternalOutput").ap() for n, sh in outs.items()}
    build(nc, a, o)
    r = run(nc, [{f"in_{n}": v for n, v in arrays.items()}], core_ids=[0]).results[0]
    r = {n: r[f"out_{n}"] for n in outs}

    cs = r["cs"].transpose(2, 1, 0).reshape(18, 512)
    return (
        r["yp"].reshape(1, SEQ, D),
        r["ys"].reshape(DB, 1, D),
        cs[0:2].reshape(1, 1, 2, 512),
        cs[2:18].reshape(1, DB, 2, 512),
        r["hp"].reshape(1, 1, 4, 128, 128),
        r["hs"].transpose(2, 0, 1, 3).reshape(1, DB, 4, 128, 128),
        r["kp"].transpose(2, 0, 1).reshape(1, 1, WIN, 4, HD),
        r["ks"].transpose(2, 1, 0, 3).reshape(1, DB, WIN, 4, HD),
        r["vp"].transpose(1, 0, 2).reshape(1, 1, WIN, 4, HD),
        r["vs"].transpose(2, 1, 0, 3).reshape(1, DB, WIN, 4, HD),
    )
```
